# Optimizing a Trainium2 kernel written in Bass

```python
import jax, jax.numpy as jnp
from jax import lax
import numpy as np

D_MODEL = 1024
BATCH = 1
SEQ = 2048
DEPTH = 2

N_MIXERS = 3
HEAD_DIM = 64
N_HEADS = D_MODEL // HEAD_DIM
MIX_WIDTH = N_HEADS * HEAD_DIM
Q_BLOCK = 128
ROPE_THETA = 10000.0
NEG_INF = -1e30
PLE_DIM = 256
MAX_POS_OFFSET = 4096
DEEPNORM_ALPHA = (2 * DEPTH) ** 0.25
DEEPNORM_BETA = (8 * DEPTH) ** -0.25
LN_EPS = 1e-5
RMS_EPS = 1e-6

SWA_WINDOW = 128
SWA_KV_HEADS = 4
SWA_GROUP = N_HEADS // SWA_KV_HEADS
SWA_KV = SWA_KV_HEADS * HEAD_DIM
SWA_IN = MIX_WIDTH + 2 * SWA_KV + MIX_WIDTH

MLA_Q_LORA = 384
MLA_KV_LORA = 256
MLA_NOPE = 64
MLA_ROPE = 32
MLA_V = 64
MLA_IN = MLA_Q_LORA + MLA_KV_LORA + MLA_ROPE + MIX_WIDTH

NSA_KV_GROUPS = 4
NSA_GROUP = N_HEADS // NSA_KV_GROUPS
NSA_KV = NSA_KV_GROUPS * HEAD_DIM
CMP_BLOCK = 32
CMP_STRIDE = 16
SEL_BLOCK = 64
N_SEL = 8
SEL_Q_BLOCK = 32
SEL_FORCE = 1e9
NSA_WINDOW = 512
PHI_HIDDEN = 256
NSA_IN = MIX_WIDTH + 6 * NSA_KV + 3 * N_HEADS + MIX_WIDTH

kernel_name = 'hybrid_swa_mla_nsa_deepnorm'

def _layernorm(x, g, b):
    xf = x.astype(jnp.float32)
    mu = xf.mean(-1, keepdims=True)
    var = jnp.square(xf - mu).mean(-1, keepdims=True)
    return ((xf - mu) * lax.rsqrt(var + LN_EPS) * g + b).astype(x.dtype)

def _rmsnorm(x, g):
    xf = x.astype(jnp.float32)
    return (xf * lax.rsqrt(jnp.mean(xf * xf, -1, keepdims=True) + RMS_EPS) * g).astype(x.dtype)

def _rope(x, pos):
    half = x.shape[-1] // 2
    inv = ROPE_THETA ** (-jnp.arange(half, dtype=jnp.float32) / half)
    ang = pos.astype(jnp.float32)[..., None] * inv
    cos = jnp.cos(ang)[:, :, None, :]
    sin = jnp.sin(ang)[:, :, None, :]
    x1 = x[..., :half].astype(jnp.float32)
    x2 = x[..., half:].astype(jnp.float32)
    return jnp.concatenate([x1 * cos - x2 * sin, x2 * cos + x1 * sin], -1).astype(x.dtype)

def _banded_gqa(q, k, v, window, sinks):
    B, S, G, R, D = q.shape
    nb = S // Q_BLOCK
    n_prev = -(-(window - 1) // Q_BLOCK)
    span = (n_prev + 1) * Q_BLOCK
    pad = n_prev * Q_BLOCK
    kp = jnp.pad(k, ((0, 0), (pad, 0), (0, 0), (0, 0)))
    vp = jnp.pad(v, ((0, 0), (pad, 0), (0, 0), (0, 0)))
    qb = q.reshape(B, nb, Q_BLOCK, G, R, D).transpose(1, 0, 2, 3, 4, 5)
    scale = D ** -0.5

    def blk(args):
        b, qblk = args
        start = b * Q_BLOCK
        kb = lax.dynamic_slice_in_dim(kp, start, span, axis=1)
        vb = lax.dynamic_slice_in_dim(vp, start, span, axis=1)
        t = start + jnp.arange(Q_BLOCK)
        j = start - pad + jnp.arange(span)
        mask = (j[None, :] <= t[:, None]) & (j[None, :] > t[:, None] - window) & (j[None, :] >= 0)
        s = jnp.einsum('bqgrd,bkgd->bgrqk', qblk, kb).astype(jnp.float32) * scale
        s = jnp.where(mask, s, NEG_INF)
        if sinks is None:
            pr = jax.nn.softmax(s, axis=-1)
        else:
            snk = jnp.broadcast_to(sinks.astype(jnp.float32).reshape(1, G, R, 1, 1), s.shape[:-1] + (1,))
            pr = jax.nn.softmax(jnp.concatenate([s, snk], -1), axis=-1)[..., :-1]
        return jnp.einsum('bgrqk,bkgd->bqgrd', pr.astype(vb.dtype), vb)

    ob = lax.map(blk, (jnp.arange(nb), qb))
    return ob.transpose(1, 0, 2, 3, 4, 5).reshape(B, S, G, R, D)

def _mla_attention(q_nope, q_rope, k_nope, k_rope, v):
    B, S, H, Dn = q_nope.shape
    Dr = q_rope.shape[-1]
    nb = S // Q_BLOCK
    scale = (Dn + Dr) ** -0.5
    qn = q_nope.reshape(B, nb, Q_BLOCK, H, Dn).transpose(1, 0, 2, 3, 4)
    qr = q_rope.reshape(B, nb, Q_BLOCK, H, Dr).transpose(1, 0, 2, 3, 4)
    kpos = jnp.arange(S)

    def blk(args):
        b, qnb, qrb = args
        t = b * Q_BLOCK + jnp.arange(Q_BLOCK)
        s = (jnp.einsum('bqhd,bkhd->bhqk', qnb, k_nope)
             + jnp.einsum('bqhd,bkd->bhqk', qrb, k_rope)).astype(jnp.float32) * scale
        pr = jax.nn.softmax(jnp.where(kpos[None, :] <= t[:, None], s, NEG_INF), axis=-1)
        return jnp.einsum('bhqk,bkhd->bqhd', pr.astype(v.dtype), v)

    ob = lax.map(blk, (jnp.arange(nb), qn, qr))
    return ob.transpose(1, 0, 2, 3, 4).reshape(B, S, H, v.shape[-1])

def _selected_attention(q, k, v, sel):
    B, S, G, R, D = q.shape
    K = sel.shape[-1]
    n_blk = S // SEL_BLOCK
    nq = S // SEL_Q_BLOCK
    scale = D ** -0.5
    kb = k.reshape(B, n_blk, SEL_BLOCK, G, D).transpose(0, 3, 1, 2, 4)
    vb = v.reshape(B, n_blk, SEL_BLOCK, G, D).transpose(0, 3, 1, 2, 4)
    qb = q.reshape(B, nq, SEL_Q_BLOCK, G, R, D).transpose(1, 0, 2, 3, 4, 5)
    ib = sel.reshape(B, G, nq, SEL_Q_BLOCK, K).transpose(2, 0, 1, 3, 4)
    gather = jax.vmap(jax.vmap(lambda blocks, ids: blocks[ids]))
    offs = jnp.arange(SEL_BLOCK)

    def blk(args):
        b, qblk, iblk = args
        t = b * SEL_Q_BLOCK + jnp.arange(SEL_Q_BLOCK)
        kg = gather(kb, iblk).reshape(B, G, SEL_Q_BLOCK, K * SEL_BLOCK, D)
        vg = gather(vb, iblk).reshape(B, G, SEL_Q_BLOCK, K * SEL_BLOCK, D)
        kpos = (iblk[..., None] * SEL_BLOCK + offs).reshape(B, G, SEL_Q_BLOCK, K * SEL_BLOCK)
        mask = (kpos <= t[None, None, :, None])[:, :, None]
        s = jnp.einsum('bqgrd,bgqkd->bgrqk', qblk, kg).astype(jnp.float32) * scale
        pr = jax.nn.softmax(jnp.where(mask, s, NEG_INF), axis=-1)
        return jnp.einsum('bgrqk,bgqkd->bqgrd', pr.astype(vg.dtype), vg)

    ob = lax.map(blk, (jnp.arange(nq), qb, ib))
    return ob.transpose(1, 0, 2, 3, 4, 5).reshape(B, S, G, R, D)

def _mixer_swa(h, positions, w_in, sinks):
    B, S, _ = h.shape
    proj = h @ w_in
    q, k, v, z = jnp.split(proj, [MIX_WIDTH, MIX_WIDTH + SWA_KV, MIX_WIDTH + 2 * SWA_KV], axis=-1)
    q = _rope(q.reshape(B, S, N_HEADS, HEAD_DIM), positions).reshape(B, S, SWA_KV_HEADS, SWA_GROUP, HEAD_DIM)
    k = _rope(k.reshape(B, S, SWA_KV_HEADS, HEAD_DIM), positions)
    v = v.reshape(B, S, SWA_KV_HEADS, HEAD_DIM)
    o = _banded_gqa(q, k, v, SWA_WINDOW, sinks).reshape(B, S, MIX_WIDTH)
    return o * jax.nn.silu(z)

def _mixer_mla(h, positions, w_in, q_norm, kv_norm, w_uq, w_ukv):
    B, S, _ = h.shape
    proj = h @ w_in
    cq, ckv, kr, z = jnp.split(proj, [MLA_Q_LORA, MLA_Q_LORA + MLA_KV_LORA,
                                      MLA_Q_LORA + MLA_KV_LORA + MLA_ROPE], axis=-1)
    q = (_rmsnorm(cq, q_norm) @ w_uq).reshape(B, S, N_HEADS, MLA_NOPE + MLA_ROPE)
    q_nope = q[..., :MLA_NOPE]
    q_rope = _rope(q[..., MLA_NOPE:], positions)
    kv = (_rmsnorm(ckv, kv_norm) @ w_ukv).reshape(B, S, N_HEADS, MLA_NOPE + MLA_V)
    k_nope = kv[..., :MLA_NOPE]
    v = kv[..., MLA_NOPE:]
    k_rope = _rope(kr[:, :, None, :], positions)[:, :, 0, :]
    o = _mla_attention(q_nope, q_rope, k_nope, k_rope, v).reshape(B, S, MIX_WIDTH)
    return o * jax.nn.silu(z)

def _mixer_nsa(h, positions, w_in, cmp_pos, phi_k1, phi_k2, phi_v1, phi_v2):
    B, S, _ = h.shape
    G, R, D = NSA_KV_GROUPS, NSA_GROUP, HEAD_DIM
    proj = h @ w_in
    cuts = np.cumsum([MIX_WIDTH] + [NSA_KV] * 6 + [3 * N_HEADS]).tolist()
    q, k_c, v_c, k_s, v_s, k_w, v_w, gl, z = jnp.split(proj, cuts, axis=-1)
    q = _rope(q.reshape(B, S, N_HEADS, D), positions).reshape(B, S, G, R, D)
    scale = D ** -0.5
    t_idx = jnp.arange(S)

    n_cmp = (S - CMP_BLOCK) // CMP_STRIDE + 1
    tok = jnp.arange(n_cmp)[:, None] * CMP_STRIDE + jnp.arange(CMP_BLOCK)[None, :]

    def compress(t, w1, w2):
        blocks = t.reshape(B, S, G, D)[:, tok] + cmp_pos[:, None, :]
        flat = blocks.transpose(0, 1, 3, 2, 4).reshape(B, n_cmp, G, CMP_BLOCK * D)
        return jax.nn.silu(flat @ w1) @ w2

    blk_end = tok[:, -1]
    kc = _rope(compress(k_c, phi_k1, phi_k2), positions[:, blk_end])
    vc = compress(v_c, phi_v1, phi_v2)
    cmask = blk_end[None, :] <= t_idx[:, None]
    sc = jnp.einsum('bsgrd,bngd->bgrsn', q, kc).astype(jnp.float32) * scale
    pc = jnp.where(cmask, jax.nn.softmax(jnp.where(cmask, sc, NEG_INF), axis=-1), 0.0)
    o_cmp = jnp.einsum('bgrsn,bngd->bsgrd', pc.astype(vc.dtype), vc)

    n_blk = S // SEL_BLOCK
    n_top = min(N_SEL, n_blk)
    j = jnp.arange(n_blk)
    cstart = tok[:, 0]
    overlap = ((cstart[:, None] < (j[None, :] + 1) * SEL_BLOCK)
               & (cstart[:, None] + CMP_BLOCK > j[None, :] * SEL_BLOCK)).astype(jnp.float32)
    imp = jnp.einsum('bgrsn,nj->bgsj', pc, overlap)
    cur = (t_idx // SEL_BLOCK)[:, None]
    forced = (j[None, :] == 0) | (j[None, :] == cur) | (j[None, :] == cur - 1)
    score = jnp.where(forced, SEL_FORCE, jnp.where(j[None, :] <= cur, imp, -SEL_FORCE))
    _, sel = lax.top_k(score, n_top)
    ks = _rope(k_s.reshape(B, S, G, D), positions)
    o_slc = _selected_attention(q, ks, v_s.reshape(B, S, G, D), sel)

    kw = _rope(k_w.reshape(B, S, G, D), positions)
    o_win = _banded_gqa(q, kw, v_w.reshape(B, S, G, D), NSA_WINDOW, None)

    g = jax.nn.sigmoid(gl.astype(jnp.float32)).astype(h.dtype).reshape(B, S, 3, G, R, 1)
    o = g[:, :, 0] * o_cmp + g[:, :, 1] * o_slc + g[:, :, 2] * o_win
    return o.reshape(B, S, MIX_WIDTH) * jax.nn.silu(z)

def setup_inputs(seed: int = 0) -> dict:
    key = jax.random.key(seed)
    ks = list(jax.random.split(key, 40))

    def nrm(shape, scale):
        return jax.random.normal(ks.pop(), shape, jnp.float32) * scale

    def gain(shape):
        return 1.0 + nrm(shape, 0.02)

    x = nrm((BATCH, SEQ, D_MODEL), 1.0)
    p = nrm((DEPTH, BATCH, SEQ, PLE_DIM), 1.0)
    positions = (jax.random.randint(ks.pop(), (BATCH, 1), 0, MAX_POS_OFFSET, dtype=jnp.int32)
                 + jnp.arange(SEQ, dtype=jnp.int32)[None, :]).astype(jnp.int32)
    return {
        'x': x,
        'p': p,
        'positions': positions,
        'w_out': nrm((DEPTH, MIX_WIDTH, D_MODEL), MIX_WIDTH ** -0.5 * DEEPNORM_BETA),
        'ln_g': gain((DEPTH, D_MODEL)),
        'ln_b': nrm((DEPTH, D_MODEL), 0.02),
        'pe_gate': nrm((DEPTH, D_MODEL, D_MODEL), D_MODEL ** -0.5),
        'pe_proj': nrm((DEPTH, PLE_DIM, D_MODEL), PLE_DIM ** -0.5),
        'l0_w_in': nrm((D_MODEL, SWA_IN), D_MODEL ** -0.5),
        'l0_sinks': nrm((N_HEADS,), 0.5),
        'l1_w_in': nrm((D_MODEL, MLA_IN), D_MODEL ** -0.5),
        'l1_q_norm': gain((MLA_Q_LORA,)),
        'l1_kv_norm': gain((MLA_KV_LORA,)),
        'l1_w_uq': nrm((MLA_Q_LORA, N_HEADS * (MLA_NOPE + MLA_ROPE)), MLA_Q_LORA ** -0.5),
        'l1_w_ukv': nrm((MLA_KV_LORA, N_HEADS * (MLA_NOPE + MLA_V)), MLA_KV_LORA ** -0.5),
        'l2_w_in': nrm((D_MODEL, NSA_IN), D_MODEL ** -0.5),
        'l2_cmp_pos': nrm((CMP_BLOCK, HEAD_DIM), 0.1),
        'l2_phi_k1': nrm((CMP_BLOCK * HEAD_DIM, PHI_HIDDEN), (CMP_BLOCK * HEAD_DIM) ** -0.5),
        'l2_phi_k2': nrm((PHI_HIDDEN, HEAD_DIM), PHI_HIDDEN ** -0.5),
        'l2_phi_v1': nrm((CMP_BLOCK * HEAD_DIM, PHI_HIDDEN), (CMP_BLOCK * HEAD_DIM) ** -0.5),
        'l2_phi_v2': nrm((PHI_HIDDEN, HEAD_DIM), PHI_HIDDEN ** -0.5),
        'l3_w_in': nrm((D_MODEL, SWA_IN), D_MODEL ** -0.5),
        'l3_sinks': nrm((N_HEADS,), 0.5),
    }

def reference(x, p, positions, w_out, ln_g, ln_b, pe_gate, pe_proj,
              l0_w_in, l0_sinks,
              l1_w_in, l1_q_norm, l1_kv_norm, l1_w_uq, l1_w_ukv,
              l2_w_in, l2_cmp_pos, l2_phi_k1, l2_phi_k2, l2_phi_v1, l2_phi_v2,
              l3_w_in, l3_sinks):
    mixers = (_mixer_swa, _mixer_mla, _mixer_nsa)
    layer_params = (
        (l0_w_in, l0_sinks),
        (l1_w_in, l1_q_norm, l1_kv_norm, l1_w_uq, l1_w_ukv),
        (l2_w_in, l2_cmp_pos, l2_phi_k1, l2_phi_k2, l2_phi_v1, l2_phi_v2),
        (l3_w_in, l3_sinks),
    )
    for i in range(DEPTH):
        y = mixers[i % N_MIXERS](x, positions, *layer_params[i]) @ w_out[i]
        x = _layernorm(DEEPNORM_ALPHA * x + y, ln_g[i], ln_b[i])
        x = x + jax.nn.sigmoid(x @ pe_gate[i]) * (p[i] @ pe_proj[i])
    return x


_drawn_inputs = setup_inputs


def setup_inputs(seed=0):
    import zlib

    import numpy as np

    out = dict(_drawn_inputs(seed))
    spreads = {}
    factors = {'l0_sinks': 8.0, 'l1_q_norm': 8.0, 'l1_kv_norm': 8.0, 'l1_w_uq': 3.231}
    for name, (base, spread) in spreads.items():
        noise = np.random.default_rng([zlib.crc32(name.encode()), seed]).standard_normal(out[name].shape)
        drawn = base * np.exp(spread * noise) if base else spread * noise
        out[name] = __import__('jax').numpy.asarray(drawn.astype(out[name].dtype))
    for name, factor in factors.items():
        out[name] = (out[name] * factor).astype(out[name].dtype)
    return out
```

```python
import numpy as np

import concourse.bass as bass
from concourse import mybir
from concourse.alu_op_type import AluOpType as ALU

ACT = mybir.ActivationFunctionType
AX = mybir.AxisListType
F32 = mybir.dt.float32
F32R = mybir.dt.float32r
BF16 = mybir.dt.bfloat16
I32 = mybir.dt.int32

P = 128
D_MODEL = 1024
SEQ = 2048
DEPTH = 2
HEADS = 16
HEAD_DIM = 64
KV_HEADS = 4
GROUP = HEADS // KV_HEADS
Q_LORA = 384
KV_LORA = 256
ROPE = 32
NOPE = 64
PLE = 256
ALPHA = (2 * DEPTH) ** 0.25
LN_EPS = 1e-5
RMS_EPS = 1e-6
THETA = 10000.0
TC = 512
NTC = SEQ // TC
NB = SEQ // P
KD = D_MODEL // P
BIG = -1e30
SWA_SCALE = HEAD_DIM ** -0.5
MLA_SCALE = (NOPE + ROPE) ** -0.5


def wait(eng, sem, value):
    if isinstance(value, int) and value <= 0:
        return
    eng.wait_ge(sem, value)


def repeat(eng, count, body, last_apart=False):
    body(0)
    end = count - 1 if last_apart and count > 1 else count
    if end == 2:
        body(1)
    elif end > 2:
        with eng.Fori(1, end) as i:
            body(i)
    if end < count:
        body(end)


class Scope:

    def __init__(self, nc, ctx, name):
        self.nc, self.ctx, self.name, self.sems = nc, ctx, name, []
        ctx.callback(self.close)

    def close(self):
        for sem in self.sems:
            self.nc.gpsimd.sem_clear(sem)
            self.nc.release_semaphore(sem)

    def sb(self, name, shape, dt=F32):
        return self.ctx.enter_context(self.nc.sbuf_tensor(f"{self.name}_{name}", shape, dt))

    def ps(self, name, shape, dt=F32):
        return self.ctx.enter_context(self.nc.psum_tensor(f"{self.name}_{name}", shape, dt))

    def sem(self, name):
        sem = self.nc.alloc_semaphore(f"{self.name}_{name}")
        if not name.split("_")[-1].startswith("stored"):
            self.sems.append(sem)
        return sem


def tables_phase(nc, consts, positions, inv, tables):
    from contextlib import ExitStack
    with ExitStack() as ctx:
        s = Scope(nc, ctx, "tab")
        pos_i, pos, inv_sb = s.sb("pos_i", [P, SEQ], I32), s.sb("pos", [P, SEQ]), s.sb("inv", [P, 2])
        ang, k, red = s.sb("ang", [P, SEQ]), s.sb("k", [P, SEQ]), s.sb("red", [P, SEQ])
        out = [[s.sb(f"out{t}{f}", [P, SEQ]) for f in range(2)] for t in range(2)]
        arg = [[s.sb(f"arg{t}{f}", [P, SEQ]) for f in range(2)] for t in range(2)]
        loaded, dve, filled, args, done, stored = (
            s.sem(n) for n in ("loaded", "dve", "filled", "args", "done", "stored"))
        block = ctx.enter_context(nc.Block())
        two_pi = 2 * np.pi
        c1 = 6.28125
        c2 = float(np.float32(np.floor((two_pi - c1) * 2 ** 20) / 2 ** 20))
        c3 = float(two_pi - c1 - c2)
        magic = 1.5 * 2 ** 23

        @block.sync
        def _(sp):
            sp.dma_start(pos_i[:], positions.partition_broadcast(P)).then_inc(loaded, 16)
            sp.dma_start(inv_sb[:], inv).then_inc(loaded, 16)
            for t in range(2):
                for f in range(2):
                    sp.wait_ge(done, 2 * t + f + 1)
                    sp.dma_start(tables[t][f], out[t][f][:]).then_inc(stored, 16)
            sp.wait_ge(stored, 64)

        @block.gpsimd
        def _(pool):
            ident, ident_b, ones, zeros = consts["ident"], consts["ident_b"], consts["ones"], consts["zeros"]
            n = 0
            for tile, value in ((ident, 0.0), (ident_b, 0.0), (ones, 1.0), (zeros, 0.0),
                                (consts["causal_t"], 0.0), (consts["prev_t"], 0.0),
                                (consts["causal_q"], 0.0), (consts["window_q"], 0.0)):
                pool.memset(tile[:], value).then_inc(filled, 1)
                n += 1
            pool.wait_ge(filled, n)
            for tile in (ident, ident_b):
                pool.affine_select(out=tile[:], in_=tile[:], compare_op=ALU.not_equal, fill=1.0, base=0,
                                   pattern=[[-1, P]], channel_multiplier=1)
            pool.affine_select(out=consts["causal_t"][:], in_=consts["causal_t"][:], compare_op=ALU.is_ge,
                               fill=BIG, base=0, pattern=[[0, GROUP], [1, P]], channel_multiplier=-1)
            pool.affine_select(out=consts["prev_t"][:], in_=consts["prev_t"][:], compare_op=ALU.is_gt,
                               fill=BIG, base=0, pattern=[[0, GROUP], [-1, P]], channel_multiplier=1)
            pool.affine_select(out=consts["causal_q"][:], in_=consts["causal_q"][:], compare_op=ALU.is_ge,
                               fill=BIG, base=0, pattern=[[-1, P]], channel_multiplier=1)
            pool.affine_select(out=consts["window_q"][:, 0:P], in_=consts["window_q"][:, 0:P],
                               compare_op=ALU.is_gt, fill=BIG, base=0, pattern=[[1, P]],
                               channel_multiplier=-1)
            pool.affine_select(out=consts["window_q"][:, P:2 * P], in_=consts["window_q"][:, P:2 * P],
                               compare_op=ALU.is_ge, fill=BIG, base=0, pattern=[[-1, P]],
                               channel_multiplier=1)

        @block.vector
        def _(dve_e):
            n = 0

            def chain(op):
                nonlocal n
                op.then_inc(dve, 1)
                n += 1
                dve_e.wait_ge(dve, n)

            v = nc.vector
            dve_e.wait_ge(loaded, 32)
            chain(v.tensor_copy(pos[:], pos_i[:]))
            for t in range(2):
                chain(v.tensor_scalar(ang[:], pos[:], inv_sb[:, t:t + 1], None, ALU.mult))
                chain(v.tensor_scalar(k[:], ang[:], float(1 / two_pi), None, ALU.mult))
                chain(v.tensor_scalar(k[:], k[:], magic, None, ALU.add))
                chain(v.tensor_scalar(k[:], k[:], magic, None, ALU.subtract))
                chain(v.scalar_tensor_tensor(red[:], k[:], -c1, ang[:], ALU.mult, ALU.add))
                chain(v.scalar_tensor_tensor(red[:], k[:], -c2, red[:], ALU.mult, ALU.add))
                chain(v.scalar_tensor_tensor(red[:], k[:], -c3, red[:], ALU.mult, ALU.add))
                chain(v.tensor_scalar(arg[t][1][:], red[:], 3.1415925, -3.1415925, ALU.min, ALU.max))
                chain(v.scalar_tensor_tensor(red[:], arg[t][1][:], -1.0, arg[t][1][:], ALU.mult, ALU.max))
                v.tensor_scalar(arg[t][0][:], red[:], -1.0, float(np.pi / 2), ALU.mult, ALU.add).then_inc(args, 1)

        @block.scalar
        def _(act):
            for t in range(2):
                act.wait_ge(args, t + 1)
                for f in range(2):
                    act.activation(out[t][f][:], arg[t][f][:], ACT.Sin).then_inc(done, 1)


def gemm_phase(nc, consts, name, xs, w, segments, tables=None, v=None):
    from contextlib import ExitStack
    with ExitStack() as ctx:
        s = Scope(nc, ctx, name)
        pairs = sum(n for _, n, _ in segments)
        kcs = [xs[0][1], xs[-1][1]]
        hi, lo, pieces = [], [], []
        for x, (src, kc) in enumerate(xs):
            hi.append(s.sb(f"xh{x}", [P, kc, SEQ], F32R))
            lo.append(s.sb(f"xl{x}", [P, kc, SEQ], F32R))
            width = 2 if kc % 2 == 0 else 1
            pieces += [(x, t, k, width) for t in range(NTC) for k in range(0, kc, width)]
        pieces.sort(key=lambda p: (p[1], p[0], p[2]))
        need = [max(n for n, p in enumerate(pieces) if p[1] == t) + 1 for t in range(NTC)]
        hi, lo = [hi[0], hi[-1]], [lo[0], lo[-1]]
        x_raw = [s.sb(f"xraw{b}", [P, 2, TC]) for b in range(2)]
        both = sum(kcs) * P
        w_raw_t, w_hi_t, w_lo_t = s.sb("wraw", [P, both]), s.sb("whi", [P, both], F32R), s.sb("wlo", [P, both], F32R)
        at_slot = [slice(0, kcs[0] * P), slice(kcs[0] * P, both)]
        w_raw, w_hi, w_lo = ([t[:, at_slot[b]] for b in range(2)] for t in (w_raw_t, w_hi_t, w_lo_t))
        banks = [[s.ps(f"bank{b}{t}", [P, TC]) for t in range(NTC)] for b in range(2)]
        x_in = [s.sem(f"x_in{b}") for b in range(2)]
        x_hi, x_lo = s.sem("x_hi"), s.sem("x_lo")
        w_in = [s.sem(f"w_in{b}") for b in range(2)]
        w_hi_ok = [s.sem(f"w_hi_ok{b}") for b in range(2)]
        w_lo_ok = [s.sem(f"w_lo_ok{b}") for b in range(2)]
        product = s.sem("product")
        bank_free = [s.sem(f"bank_free{b}") for b in range(2)]
        if tables:
            cos, sin = s.sb("cos", [P, SEQ]), s.sb("sin", [P, SEQ])
            tab_in = s.sem("tab_in")
        kinds = {kind for kind, _, _ in segments}
        if "rope" in kinds:
            ta, tb, tc_, td = (s.sb(f"t{n}", [P, TC]) for n in "abcd")
            rope_out = [s.sb(f"rope{n}", [P, TC], F32R) for n in range(4)]
        if kinds & {"raw", "silu", "resid", "gate"}:
            out_f = s.sb("out_f", [P, TC])
        if kinds & {"silu", "gate"}:
            sig = s.sb("sig", [P, NTC, TC] if "gate" in kinds else [P, 1, TC])
        if kinds & {"resid", "gate"}:
            old = s.sb("old", [P, TC])
        if kinds & {"gate"}:
            prod = s.sb("prod", [P, TC])
        if kinds & {"split"}:
            out_h, out_l = s.sb("out_h", [P, TC], F32R), s.sb("out_l", [P, TC], F32R)
        seg_sems = [{n: s.sem(f"seg{g}_{n}") for n in {
            "rope": ("steps", "hi_a", "hi_b", "ready", "stored"),
            "raw": ("ready", "stored"), "silu": ("sig", "ready", "stored"),
            "split": ("hi", "ready", "stored"), "resid": ("old", "ready", "stored"),
            "gate": ("old", "sig", "prod", "ready", "stored")}[kind]}
            for g, (kind, _, _) in enumerate(segments)]
        if v:
            v_src, v_cols, v_dst = v
            kc_v = kcs[0]
            parts = -(-v_cols // TC)
            v_n = v_cols // parts
            v_heads = v_n // HEAD_DIM
            shared = kc_v * v_cols == both
            wv_raw, wv_hi, wv_lo = (w_raw_t, w_hi_t, w_lo_t) if shared else (
                s.sb("wvraw", [P, kc_v * v_cols]), s.sb("wvhi", [P, kc_v * v_cols], F32R),
                s.sb("wvlo", [P, kc_v * v_cols], F32R))
            v_out = [s.sb(f"vout{b}", [P, v_heads, 2, HEAD_DIM], F32R) for b in range(2)]
            v_in, v_w_hi, v_w_lo, v_prod, v_hi, v_ready = (
                s.sem(n) for n in ("v_in", "v_w_hi", "v_w_lo", "v_prod", "v_hi", "v_ready"))
            v_stored = [s.sem(f"v_stored{b}") for b in range(2)]
            v_items = [(b, h) for b in range(NB) for h in range(parts)]
        block = ctx.enter_context(nc.Block())
        starts = [sum(n for _, n, _ in segments[:g]) for g in range(len(segments))]

        per = {"raw": 128, "silu": 128, "resid": 128, "split": 256, "gate": 64, "rope": 256}

        def each_pair(eng, body):
            for g, (kind, n, _) in enumerate(segments):
                end = g == len(segments) - 1

                def one(li, g=g, n=n, end=end):
                    follows = not (end and isinstance(li, int) and li == n - 1)
                    if g and isinstance(li, int) and li == 0 and eng is not nc.sync:
                        eng.wait_ge(seg_sems[g - 1]["stored"], per[segments[g - 1][0]] * segments[g - 1][1])
                    body(g, li, li + starts[g], follows)
                repeat(eng, n, one, last_apart=end)

        @block.sync
        def _(sp):
            for b in range(2):
                sp.dma_start(w_raw[b], w[b][0]).then_inc(w_in[b], 16)
            if tables:
                sp.dma_start(cos[:], tables[0]).then_inc(tab_in, 16)
                sp.dma_start(sin[:], tables[1]).then_inc(tab_in, 16)
            for n, (x, t, k, width) in enumerate(pieces):
                if n >= 2:
                    sp.wait_ge(x_lo, n - 1)
                src = xs[x][0].rearrange("(k p) t -> p k t", p=P)
                sp.dma_start(x_raw[n % 2][:, 0:width, :],
                             src[:, k:k + width, t * TC:(t + 1) * TC]).then_inc(x_in[n % 2], 16)
            if v and not shared:
                sp.dma_start(wv_raw[:], v_src).then_inc(v_in, 16)

            def body(g, li, i, follows):
                kind, _, arg = segments[g]
                sems = seg_sems[g]
                if follows:
                    for b in range(2):
                        sp.wait_ge(w_lo_ok[b], i + 1)
                        sp.dma_start(w_raw[b], w[b][i + 1]).then_inc(w_in[b], 16)
                if kind in ("resid", "gate"):
                    per = 8 if kind == "resid" else 4
                    for b in range(per // 4):
                        for t in range(NTC):
                            n = li * per + b * 4 + t
                            wait(sp, sems["ready"], n)
                            row = (i * 2 + b) if kind == "resid" else i
                            sp.dma_start(old[:], arg["old"].rearrange("(r p) t -> r p t", p=P)[
                                row, :, t * TC:(t + 1) * TC]).then_inc(sems["old"], 16)
            each_pair(sp, body)
            if v and shared:
                for b in range(2):
                    sp.wait_ge(w_lo_ok[b], pairs)
                sp.dma_start(wv_raw[:], v_src).then_inc(v_in, 16)

        @block.scalar
        def _(act):
            def split_w(b, i):
                act.wait_ge(w_in[b], (i + 1) * 16)
                wait(act, product, i * 8 - 4 + b * 4)
                act.copy(w_hi[b], w_raw[b]).then_inc(w_hi_ok[b], 1)

            for n, (x, t, k, width) in enumerate(pieces):
                act.wait_ge(x_in[n % 2], 16 * (n // 2 + 1))
                slot = x if len(xs) == 2 else 0
                act.copy(hi[slot][:, k:k + width, t * TC:(t + 1) * TC],
                         x_raw[n % 2][:, 0:width, :]).then_inc(x_hi, 1)
                if n == 1:
                    for b in range(2):
                        act.wait_ge(w_in[b], 16)
                        act.copy(w_hi[b], w_raw[b]).then_inc(w_hi_ok[b], 1)
            def split_v():
                act.wait_ge(v_in, 16)
                if shared:
                    act.wait_ge(product, 8 * pairs)
                act.copy(wv_hi[:], wv_raw[:]).then_inc(v_w_hi, 1)

            if v and not shared:
                split_v()

            def body(g, li, i, follows):
                kind, _, arg = segments[g]
                sems = seg_sems[g]
                for b in range(2):
                    for t in range(NTC):
                        n = li * 8 + b * 4 + t
                        if kind in ("raw", "silu", "split") or (kind == "gate" and b == 0):
                            act.wait_ge(product, i * 8 + b * 4 + t + 1)
                        if kind == "raw":
                            wait(act, sems["stored"], n * 16)
                            act.copy(out_f[:], banks[b][t][:]).then_inc(bank_free[b], 1)
                            act.wait_ge(bank_free[b], i * 4 + t + 1)
                            act.sem_inc(sems["ready"], 1)
                        elif kind == "silu":
                            wait(act, sems["ready"], n)
                            act.activation(sig[:, 0, :], banks[b][t][:], ACT.Sigmoid).then_inc(sems["sig"], 1)
                        elif kind == "split":
                            wait(act, sems["stored"], n * 32)
                            act.copy(out_h[:], banks[b][t][:]).then_inc(sems["hi"], 1)
                        elif kind == "gate" and b == 0:
                            m = li * 4 + t
                            wait(act, sems["prod"], 0 if isinstance(li, int) and li == 0 else m - 3)
                            act.activation(sig[:, t, :], banks[0][t][:], ACT.Sigmoid).then_inc(sems["sig"], 1)
                        elif kind == "rope" and b == 1:
                            m = li * 4 + t
                            act.wait_ge(sems["steps"], m * 6 + 5)
                            wait(act, sems["stored"], m * 64)
                            act.copy(rope_out[0][:], ta[:]).then_inc(sems["hi_a"], 1)
                            act.wait_ge(sems["steps"], m * 6 + 6)
                            act.copy(rope_out[2][:], tc_[:]).then_inc(sems["hi_b"], 1)
                    if follows:
                        split_w(b, i + 1)
            each_pair(act, body)
            if v and shared:
                split_v()
            if v:
                for n, (blk, h) in enumerate(v_items):
                    act.wait_ge(v_prod, n + 1)
                    if n >= 2:
                        act.wait_ge(v_stored[n % 2], 16 * (n // 2))
                    act.copy(v_out[n % 2][:, :, 0, :],
                             banks[(n // 4) % 2][n % 4][:, 0:v_n].rearrange("p (h d) -> p h d", d=HEAD_DIM)
                             ).then_inc(v_hi, 1)

        @block.vector
        def _(dve):
            vec = nc.vector

            def split_w(b, i):
                dve.wait_ge(w_hi_ok[b], i + 1)
                vec.tensor_tensor(w_lo[b], w_raw[b], w_hi[b].bitcast(F32),
                                  ALU.subtract).then_inc(w_lo_ok[b], 1)

            for n, (x, t, k, width) in enumerate(pieces):
                dve.wait_ge(x_hi, n + 1)
                slot = x if len(xs) == 2 else 0
                at = (slice(None), slice(k, k + width), slice(t * TC, (t + 1) * TC))
                vec.tensor_tensor(lo[slot][at], x_raw[n % 2][:, 0:width, :],
                                  hi[slot][at].bitcast(F32), ALU.subtract).then_inc(x_lo, 1)
                if n == 1:
                    split_w(0, 0)
                    split_w(1, 0)
            def split_v():
                dve.wait_ge(v_w_hi, 1)
                vec.tensor_tensor(wv_lo[:], wv_raw[:], wv_hi[:].bitcast(F32),
                                  ALU.subtract).then_inc(v_w_lo, 1)

            if v and not shared:
                split_v()
            if tables:
                dve.wait_ge(tab_in, 32)

            def body(g, li, i, follows):
                kind, _, arg = segments[g]
                sems = seg_sems[g]
                for b in range(2):
                    for t in range(NTC):
                        n = li * 8 + b * 4 + t
                        tok = slice(t * TC, (t + 1) * TC)
                        if kind == "silu":
                            dve.wait_ge(sems["sig"], n + 1)
                            wait(dve, sems["stored"], n * 16)
                            vec.tensor_tensor(out_f[:], banks[b][t][:], sig[:, 0, :], ALU.mult
                                              ).then_inc(sems["ready"], 1)
                            dve.wait_ge(sems["ready"], n + 1)
                            dve.sem_inc(bank_free[b], 1)
                        elif kind == "split":
                            dve.wait_ge(sems["hi"], n + 1)
                            vec.tensor_tensor(out_l[:], banks[b][t][:], out_h[:].bitcast(F32),
                                              ALU.subtract).then_inc(sems["ready"], 1)
                            dve.wait_ge(sems["ready"], n + 1)
                            dve.sem_inc(bank_free[b], 1)
                        elif kind == "resid":
                            dve.wait_ge(product, i * 8 + b * 4 + t + 1)
                            dve.wait_ge(sems["old"], (n + 1) * 16)
                            wait(dve, sems["stored"], n * 16)
                            vec.scalar_tensor_tensor(out_f[:], old[:], float(ALPHA), banks[b][t][:],
                                                     ALU.mult, ALU.add).then_inc(sems["ready"], 1)
                            dve.wait_ge(sems["ready"], n + 1)
                            dve.sem_inc(bank_free[b], 1)
                        elif kind == "gate" and b == 1:
                            m = li * 4 + t
                            dve.wait_ge(sems["sig"], m + 1)
                            wait(dve, sems["ready"], m)
                            dve.wait_ge(product, i * 8 + 4 + t + 1)
                            vec.tensor_tensor(prod[:], banks[1][t][:], sig[:, t, :], ALU.mult
                                              ).then_inc(sems["prod"], 1)
                            dve.wait_ge(sems["prod"], m + 1)
                            dve.sem_inc(bank_free[0], 1)
                            dve.sem_inc(bank_free[1], 1)
                            dve.wait_ge(sems["old"], (m + 1) * 16)
                            wait(dve, sems["stored"], m * 16)
                            vec.tensor_tensor(out_f[:], prod[:], old[:], ALU.add
                                              ).then_inc(sems["ready"], 1)
                        elif kind == "rope" and b == 1:
                            m = li * 4 + t
                            st = sems["steps"]
                            dve.wait_ge(product, i * 8 + 4 + t + 1)
                            wait(dve, sems["ready"], m)
                            a, c = banks[0][t], banks[1][t]
                            vec.tensor_tensor(ta[:], a[:], cos[:, tok], ALU.mult).then_inc(st, 1)
                            vec.tensor_tensor(tb[:], c[:], sin[:, tok], ALU.mult).then_inc(st, 1)
                            vec.tensor_tensor(tc_[:], c[:], cos[:, tok], ALU.mult).then_inc(st, 1)
                            vec.tensor_tensor(td[:], a[:], sin[:, tok], ALU.mult).then_inc(st, 1)
                            dve.wait_ge(st, m * 6 + 4)
                            dve.sem_inc(bank_free[0], 1)
                            dve.sem_inc(bank_free[1], 1)
                            vec.tensor_tensor(ta[:], ta[:], tb[:], ALU.subtract).then_inc(st, 1)
                            vec.tensor_tensor(tc_[:], tc_[:], td[:], ALU.add).then_inc(st, 1)
                            dve.wait_ge(sems["hi_a"], m + 1)
                            vec.tensor_tensor(rope_out[1][:], ta[:], rope_out[0][:].bitcast(F32), ALU.subtract)
                            dve.wait_ge(sems["hi_b"], m + 1)
                            vec.tensor_tensor(rope_out[3][:], tc_[:], rope_out[2][:].bitcast(F32),
                                              ALU.subtract).then_inc(sems["ready"], 1)
                    if follows:
                        split_w(b, i + 1)
            each_pair(dve, body)
            if v and shared:
                split_v()
            if v:
                for n, (blk, h) in enumerate(v_items):
                    dve.wait_ge(v_hi, n + 1)
                    vec.tensor_tensor(v_out[n % 2][:, :, 1, :],
                                      banks[(n // 4) % 2][n % 4][:, 0:v_n].rearrange(
                                          "p (h d) -> p h d", d=HEAD_DIM),
                                      v_out[n % 2][:, :, 0, :].bitcast(F32), ALU.subtract).then_inc(v_ready, 1)

        @block.tensor
        def _(pe):
            def body(g, li, i, follows):
                first = isinstance(i, int) and i == 0
                for b in range(2):
                    pe.wait_ge(w_lo_ok[b], i + 1)
                    for t in range(NTC):
                        if first and b == 0:
                            pe.wait_ge(x_lo, need[t])
                        wait(pe, bank_free[b], (i - 1) * 4 + t + 1 if isinstance(i, int) else i * 4 + (t - 3))
                        tok = slice(t * TC, (t + 1) * TC)
                        for k in range(kcs[b]):
                            cols = slice(k * P, (k + 1) * P)
                            nc.tensor.matmul(banks[b][t][:], w_hi[b][:, cols], hi[b][:, k, tok],
                                             start=(k == 0), stop=False)
                            nc.tensor.matmul(banks[b][t][:], w_hi[b][:, cols], lo[b][:, k, tok],
                                             start=False, stop=False)
                            last = nc.tensor.matmul(banks[b][t][:], w_lo[b][:, cols], hi[b][:, k, tok],
                                                    start=False, stop=(k == kcs[b] - 1))
                        last.then_inc(product, 1)

            def pe_pairs(i):
                body(0, i, i, True)
            repeat(pe, pairs, pe_pairs)
            if v:
                pe.wait_ge(v_w_lo, 1)
                for n, (blk, h) in enumerate(v_items):
                    if n < 8:
                        pe.wait_ge(bank_free[n // 4], 4 * (pairs - 1) + n % 4 + 1)
                    else:
                        pe.wait_ge(v_ready, n - 7)
                    out = banks[(n // 4) % 2][n % 4][:, 0:v_n]
                    tok = slice(blk * P, (blk + 1) * P)
                    for k in range(kc_v):
                        cols = slice(k * v_cols + h * v_n, k * v_cols + (h + 1) * v_n)
                        nc.tensor.matmul(out, hi[0][:, k, tok], wv_hi[:, cols], start=(k == 0), stop=False)
                        nc.tensor.matmul(out, hi[0][:, k, tok], wv_lo[:, cols], start=False, stop=False)
                        last = nc.tensor.matmul(out, lo[0][:, k, tok], wv_hi[:, cols],
                                                start=False, stop=(k == kc_v - 1))
                    last.then_inc(v_prod, 1)

        @block.gpsimd
        def _(pool):
            def body(g, li, i, follows):
                kind, _, arg = segments[g]
                sems = seg_sems[g]
                for b in range(2):
                    for t in range(NTC):
                        n = li * 8 + b * 4 + t
                        tok = slice(t * TC, (t + 1) * TC)
                        row = li * 2 + b
                        if kind in ("raw", "silu", "resid"):
                            pool.wait_ge(sems["ready"], n + 1)
                            pool.dma_start(arg["dst"].rearrange("(r p) t -> r p t", p=P)[row, :, tok],
                                           out_f[:]).then_inc(sems["stored"], 16)
                        elif kind == "split":
                            pool.wait_ge(sems["ready"], n + 1)
                            for part, tile in ((0, out_h), (1, out_l)):
                                pool.dma_start(arg["dst"][part][li * 2 + b, :, tok],
                                               tile[:].bitcast(F32)).then_inc(sems["stored"], 16)
                        elif kind == "gate" and b == 1:
                            pool.wait_ge(sems["ready"], li * 4 + t + 1)
                            pool.dma_start(arg["dst"].rearrange("(r p) t -> r p t", p=P)[li, :, tok],
                                           out_f[:]).then_inc(sems["stored"], 16)
                        elif kind == "rope" and b == 1:
                            pool.wait_ge(sems["ready"], li * 4 + t + 1)
                            for half in range(2):
                                for part in range(2):
                                    pool.dma_start(arg["dst"][part][half, li, :, tok],
                                                   rope_out[2 * half + part][:].bitcast(F32)).then_inc(sems["stored"], 16)
            for g, (kind, n, _) in enumerate(segments):
                repeat(pool, n, lambda li, g=g: body(g, li, None, True))
            if v:
                for n, (blk, h) in enumerate(v_items):
                    pool.wait_ge(v_ready, n + 1)
                    pool.dma_start(v_dst[h * v_heads:(h + 1) * v_heads, :, blk].rearrange("h p d -> p h d"),
                                   v_out[n % 2][:].bitcast(F32).rearrange("p h two d -> p h (two d)")
                                   ).then_inc(v_stored[n % 2], 16)
                for b in range(2):
                    pool.wait_ge(v_stored[b], 16 * (len(v_items) // 2))
            for g, (kind, n, _) in enumerate(segments):
                pool.wait_ge(seg_sems[g]["stored"], per[kind] * n)


def norm_phase(nc, consts, name, jobs):
    from contextlib import ExitStack
    with ExitStack() as ctx:
        s = Scope(nc, ctx, name)
        kmax = max(j[2] for j in jobs)
        x = [s.sb(f"x{b}", [P, kmax, TC]) for b in range(2)]
        sq = s.sb("sq", [P, kmax, TC])
        y = [s.sb(f"y{b}", [P, kmax, TC]) for b in range(2)]
        rstd = s.sb("rstd", [P, TC])
        std = s.sb("std", [P, TC])
        gains = [s.sb(f"gain{n}", [P, j[2]]) for n, j in enumerate(jobs)]
        biases = [s.sb(f"bias{n}", [P, j[2]]) for n, j in enumerate(jobs)]
        mean_ps, sq_ps = s.ps("mean", [P, TC]), s.ps("sumsq", [P, TC])
        x_in = [s.sem(f"x_in{b}") for b in range(2)]
        stored = [s.sem(f"stored{b}") for b in range(2)]
        par, summed, centred, squared, sumsq, var, rooted, scaled, ready, inv = (
            s.sem(n) for n in ("par", "summed", "centred", "squared", "sumsq", "var", "rooted", "scaled", "ready", "inv"))
        block = ctx.enter_context(nc.Block())
        items = [(j, t) for j in range(len(jobs)) for t in range(NTC)]
        n_par = sum(2 if j[4] is not None else 1 for j in jobs)
        n_ln = [sum(1 for j, _ in items[:n] if jobs[j][4] is not None) for n in range(len(items) + 1)]

        @block.sync
        def _(sp):
            for j, job in enumerate(jobs):
                sp.dma_start(gains[j][:], job[3]).then_inc(par, 16)
                if job[4] is not None:
                    sp.dma_start(biases[j][:], job[4]).then_inc(par, 16)
            for n, (j, t) in enumerate(items):
                if n >= 2:
                    sp.wait_ge(ready, n - 1)
                sp.dma_start(x[n % 2][:, 0:jobs[j][2], :],
                             jobs[j][0].rearrange("(k p) t -> p k t", p=P)[:, :, t * TC:(t + 1) * TC]
                             ).then_inc(x_in[n % 2], 16)

        @block.tensor
        def _(pe):
            for n, (j, t) in enumerate(items):
                k_n, ln = jobs[j][2], jobs[j][4] is not None
                if ln:
                    pe.wait_ge(x_in[n % 2], 16 * (n // 2 + 1))
                    if n_ln[n]:
                        pe.wait_ge(centred, n_ln[n])
                    for k in range(k_n):
                        last = nc.tensor.matmul(mean_ps[:], consts["ones"][:], x[n % 2][:, k, :],
                                                start=(k == 0), stop=(k == k_n - 1))
                    last.then_inc(summed, 1)
                pe.wait_ge(squared, n + 1)
                if n:
                    pe.wait_ge(var, n)
                for k in range(k_n):
                    last = nc.tensor.matmul(sq_ps[:], consts["ones"][:], sq[:, k, :],
                                            start=(k == 0), stop=(k == k_n - 1))
                last.then_inc(sumsq, 1)

        @block.scalar
        def _(act):
            act.wait_ge(par, 16 * n_par)
            for n, (j, t) in enumerate(items):
                k_n, ln = jobs[j][2], jobs[j][4] is not None
                if ln:
                    act.wait_ge(centred, n_ln[n + 1])
                else:
                    act.wait_ge(x_in[n % 2], 16 * (n // 2 + 1))
                if n:
                    act.wait_ge(sumsq, n)
                act.activation(sq[:, 0:k_n, :], x[n % 2][:, 0:k_n, :], ACT.Square).then_inc(squared, 1)
                act.wait_ge(var, n + 1)
                act.activation(std[:], rstd[:], ACT.Sqrt).then_inc(rooted, 1)
                act.wait_ge(scaled, n + 1)
                if n >= 2:
                    act.wait_ge(stored[n % 2], 16 * (n // 2))
                for k in range(k_n):
                    last = act.activation(y[n % 2][:, k, :], x[n % 2][:, k, :], ACT.Identity,
                                          bias=(biases[j][:, k:k + 1] if ln else 0.0),
                                          scale=gains[j][:, k:k + 1])
                last.then_inc(ready, 1)

        @block.vector
        def _(dve):
            vec = nc.vector
            for n, (j, t) in enumerate(items):
                k_n, ln, width = jobs[j][2], jobs[j][4] is not None, jobs[j][2] * P
                if ln:
                    dve.wait_ge(summed, n_ln[n + 1])
                    for k in range(k_n):
                        last = vec.scalar_tensor_tensor(x[n % 2][:, k, :], mean_ps[:], -1.0 / width,
                                                        x[n % 2][:, k, :], ALU.mult, ALU.add)
                    last.then_inc(centred, 1)
                dve.wait_ge(sumsq, n + 1)
                if n:
                    dve.wait_ge(scaled, n)
                vec.tensor_scalar(rstd[:], sq_ps[:], 1.0 / width, jobs[j][5], ALU.mult, ALU.add).then_inc(var, 1)
                dve.wait_ge(rooted, n + 1)
                vec.reciprocal(rstd[:], std[:]).then_inc(inv, 1)
                dve.wait_ge(inv, n + 1)
                if n == 0 or not ln:
                    dve.wait_ge(x_in[n % 2], 16 * (n // 2 + 1))
                for k in range(k_n):
                    last = vec.tensor_tensor(x[n % 2][:, k, :], x[n % 2][:, k, :], rstd[:], ALU.mult)
                last.then_inc(scaled, 1)

        @block.gpsimd
        def _(pool):
            for n, (j, t) in enumerate(items):
                pool.wait_ge(ready, n + 1)
                pool.dma_start(jobs[j][1].rearrange("(k p) t -> p k t", p=P)[:, :, t * TC:(t + 1) * TC],
                               y[n % 2][:, 0:jobs[j][2], :]).then_inc(stored[n % 2], 16)
            for b in range(2):
                pool.wait_ge(stored[b], 16 * len(items[b::2]))


def key_rope_phase(nc, tables, src, dst):
    from contextlib import ExitStack
    half = ROPE // 2
    with ExitStack() as ctx:
        s = Scope(nc, ctx, "kr")
        a, b, cos, sin, t1, t2 = (s.sb(n, [half, SEQ]) for n in ("a", "b", "cos", "sin", "t1", "t2"))
        r = [s.sb(f"r{n}", [half, SEQ]) for n in range(2)]
        out = [[s.sb(f"out{n}{part}", [half, SEQ], F32R) for part in range(2)] for n in range(2)]
        loaded, steps, stored = s.sem("loaded"), s.sem("steps"), s.sem("stored")
        block = ctx.enter_context(nc.Block())

        @block.sync
        def _(sp):
            for dst_t, src_t in ((a, src[0:half]), (b, src[half:ROPE]), (cos, tables[0][0:half]),
                                 (sin, tables[1][0:half])):
                sp.dma_start(dst_t[:], src_t).then_inc(loaded, 16)
            sp.wait_ge(steps, 10)
            for n in range(2):
                for part in range(2):
                    sp.dma_start(dst[part][n * half:(n + 1) * half], out[n][part][:].bitcast(F32)).then_inc(stored, 16)
            sp.wait_ge(stored, 64)

        @block.vector
        def _(dve):
            n = 0

            def chain(op):
                nonlocal n
                op.then_inc(steps, 1)
                n += 1
                dve.wait_ge(steps, n)

            dve.wait_ge(loaded, 64)
            vec = nc.vector
            for i, (x, y, op) in enumerate(((a, b, ALU.subtract), (b, a, ALU.add))):
                chain(vec.tensor_tensor(t1[:], x[:], cos[:], ALU.mult))
                chain(vec.tensor_tensor(t2[:], y[:], sin[:], ALU.mult))
                chain(vec.tensor_tensor(r[i][:], t1[:], t2[:], op))
                chain(vec.tensor_copy(out[i][0][:], r[i][:]))
                chain(vec.tensor_tensor(out[i][1][:], r[i][:], out[i][0][:].bitcast(F32), ALU.subtract))


def attention_phase(nc, consts, name, cfg):
    from contextlib import ExitStack
    with ExitStack() as ctx:
        s = Scope(nc, ctx, name)
        rows, qw, kw, vb = cfg["rows"], cfg["q_cols"], cfg["k_cols"], cfg["v_blocks"]
        scale, its, chunks = cfg["scale"], cfg["iterations"], cfg["chunks"]
        steps, items, sinks = cfg["steps"], cfg["items"], cfg["sinks"]
        blocks = qw // P
        pad = cfg["pad"]
        lag = 2
        kr = rows + 1
        q_hi = [s.sb(f"qh{b}", [kr, qw], F32R) for b in range(2)]
        q_lo = [s.sb(f"ql{b}", [kr, qw], F32R) for b in range(2)]
        k_hi = [s.sb(f"kh{b}", [kr, kw], F32R) for b in range(2)]
        k_lo = [s.sb(f"kl{b}", [kr, kw], F32R) for b in range(2)]
        vals = [s.sb(f"v{b}", [P, vb, P], F32R) for b in range(2)]
        prob = [s.sb(f"p{b}", [P, TC]) for b in range(3)]
        p_hi = [s.sb(f"ph{b}", [P, TC], F32R) for b in range(3)]
        p_lo = [s.sb(f"pl{b}", [P, TC], F32R) for b in range(3)]
        acc = [s.sb(f"acc{b}", [P, TC]) for b in range(2)]
        n_mx = cfg["max_cols"]
        mx, m_all = s.sb("mx", [P, n_mx]), s.sb("m_all", [P, blocks])
        m_t = s.sb("m_t", [blocks, P], F32R)
        o_low, o_sum, o_div, den_inv = (s.sb(n, [HEAD_DIM, TC]) for n in ("o_low", "o_sum", "o_div", "den_inv"))
        gate = [s.sb(f"gate{b}", [HEAD_DIM, TC]) for b in range(2)]
        o_out = [s.sb(f"o_out{b}", [HEAD_DIM, TC]) for b in range(2)]
        if sinks is not None:
            sink_q, sink_t = s.sb("sink_q", [P, GROUP]), s.sb("sink_t", [blocks, 1])
            sink_e = s.sb("sink_e", [blocks, P])
            sink_row = [s.sb(f"sink_row{b}", [1, qw]) for b in range(2)]
            sink_in, sink_e_ok, sink_row_in = s.sem("sink_in"), s.sem("sink_e_ok"), [s.sem(f"sink_row_in{b}") for b in range(2)]
        score = [s.ps(f"score{b}", [P, TC]) for b in range(3)]
        mx_w = cfg["max_width"]
        mx_ps = [s.ps(f"mx{b}", [P, mx_w]) for b in range(2 * TC // mx_w)]
        o_ps = [s.ps(f"o{b}", [P, TC]) for b in range(2)]
        den_ps = s.ps("den", [P, TC])
        ld_a, ld_b, mrow = ([s.sem(f"{n}{b}") for b in range(2)] for n in ("load_a", "load_b", "max_row"))
        gate_in, stored = ([s.sem(f"{n}{b}") for b in range(2)] for n in ("gate_in", "stored"))
        (const_ok, scores, probs, p_hi_ok, p_lo_ok, summed, weighed, mx_prod, mx_done, m_done, m_turned,
         m_t_ok, low_ok, sum_ok, den_ok, inv_ok, div_ok, gated) = (s.sem(n) for n in (
             "const_ok", "scores", "probs", "p_hi_ok", "p_lo_ok", "summed", "weighed", "mx_prod", "mx_done",
             "m_done", "m_turned", "m_t_ok", "low_ok", "sum_ok", "den_ok", "inv_ok", "div_ok", "gated"))
        block = ctx.enter_context(nc.Block())

        ns = [len(x) for x in steps]
        ni = [len(x) for x in items]
        def step0(it, b):
            return it * sum(ns) + (ns[0] if b else 0)

        def chunk0(it, b):
            return it * 2 * chunks + b * chunks

        def item0(it, b):
            return it * sum(ni) + (ni[0] if b else 0)

        def unit(it, b):
            return it * 2 + b

        sink_ops = 1 if sinks is not None else 0
        def sum0(it, b):
            return step0(it, b) + sink_ops * chunk0(it, b)

        last_step = [[max(k for k, st in enumerate(steps[b]) if st["chunk"] == c) for c in range(chunks)]
                     for b in range(2)]
        first_at, last_at = cfg["items_from"], cfg["items_to"]

        def after(b, k):
            n, span = ni[1 - b], last_at[b] - first_at[b] + 1
            if not first_at[b] <= k <= last_at[b]:
                return []
            j = k - first_at[b]
            return list(range(j * n // span, (j + 1) * n // span))

        def next_of(it, b):
            return (it, 1) if b == 0 else (it + 1, 0)

        def is_first(it, b):
            return isinstance(it, int) and it == 0 and b == 0

        @block.sync
        def _(sp):
            def load(it, b):
                u = unit(it, b)
                if not (isinstance(it, int) and it == 0):
                    sp.wait_ge(weighed, step0(it, b) - (ns[1 - b]))
                for dst, src in cfg["load_a"](it, b, q_hi[b], k_hi[b]):
                    sp.dma_start(dst.bitcast(F32), src).then_inc(ld_a[b], 16)
                if sinks is not None:
                    if not is_first(it, b):
                        sp.wait_ge(sink_e_ok, u)
                    sp.dma_start(sink_q[:], sinks[it * GROUP:(it + 1) * GROUP].partition_broadcast(P)
                                 if isinstance(it, int) else
                                 sinks[bass.ds(it * GROUP, GROUP)].partition_broadcast(P)).then_inc(sink_in, 16)
                    own = sinks[bass.ds(it * GROUP, GROUP)].rearrange("(j x) -> j x", x=1)
                    for n in range(blocks // GROUP):
                        sp.dma_start(sink_t[n * GROUP:(n + 1) * GROUP, :], own).then_inc(sink_in, 16)
                for dst, src in cfg["load_b"](it, b, q_lo[b], k_lo[b], vals[b]):
                    sp.dma_start(dst.bitcast(F32), src).then_inc(ld_b[b], 16)

            def load_max(it, b):
                u = unit(it, b)
                sp.wait_ge(m_t_ok, u + 1)
                sp.dma_start(q_hi[b][rows:rows + 1, :].bitcast(F32).rearrange("o (n q) -> o n q", q=P),
                             m_t[:].bitcast(F32)
                             ).then_inc(mrow[b], 16)
                if sinks is not None:
                    sp.wait_ge(sink_e_ok, u + 1)
                    sp.dma_start(sink_row[b][:].rearrange("o (n q) -> o n q", q=P), sink_e[:]
                                 ).then_inc(sink_row_in[b], 16)

            def load_gate(it, b, c):
                n = chunk0(it, b) + c
                if not (is_first(it, b) and c < 2):
                    sp.wait_ge(gated, n - 1)
                sp.dma_start(cfg["gate"](it, b, c, gate[c % 2]), cfg["gate_src"](it, b, c)
                             ).then_inc(gate_in[c % 2], 16)

            def store(it, b, c):
                sp.wait_ge(gated, chunk0(it, b) + c + 1)
                sp.dma_start(cfg["dst"](it, b, c), cfg["gate"](it, b, c, o_out[c % 2])
                             ).then_inc(stored[c % 2], 16)

            load(0, 0)
            load_max(0, 0)

            def body(it):
                for b in range(2):
                    follows = b == 0 or not (isinstance(it, int) and it == its - 1)
                    nxt = next_of(it, b)
                    if follows:
                        load(*nxt)
                    if b == 1:
                        store(it, 0, chunks - 1)
                    elif not is_first(it, b):
                        store(it - 1, 1, chunks - 1)
                    load_gate(it, b, 0)
                    for c in range(1, chunks):
                        load_gate(it, b, c)
                        store(it, b, c - 1)
                        if follows and c == cfg["max_after_chunk"]:
                            load_max(*nxt)
            repeat(sp, its, body, last_apart=True)
            store(its - 1, 1, chunks - 1)
            for b in range(2):
                sp.wait_ge(stored[b], 16 * its * chunks)

        @block.tensor
        def _(pe):
            def mm(out, lhs, rhs, start, stop):
                return nc.tensor.matmul(out, lhs, rhs, start=start, stop=stop)

            def item(it, b, n):
                x = items[b][n]
                buf = mx_ps[n % len(mx_ps)]
                if n == 0:
                    pe.wait_ge(ld_a[b], 16 * cfg["n_load_a"] * (it + 1))
                prev = item0(it, b) + n - len(mx_ps) + 1
                if n < len(mx_ps):
                    if not is_first(it, b):
                        pe.wait_ge(m_t_ok, unit(it, b))
                else:
                    pe.wait_ge(mx_done, prev)
                for q, k, width, mask, col in x["products"]:
                    lastm = mm(buf[:, col:col + width], q_hi[b][0:rows, q:q + P], k_hi[b][0:rows, k:k + width],
                               True, mask is None)
                    if mask is not None:
                        mt, m0, mw = mask
                        lastm = mm(buf[:, col + m0:col + m0 + mw], consts["ident_b"][:],
                                   consts[mt][:, 2 * P - mw:2 * P] if mt == "window_q" else consts[mt][:],
                                   False, True)
                lastm.then_inc(mx_prod, 1)

            def turn(it, b):
                pe.wait_ge(m_done, unit(it, b) + 1)
                nc.tensor.transpose(mx_ps[0][0:blocks, 0:P], m_all[:], consts["ident"][:]).then_inc(m_turned, 1)

            def weigh(it, b, k):
                st = steps[b][k]
                c, off = st["chunk"], st["off"]
                n = step0(it, b) + k
                pe.wait_ge(p_lo_ok, n + 1)
                if st["first"] and not (is_first(it, b) and c < 2):
                    pe.wait_ge(sum_ok, chunk0(it, b) + c - 1)
                if k == 0:
                    pe.wait_ge(ld_b[b], 16 * cfg["n_load_b"] * (it + 1))
                v = vals[b][:, st["v"], :]
                out = o_ps[c % 2][:, off:TC]
                mm(out, v, p_hi[k % 3][:, off:TC], st["first"], False)
                mm(out, v, p_lo[k % 3][:, off:TC], False, st["last"]).then_inc(weighed, 1)

            def denominator(it, b, c):
                n = chunk0(it, b) + c
                pe.wait_ge(summed, sum0(it, b) + last_step[b][c] + 1 + sink_ops * (c + 1))
                if not (is_first(it, b) and c == 0):
                    pe.wait_ge(inv_ok, n)
                mm(den_ps[0:HEAD_DIM, :], consts["ones"][:, 0:HEAD_DIM], acc[c % 2][:], True, True
                   ).then_inc(den_ok, 1)

            pe.wait_ge(const_ok, 1)
            for n in range(ni[0]):
                item(0, 0, n)
            turn(0, 0)

            def body(it):
                for b in range(2):
                    follows = b == 0 or not (isinstance(it, int) and it == its - 1)
                    nxt = next_of(it, b)
                    pe.wait_ge(ld_b[b], 16 * cfg["n_load_b"] * (it + 1))
                    pe.wait_ge(mrow[b], 16 * (it + 1))
                    for k, st in enumerate(steps[b]):
                        n = step0(it, b) + k
                        if k >= 3:
                            pe.wait_ge(p_hi_ok, n - 2)
                        elif not is_first(it, b):
                            pe.wait_ge(p_hi_ok, step0(it, b))
                        off, kb, q0 = st["off"], st["k"] * P, st["chunk"] * TC
                        out = score[k % 3][:, off:TC]
                        q = slice(q0 + off, q0 + TC)
                        ks = slice(kb, kb + P)
                        low = kr if pad else rows
                        mm(out, k_hi[b][0:kr, ks], q_hi[b][0:kr, q], True, False)
                        mm(out, k_hi[b][0:low, ks], q_lo[b][0:low, q], False, False)
                        if st["mask"]:
                            w = cfg["mask_width"]
                            mm(score[k % 3][:, off:off + w], consts["ident_b"][:], consts[st["mask"]][:].rearrange(
                                "p j q -> p (j q)")[:, 0:w], False, False)
                        mm(out, k_lo[b][0:low, ks], q_hi[b][0:low, q], False, True).then_inc(scores, 1)
                        if follows:
                            for x in after(b, k):
                                item(*nxt, x)
                            if k == last_at[b] + 2:
                                turn(*nxt)
                        if k >= lag:
                            weigh(it, b, k - lag)
                        for c in range(chunks - 1):
                            if k == last_step[b][c] + lag + 1:
                                denominator(it, b, c)
                    for k in range(ns[b] - lag, ns[b]):
                        weigh(it, b, k)
                    for c in range(chunks):
                        if c == chunks - 1 or last_step[b][c] + lag + 1 >= ns[b]:
                            denominator(it, b, c)
            repeat(pe, its, body, last_apart=True)

        @block.scalar
        def _(act):
            def sink_exp(it, b):
                if sinks is None:
                    return
                u = unit(it, b)
                act.wait_ge(m_t_ok, u + 1)
                act.wait_ge(sink_in, 16 * (1 + blocks // GROUP) * (u + 1))
                if not is_first(it, b):
                    act.wait_ge(sink_row_in[1 - b], 16 * (it + 1 if b else it))
                act.activation(sink_e[:], m_t[:].bitcast(F32), ACT.Exp, bias=sink_t[:], scale=scale
                               ).then_inc(sink_e_ok, 1)

            def low_half(it, b, c):
                n = chunk0(it, b) + c
                act.wait_ge(weighed, step0(it, b) + last_step[b][c] + 1)
                if not (is_first(it, b) and c == 0):
                    act.wait_ge(sum_ok, n)
                act.copy(o_low[:], o_ps[c % 2][HEAD_DIM:P, :]).then_inc(low_ok, 1)

            sink_exp(0, 0)

            def body(it):
                for b in range(2):
                    follows = b == 0 or not (isinstance(it, int) and it == its - 1)
                    for k, st in enumerate(steps[b]):
                        n = step0(it, b) + k
                        off = st["off"]
                        act.wait_ge(scores, n + 1)
                        if k >= 3:
                            act.wait_ge(p_lo_ok, n - 2)
                            act.wait_ge(summed, sum0(it, b) + k - 2 + sink_ops * steps[b][k - 3]["chunk"])
                        elif not is_first(it, b):
                            act.wait_ge(p_lo_ok, step0(it, b))
                            act.wait_ge(summed, sum0(it, b))
                        act.activation(prob[k % 3][:, off:TC], score[k % 3][:, off:TC], ACT.Exp, scale=scale
                                       ).then_inc(probs, 1)
                        if k >= 3:
                            act.wait_ge(weighed, n - 2)
                        elif not is_first(it, b):
                            act.wait_ge(weighed, step0(it, b))
                        act.activation(p_hi[k % 3][:, off:TC], score[k % 3][:, off:TC], ACT.Exp, scale=scale
                                       ).then_inc(p_hi_ok, 1)
                        if follows and k == last_at[b] + 3:
                            sink_exp(*next_of(it, b))
                        for c in range(chunks):
                            if k == last_step[b][c] + lag + 1:
                                low_half(it, b, c)
                    for c in range(chunks):
                        if last_step[b][c] + lag + 1 >= ns[b]:
                            low_half(it, b, c)
            repeat(act, its, body, last_apart=True)

        @block.vector
        def _(dve):
            vec = nc.vector
            for b in range(2):
                vec.memset(k_hi[b][rows:kr, :].bitcast(F32), 1.0)
                if pad:
                    vec.memset(k_lo[b][rows:kr, :].bitcast(F32), 0.0)
                    vec.memset(q_lo[b][rows:kr, :].bitcast(F32), 0.0)
            vec.memset(mx[:], -3e38).then_inc(const_ok, 1)

            def item(it, b, n):
                x = items[b][n]
                dve.wait_ge(mx_prod, item0(it, b) + n + 1)
                if n == 0 and not is_first(it, b):
                    dve.wait_ge(m_done, unit(it, b))
                buf = mx_ps[n % len(mx_ps)]
                src = buf[:].rearrange("p (j k) -> p j k", k=x["stride"])[:, 0:x["groups"], 0:x["width"]]
                vec.tensor_reduce(mx[:, x["col"]:x["col"] + x["groups"]], src, AX.X, ALU.max
                                  ).then_inc(mx_done, 1)

            def gather(it, b):
                u = unit(it, b)
                dve.wait_ge(mx_done, item0(it, b) + ni[b])
                if not is_first(it, b):
                    dve.wait_ge(m_turned, u)
                if sinks is None:
                    for n, (col, per, out) in enumerate(cfg["gather"]):
                        op = vec.tensor_reduce(m_all[:, out:out + 4],
                                               mx[:, col:col + 4 * per].rearrange("p (i k) -> p i k", k=per),
                                               AX.X, ALU.max)
                else:
                    dve.wait_ge(sink_in, 16 * (1 + blocks // GROUP) * (u + 1))
                    op = vec.scalar_tensor_tensor(
                        m_all[:].rearrange("p (n j) -> p n j", j=GROUP),
                        sink_q[:].rearrange("p (x j) -> p x j", x=1).broadcast_to([P, blocks // GROUP, GROUP]),
                        1.0 / scale, mx[:].rearrange("p (n j) -> p n j", j=GROUP), ALU.mult, ALU.max)
                op.then_inc(m_done, 1)

            def negate(it, b):
                u = unit(it, b)
                dve.wait_ge(m_turned, u + 1)
                if not is_first(it, b):
                    dve.wait_ge(mrow[1 - b], 16 * (it + 1 if b else it))
                    if sinks is not None:
                        dve.wait_ge(sink_e_ok, u)
                vec.tensor_scalar(m_t[:], mx_ps[0][0:blocks, 0:P], -1.0, None, ALU.mult).then_inc(m_t_ok, 1)

            def finish(it, b, c):
                n = chunk0(it, b) + c
                dve.wait_ge(low_ok, n + 1)
                if not (is_first(it, b) and c == 0):
                    dve.wait_ge(div_ok, n)
                vec.tensor_tensor(o_sum[:], o_ps[c % 2][0:HEAD_DIM, :], o_low[:], ALU.add).then_inc(sum_ok, 1)
                dve.wait_ge(den_ok, n + 1)
                vec.reciprocal(den_inv[:], den_ps[0:HEAD_DIM, :]).then_inc(inv_ok, 1)
                dve.wait_ge(sum_ok, n + 1)
                dve.wait_ge(inv_ok, n + 1)
                if not (is_first(it, b) and c == 0):
                    dve.wait_ge(gated, n)
                vec.tensor_tensor(o_div[:], o_sum[:], den_inv[:], ALU.mult).then_inc(div_ok, 1)

            for n in range(ni[0]):
                item(0, 0, n)
            gather(0, 0)
            negate(0, 0)

            def body(it):
                for b in range(2):
                    follows = b == 0 or not (isinstance(it, int) and it == its - 1)
                    nxt = next_of(it, b)
                    for k, st in enumerate(steps[b]):
                        n = step0(it, b) + k
                        off = st["off"]
                        dve.wait_ge(p_hi_ok, n + 1)
                        vec.tensor_tensor(p_lo[k % 3][:, off:TC], prob[k % 3][:, off:TC],
                                          p_hi[k % 3][:, off:TC].bitcast(F32), ALU.subtract
                                          ).then_inc(p_lo_ok, 1)
                        if follows:
                            for x in after(b, k):
                                item(*nxt, x)
                            if k == last_at[b]:
                                gather(*nxt)
                            if k == last_at[b] + 2:
                                negate(*nxt)
                        for c in range(chunks):
                            if k == last_step[b][c] + lag + 2:
                                finish(it, b, c)
                    for c in range(chunks):
                        if last_step[b][c] + lag + 2 >= ns[b]:
                            finish(it, b, c)
            repeat(dve, its, body, last_apart=True)

        @block.gpsimd
        def _(pool):
            def out_gate(it, b, c):
                n = chunk0(it, b) + c
                pool.wait_ge(div_ok, n + 1)
                pool.wait_ge(gate_in[c % 2], 16 * (it * chunks + (chunks // 2 if b else 0) + c // 2 + 1))
                if not (is_first(it, b) and c < 2):
                    pool.wait_ge(stored[c % 2], 16 * (it * chunks + (chunks // 2 if b else 0) + c // 2))
                pool.tensor_tensor(o_out[c % 2][:], o_div[:], gate[c % 2][:], ALU.mult).then_inc(gated, 1)

            def body(it):
                for b in range(2):
                    for k, st in enumerate(steps[b]):
                        n = step0(it, b) + k
                        c, off = st["chunk"], st["off"]
                        done = sum0(it, b) + k + sink_ops * c
                        pool.wait_ge(probs, n + 1)
                        if st["first"]:
                            if not (is_first(it, b) and c < 2):
                                pool.wait_ge(den_ok, chunk0(it, b) + c - 1)
                            pool.tensor_tensor(acc[c % 2][:], prob[k % 3][:], consts["zeros"][:], ALU.add
                                               ).then_inc(summed, 1)
                        else:
                            pool.wait_ge(summed, done)
                            pool.tensor_tensor(acc[c % 2][:, off:TC], acc[c % 2][:, off:TC],
                                               prob[k % 3][:, off:TC], ALU.add).then_inc(summed, 1)
                        if st["last"] and sinks is not None:
                            pool.wait_ge(summed, done + 1)
                            pool.wait_ge(sink_row_in[b], 16 * (it + 1))
                            pool.tensor_tensor(acc[c % 2][0:1, :], acc[c % 2][0:1, :],
                                               sink_row[b][:, c * TC:(c + 1) * TC], ALU.add).then_inc(summed, 1)
                        for cc in range(chunks):
                            if k == last_step[b][cc] + lag + 3:
                                out_gate(it, b, cc)
                    for cc in range(chunks):
                        if last_step[b][cc] + lag + 3 >= ns[b]:
                            out_gate(it, b, cc)
            repeat(pool, its, body, last_apart=True)


def swa_config(q, k, v, gates, out, sinks):
    half_b = NB // 2
    steps, items = [], []
    for b in range(2):
        st, it = [], []
        for c in range(half_b):
            own = c + b
            blks = ([(own - 1, "prev_t")] if own > 0 else []) + [(own, "causal_t")]
            for n, (kb, mask) in enumerate(blks):
                st.append(dict(chunk=c, k=kb, v=kb, off=0, mask=mask, first=n == 0, last=n == len(blks) - 1))
            width = P * len(blks)
            it.append(dict(products=[(c * TC + j * P, blks[0][0] * P, width, ("window_q", 0, width), j * 2 * P)
                                     for j in range(GROUP)],
                           stride=2 * P, groups=GROUP, width=width, col=c * GROUP))
        steps.append(st)
        items.append(it)

    def tok(b):
        return (half_b * b - b) * P, (half_b + b) * P

    def queries(it, b, tile, part):
        src = q[part].rearrange("s g (j r) (n t) -> s g r n j t", j=GROUP, t=P)
        for s in range(2):
            for j in range(GROUP):
                yield (tile[s * 32:(s + 1) * 32, :].rearrange("r (n j t) -> r n j t", j=GROUP, t=P)[:, :, j, :],
                       src[s, it, :, b * half_b:(b + 1) * half_b, j, :])

    def keys(it, b, tile, part):
        t0, n = tok(b)
        src = k[part].rearrange("s o (g r) t -> s (o g) r t", g=KV_HEADS)
        for s in range(2):
            yield tile[s * 32:(s + 1) * 32, 0:n], src[s, it, :, t0:t0 + n]

    def load_a(it, b, q_hi, k_hi):
        yield from queries(it, b, q_hi, 0)
        yield from keys(it, b, k_hi, 0)

    def load_b(it, b, q_lo, k_lo, vals):
        yield from queries(it, b, q_lo, 1)
        yield from keys(it, b, k_lo, 1)
        t0, n = tok(b)
        yield vals[:, 0:n // P, :], v[it, :, t0 // P:(t0 + n) // P]

    def heads(x, it, b, c):
        t0 = (b * half_b + c) * P
        return x.rearrange("(g j d) t -> g d j t", j=GROUP, d=HEAD_DIM)[it, :, :, t0:t0 + P]

    return dict(rows=HEAD_DIM, q_cols=SEQ * GROUP // 2, k_cols=(half_b + 1) * P, v_blocks=half_b + 1,
                scale=SWA_SCALE, iterations=KV_HEADS, chunks=half_b, steps=steps, items=items, sinks=sinks,
                max_cols=half_b * GROUP, max_width=2 * TC, items_from=(3, 3), items_to=(10, 10), pad=True,
                mask_width=TC, load_a=load_a, load_b=load_b, n_load_a=10, n_load_b=11,
                gate=lambda it, b, c, tile: tile[:].rearrange("d (j t) -> d j t", j=GROUP),
                gate_src=lambda it, b, c: heads(gates, it, b, c), dst=lambda it, b, c: heads(out, it, b, c),
                max_after_chunk=half_b - 1)


def mla_config(q_nope, q_rope, k_nope, k_rope, v, gates, out):
    steps, items, gather = [], [], []
    for c in range(NTC):
        for kb in range(4 * c + 4):
            off = max(0, kb - 4 * c) * P
            steps.append(dict(chunk=c, k=kb, v=kb, off=off, mask="causal_t" if kb >= 4 * c else None,
                              first=kb == 0, last=kb == 4 * c + 3))
        gather.append((len(items), c + 1, 4 * c))
        for i in range(4 * c, 4 * c + 4):
            for kc in range(c + 1):
                width = TC if kc < c else (i % 4 + 1) * P
                mask = ("causal_q", width - P, P) if kc == c else None
                items.append(dict(products=[(i * P, kc * TC, width, mask, 0)], stride=TC, groups=1,
                                  width=width, col=len(items)))

    def load(it, b, q_tile, k_tile, part):
        u = it * 2 + b
        half = ROPE // 2
        qr = q_rope[part].rearrange("s l (h r) t -> s (l h) r t", r=half)
        yield q_tile[0:NOPE, :], q_nope[part].rearrange("l (h d) t -> (l h) d t", d=NOPE)[u]
        for s in range(2):
            yield q_tile[NOPE + s * half:NOPE + (s + 1) * half, :], qr[s, u]
        yield k_tile[0:NOPE, :], k_nope[part].rearrange("l (h d) t -> (l h) d t", d=NOPE)[u]
        yield k_tile[NOPE:NOPE + ROPE, :], k_rope[part]

    def load_a(it, b, q_hi, k_hi):
        yield from load(it, b, q_hi, k_hi, 0)

    def load_b(it, b, q_lo, k_lo, vals):
        yield from load(it, b, q_lo, k_lo, 1)
        yield vals[:], v[it * 2 + b]

    def rows_of(x, it, b, c):
        return x.rearrange("(h d) t -> h d t", d=HEAD_DIM)[it * 2 + b, :, c * TC:(c + 1) * TC]

    return dict(rows=NOPE + ROPE, q_cols=SEQ, k_cols=SEQ, v_blocks=NB, scale=MLA_SCALE, iterations=HEADS // 2,
                chunks=NTC, steps=[steps, steps], items=[items, items], sinks=None, max_cols=len(items),
                max_width=TC, items_from=(8, 8), items_to=(34, 34), pad=False, mask_width=P,
                load_a=load_a, load_b=load_b, n_load_a=5, n_load_b=6, gather=gather,
                gate=lambda it, b, c, tile: tile[:],
                gate_src=lambda it, b, c: rows_of(gates, it, b, c), dst=lambda it, b, c: rows_of(out, it, b, c),
                max_after_chunk=NTC - 1)


def build(nc, a, out):
    from contextlib import ExitStack
    ctx = ExitStack()
    with ctx:
        def dram(name, shape, dt=F32):
            return nc.dram_tensor(f"scratch_{name}", shape, dt, kind="Internal").ap()

        def parts(name, shape):
            return [dram(f"{name}_hi", shape), dram(f"{name}_lo", shape)]

        consts = {}
        for n, shape, dt in (("ident", [P, P], F32), ("ident_b", [P, P], BF16), ("ones", [P, P], F32),
                             ("zeros", [P, TC], F32), ("causal_t", [P, GROUP, P], BF16),
                             ("prev_t", [P, GROUP, P], BF16), ("causal_q", [P, P], BF16),
                             ("window_q", [P, 2 * P], BF16)):
            consts[n] = ctx.enter_context(nc.sbuf_tensor(f"const_{n}", shape, dt))

        tables = [[dram(f"table{t}{f}", [P, SEQ]) for f in range(2)] for t in range(2)]
        tables_phase(nc, consts, a["positions"], a["inv"], tables)

        def close_layer(layer, x, attn, dst):
            summed, normed = dram(f"sum{layer}", [D_MODEL, SEQ]), dram(f"norm{layer}", [D_MODEL, SEQ])
            gemm_phase(nc, consts, f"wo{layer}", [(attn, KD)], [a[f"w_out{layer}_{b}"] for b in range(2)],
                       [("resid", KD // 2, dict(old=x, dst=summed))])
            norm_phase(nc, consts, f"ln{layer}", [(summed, normed, KD, a[f"ln_g{layer}"], a[f"ln_b{layer}"], LN_EPS)])
            gemm_phase(nc, consts, f"pe{layer}", [(normed, KD), (a[f"p{layer}"], PLE // P)],
                       [a[f"pe_gate{layer}"], a[f"pe_proj{layer}"]], [("gate", KD, dict(old=normed, dst=dst))])

        q0, k0 = parts("q0", [2, KV_HEADS, P, SEQ]), parts("k0", [2, 1, P, SEQ])
        v0 = dram("v0", [KV_HEADS, P, NB, P])
        z0, o0, x1 = (dram(n, [D_MODEL, SEQ]) for n in ("z0", "o0", "x1"))
        gemm_phase(nc, consts, "in0", [(a["x"], KD)], [a["w_in0_0"], a["w_in0_1"]],
                   [("rope", 4, dict(dst=q0)), ("rope", 1, dict(dst=k0)), ("silu", 4, dict(dst=z0))],
                   tables=tables[0], v=(a["w_v0"], KV_HEADS * HEAD_DIM, v0))
        attention_phase(nc, consts, "swa", swa_config(q0, k0, v0, z0, o0, a["sinks"]))
        close_layer(0, a["x"], o0, x1)

        c1 = dram("c1", [Q_LORA + P + KV_LORA, SEQ])
        cq, ckv = dram("cq", [Q_LORA, SEQ]), dram("ckv", [KV_LORA, SEQ])
        z1, o1 = dram("z1", [D_MODEL, SEQ]), dram("o1", [D_MODEL, SEQ])
        gemm_phase(nc, consts, "in1", [(x1, KD)], [a["w_in1_0"], a["w_in1_1"]],
                   [("raw", 3, dict(dst=c1)), ("silu", 4, dict(dst=z1))])
        norm_phase(nc, consts, "rms", [(c1[0:Q_LORA], cq, Q_LORA // P, a["q_norm"], None, RMS_EPS),
                                       (c1[Q_LORA + P:], ckv, KV_LORA // P, a["kv_norm"], None, RMS_EPS)])
        kr = parts("kr", [ROPE, SEQ])
        key_rope_phase(nc, tables[1], c1[Q_LORA:Q_LORA + ROPE], kr)
        qn, qr = parts("qn", [HEADS // 2, P, SEQ]), parts("qr", [2, 2, P, SEQ])
        gemm_phase(nc, consts, "uq", [(cq, Q_LORA // P)], [a["w_uq_0"], a["w_uq_1"]],
                   [("split", 4, dict(dst=qn)), ("rope", 2, dict(dst=qr))], tables=tables[1])
        kn, v1 = parts("kn", [HEADS // 2, P, SEQ]), dram("v1", [HEADS, P, NB, P])
        gemm_phase(nc, consts, "ukv", [(ckv, KV_LORA // P)], [a["w_uk_0"], a["w_uk_1"]],
                   [("split", 4, dict(dst=kn))], v=(a["w_uv"], HEADS * HEAD_DIM, v1))
        attention_phase(nc, consts, "mla", mla_config(qn, qr, kn, kr, v1, z1, o1))
        close_layer(1, x1, o1, out)


def column_tiles(w, order=None):
    w = w if order is None else w[:, order]
    k, n = w.shape
    return np.ascontiguousarray(w.reshape(k // P, P, n // P, P).transpose(2, 1, 0, 3)).reshape(n // P, P, k)


def lay_out(x, p, positions, w_out, ln_g, ln_b, pe_gate, pe_proj, l0_w_in, l0_sinks, l1_w_in, l1_q_norm,
            l1_kv_norm, l1_w_uq, l1_w_ukv):
    a = {"x": np.ascontiguousarray(x[0].T), "positions": positions[0], "sinks": l0_sinks}
    exps = [np.arange(h, dtype=np.float32) / np.float32(h) for h in (HEAD_DIM // 2, ROPE // 2)]
    a["inv"] = np.stack([np.tile(np.power(np.float32(THETA), -e), P // len(e)) for e in exps], 1).astype(np.float32)

    def slots(name, tiles):
        a[f"{name}_0"], a[f"{name}_1"] = np.ascontiguousarray(tiles[0::2]), np.ascontiguousarray(tiles[1::2])

    def by_tile(g):
        return np.ascontiguousarray(g.reshape(-1, P).T)

    for layer in range(DEPTH):
        slots(f"w_out{layer}", column_tiles(w_out[layer]))
        a[f"ln_g{layer}"], a[f"ln_b{layer}"] = by_tile(ln_g[layer]), by_tile(ln_b[layer])
        a[f"pe_gate{layer}"] = column_tiles(pe_gate[layer])
        a[f"pe_proj{layer}"] = column_tiles(pe_proj[layer])
        a[f"p{layer}"] = np.ascontiguousarray(p[layer, 0].T)

    def rotary(first, heads, dim, stride=None):
        stride, half = stride or dim, dim // 2
        per = P // half
        return np.concatenate([first + (g + np.arange(per))[:, None] * stride + s * half + np.arange(half)
                               for g in range(0, heads, per) for s in range(2)]).ravel()

    kv = KV_HEADS * HEAD_DIM
    q_end, k_end, v_end = D_MODEL, D_MODEL + kv, D_MODEL + 2 * kv
    slots("w_in0", column_tiles(l0_w_in, np.concatenate([
        rotary(0, HEADS, HEAD_DIM), rotary(q_end, KV_HEADS, HEAD_DIM), np.arange(v_end, l0_w_in.shape[1])])))

    def token_weights(w):
        k, n = w.shape
        return np.ascontiguousarray(w.reshape(k // P, P, n).transpose(1, 0, 2)).reshape(P, -1)

    a["w_v0"] = token_weights(l0_w_in[:, k_end:v_end])
    pad = np.zeros((D_MODEL, P - ROPE), l1_w_in.dtype)
    c = [Q_LORA, Q_LORA + KV_LORA, Q_LORA + KV_LORA + ROPE]
    slots("w_in1", column_tiles(np.concatenate(
        [l1_w_in[:, :c[0]], l1_w_in[:, c[1]:c[2]], pad, l1_w_in[:, c[0]:c[1]], l1_w_in[:, c[2]:]], 1)))
    a["q_norm"], a["kv_norm"] = by_tile(l1_q_norm), by_tile(l1_kv_norm)
    heads = np.arange(HEADS)[:, None]
    slots("w_uq", column_tiles(l1_w_uq, np.concatenate([
        (heads * (NOPE + ROPE) + np.arange(NOPE)).ravel(), rotary(NOPE, HEADS, ROPE, NOPE + ROPE)])))
    slots("w_uk", column_tiles(l1_w_ukv, (heads * 2 * NOPE + np.arange(NOPE)).ravel()))
    a["w_uv"] = token_weights(l1_w_ukv[:, (heads * 2 * NOPE + NOPE + np.arange(NOPE)).ravel()])
    return a


def kernel(x, p, positions, w_out, ln_g, ln_b, pe_gate, pe_proj, l0_w_in, l0_sinks, l1_w_in, l1_q_norm,
           l1_kv_norm, l1_w_uq, l1_w_ukv, **unused):
    import concourse.bacc as bacc
    from concourse.bass_utils import run_bass_kernel_spmd

    arrays = {f"in_{n}": np.ascontiguousarray(v) for n, v in lay_out(
        *(np.asarray(v) for v in (x, p, positions, w_out, ln_g, ln_b, pe_gate, pe_proj, l0_w_in, l0_sinks,
                                  l1_w_in, l1_q_norm, l1_kv_norm, l1_w_uq, l1_w_ukv))).items()}
    nc = bacc.Bacc("TRN2", target_bir_lowering=False, num_devices=1)
    ins = {n[3:]: nc.dram_tensor(n, v.shape, mybir.dt.from_np(v.dtype), kind="ExternalInput").ap()
           for n, v in arrays.items()}
    out = nc.dram_tensor("out_t", (D_MODEL, SEQ), F32, kind="ExternalOutput").ap()
    build(nc, ins, out)
    r = run_bass_kernel_spmd(nc, [arrays], core_ids=[0])
    return np.ascontiguousarray(r.results[0]["out_t"].T)[None]
```

```python
import numpy as np

import concourse.bass as bass
from concourse import mybir
from concourse.alu_op_type import AluOpType as ALU

ACT = mybir.ActivationFunctionType
AX = mybir.AxisListType
F32 = mybir.dt.float32
F32R = mybir.dt.float32r
BF16 = mybir.dt.bfloat16
I32 = mybir.dt.int32

P = 128
D_MODEL = 1024
SEQ = 2048
DEPTH = 2
HEADS = 16
HEAD_DIM = 64
KV_HEADS = 4
GROUP = HEADS // KV_HEADS
Q_LORA = 384
KV_LORA = 256
ROPE = 32
NOPE = 64
PLE = 256
ALPHA = (2 * DEPTH) ** 0.25
LN_EPS = 1e-5
RMS_EPS = 1e-6
THETA = 10000.0
TC = 512
NTC = SEQ // TC
NB = SEQ // P
KD = D_MODEL // P
BIG = -1e30
TAB_STEPS = 10
SWA_SCALE = HEAD_DIM ** -0.5
MLA_SCALE = (NOPE + ROPE) ** -0.5


def wait(eng, sem, value):
    if isinstance(value, int) and value <= 0:
        return
    eng.wait_ge(sem, value)


def repeat(eng, count, body, last_apart=False):
    body(0)
    end = count - 1 if last_apart and count > 1 else count
    if end == 2:
        body(1)
    elif end > 2:
        with eng.Fori(1, end) as i:
            body(i)
    if end < count:
        body(end)


def bcast(row, n):
    return row.partition_broadcast(n)


def tile_of(parts, i, tok):
    return (parts[:, i, tok] if isinstance(i, int) else parts[:, bass.ds(i, 1), tok].rearrange(
        "p o t -> p (o t)")).bitcast(F32)


class Scope:

    def __init__(self, nc, ctx, name):
        self.nc, self.ctx, self.name, self.sems = nc, ctx, name, []
        ctx.callback(self.close)

    def close(self):
        for sem in self.sems:
            self.nc.gpsimd.sem_clear(sem)
            self.nc.release_semaphore(sem)

    def sb(self, name, shape, dt=F32):
        return self.ctx.enter_context(self.nc.sbuf_tensor(f"{self.name}_{name}", shape, dt))

    def ps(self, name, shape, dt=F32):
        return self.ctx.enter_context(self.nc.psum_tensor(f"{self.name}_{name}", shape, dt))

    def sem(self, name):
        sem = self.nc.alloc_semaphore(f"{self.name}_{name}")
        if not name.split("_")[-1].startswith("stored"):
            self.sems.append(sem)
        return sem


def fill_constants(pool, consts, filled):
    n = 0
    for name, value in (("ident", 0.0), ("ident_b", 0.0), ("ones", 1.0), ("causal_t", 0.0), ("prev_t", 0.0),
                        ("causal_q", 0.0), ("window_q", 0.0)):
        pool.memset(consts[name][:], value).then_inc(filled, 1)
        n += 1
    pool.wait_ge(filled, n)

    def select(tile, op, fill, step, pattern):
        pool.affine_select(out=tile, in_=tile, compare_op=op, fill=fill, base=0, pattern=pattern,
                           channel_multiplier=step)

    for name in ("ident", "ident_b"):
        select(consts[name][:], ALU.not_equal, 1.0, 1, [[-1, P]])
    select(consts["causal_t"][:], ALU.is_ge, BIG, -1, [[0, GROUP], [1, P]])
    select(consts["prev_t"][:], ALU.is_gt, BIG, 1, [[0, GROUP], [-1, P]])
    select(consts["causal_q"][:], ALU.is_ge, BIG, 1, [[-1, P]])
    select(consts["window_q"][:, 0:P], ALU.is_gt, BIG, -1, [[1, P]])
    select(consts["window_q"][:, P:2 * P], ALU.is_ge, BIG, 1, [[-1, P]])


def gemm_phase(nc, consts, name, xs, w, segments, rope=None, v=None, prep=None, stats=None, key_rope=None,
               constants=False):
    from contextlib import ExitStack
    with ExitStack() as ctx:
        s = Scope(nc, ctx, name)
        pairs = sum(n for _, n, _ in segments)
        kinds = {kind for kind, _, _ in segments}
        kcs = [xs[0][1], xs[-1][1]]
        small = kcs[0] < KD
        hi, lo, pieces = [], [], []
        for x, (src, kc) in enumerate(xs):
            hi.append(s.sb(f"xh{x}", [P, kc, SEQ], F32R))
            lo.append(s.sb(f"xl{x}", [P, kc, SEQ], F32R))
            width = 2 if kc % 2 == 0 else 1
            pieces += [(x, t, k, width) for t in range(NTC) for k in range(0, kc, width)]
        pieces.sort(key=lambda p: (p[1], -p[0], p[2]))
        need = [[max(n for n, p in enumerate(pieces) if p[1] == t and p[0] == x) + 1 for t in range(NTC)]
                for x in range(len(xs))]
        need = [need[0], need[-1]]
        hi, lo = [hi[0], hi[-1]], [lo[0], lo[-1]]
        nx = 2 if (rope or len(xs) == 2) and not small else 3 if prep and not small else 4
        x_raw = [s.sb(f"xraw{b}", [P, 2, TC]) for b in range(nx)]
        both = sum(kcs) * P
        w_raw_t, w_hi_t, w_lo_t = s.sb("wraw", [P, both]), s.sb("whi", [P, both], F32R), s.sb("wlo", [P, both], F32R)
        at_slot = [slice(0, kcs[0] * P), slice(kcs[0] * P, both)]
        w_raw, w_hi, w_lo = ([t[:, at_slot[b]] for b in range(2)] for t in (w_raw_t, w_hi_t, w_lo_t))
        banks = [[s.ps(f"bank{b}{t}", [P, TC]) for t in range(NTC)] for b in range(2)]
        x_in = [s.sem(f"x_in{b}") for b in range(nx)]
        x_hi, x_lo = s.sem("x_hi"), s.sem("x_lo")
        w_in = [s.sem(f"w_in{b}") for b in range(2)]
        w_hi_ok = [s.sem(f"w_hi_ok{b}") for b in range(2)]
        w_lo_ok = [s.sem(f"w_lo_ok{b}") for b in range(2)]
        product = s.sem("product")
        bank_free = [s.sem(f"bank_free{b}") for b in range(2)]
        sets = 2 if small else 1
        if "rope" in kinds:
            cos, sin = s.sb("cos", [P, SEQ]), s.sb("sin", [P, SEQ])
            freq = s.sb("freq", [P, 1])
            pos_in, freq_in, tab_steps, tab_args, tab_done = (
                s.sem(n) for n in ("pos_in", "freq_in", "tab_steps", "tab_args", "tab_done"))
            ta, tb, tc_, td = (s.sb(f"t{n}", [P, TC]) for n in "abcd")
            rope_out = [[s.sb(f"rope{r}{n}", [P, TC], F32R) for n in range(4)] for r in range(sets)]
        if kinds & {"raw", "silu", "resid", "gate"}:
            out_f = s.sb("out_f", [P, TC])
        if kinds & {"silu", "gate"}:
            sig = s.sb("sig", [P, NTC, TC] if "gate" in kinds else [P, 1, TC])
        if "resid" in kinds:
            old = s.sb("old", [P, TC])
        if "gate" in kinds:
            prod, part = s.sb("prod", [P, TC]), s.sb("part", [P, TC])
        if "split" in kinds:
            out_h = [s.sb(f"out_h{b}", [P, SEQ], F32R) for b in range(2)]
            out_l = [s.sb(f"out_l{b}", [P, SEQ], F32R) for b in range(2)]
        if stats:
            square = s.sb("square", [P, TC])
            n_rows = len({row for g in stats["rows"].values() for row, _ in g if row is not None})
            sums = [s.sb(f"sums{r}", [P, SEQ]) for r in range(n_rows)]
            sum_row = s.sb("sum_row", [1, TC])
            squared, added, sums_zero, row_sum, row_out, row_stored = (
                s.sem(n) for n in ("squared", "added", "sums_zero", "row_sum", "row_out", "row_stored"))
            row_items = [(r, t) for r in range(n_rows) for t in range(NTC)]
        if prep:
            cols = prep["cols"]
            n_src = len(prep["sources"])
            fold = [s.sb(f"fold{n}", [P, cols]) for n in range(n_src)]
            work = [s.sb(f"work{n}", [P, cols]) for n in range(1 if prep["kind"] == "divide" else 3)]
            fold_in, fold_steps, fold_root, fold_done, fold_stored = (
                s.sem(n) for n in ("fold_in", "fold_steps", "fold_root", "fold_done", "fold_stored"))
            if prep["kind"] == "divide":
                factor = [s.sb(f"factor{b}", [P, 2, TC]) for b in range(nx)]
                factor_in = [s.sem(f"factor_in{b}") for b in range(nx)]
            else:
                n_fac = 2 if prep["kind"] == "layer" else 1
                chunk_fac = [[s.sb(f"fac{b}{n}", [P, TC]) for n in range(n_fac)]
                             for b in range(1 if "gate" in kinds else 2)]
                if "gate" in kinds:
                    chunk_fac.append([prod, part])
                factor_in = [s.sem(f"factor_in{b}") for b in range(2)]
                gain = s.sb("gain", [P, kcs[0]])
                bias = s.sb("bias", [P, kcs[0]]) if prep["kind"] == "layer" else None
                gain_in, x_centred, x_affine = s.sem("gain_in"), s.sem("x_centred"), s.sem("x_affine")
            x_scaled = s.sem("x_scaled")
            own = [sum(1 for q in pieces[:n] if q[0] == 0) for n in range(len(pieces) + 1)]
        seg_sems = [{n: s.sem(f"seg{g}_{n}") for n in {
            "rope": ("steps", "sum_a", "sum_b", "hi_a", "hi_b", "ready") + ("stored0", "stored1")[:sets],
            "raw": ("ready", "stored"), "silu": ("sig", "ready", "stored"),
            "split": ("hi", "ready", "stored0", "stored1"), "resid": ("old", "ready", "stored"),
            "gate": ("sig", "prod", "part", "ready", "stored")}[kind]}
            for g, (kind, _, _) in enumerate(segments)]
        if v:
            v_src, v_cols, v_dst = v
            kc_v = kcs[0]
            v_parts = -(-v_cols // TC)
            v_n = v_cols // v_parts
            v_heads = v_n // HEAD_DIM
            shared = kc_v * v_cols == both
            wv_raw, wv_hi, wv_lo = (w_raw_t, w_hi_t, w_lo_t) if shared else (
                s.sb("wvraw", [P, kc_v * v_cols]), s.sb("wvhi", [P, kc_v * v_cols], F32R),
                s.sb("wvlo", [P, kc_v * v_cols], F32R))
            v_group = 4 if small else 1
            v_out = [s.sb(f"vout{b}", [P, v_heads, v_group, 2, HEAD_DIM], F32R) for b in range(2)]
            v_in, v_w_hi, v_w_lo, v_prod, v_hi, v_ready = (
                s.sem(n) for n in ("v_in", "v_w_hi", "v_w_lo", "v_prod", "v_hi", "v_ready"))
            v_stored = [s.sem(f"v_stored{b}") for b in range(2)]
            v_items = [(h, b) for h in range(v_parts) for b in range(NB)]
        if key_rope:
            half = ROPE // 2
            kra, krb, kr1, kr2 = (s.sb(f"kr{n}", [half, SEQ]) for n in ("a", "b", "1", "2"))
            kr_out = [[s.sb(f"kr_out{q}", [half, SEQ], F32R) for q in range(2)],
                      [x[:].bitcast(F32R) for x in (kra, kr2)]]
            kr_in, kr_steps, kr_stored = (s.sem(n) for n in ("kr_in", "kr_steps", "kr_stored"))
        if constants:
            filled = s.sem("filled")
        block = ctx.enter_context(nc.Block())
        starts = [sum(n for _, n, _ in segments[:g]) for g in range(len(segments))]

        def stores_of(g):
            kind, n, _ = segments[g]
            sems = seg_sems[g]
            if kind == "rope":
                return [(sems[f"stored{r}"], 64 * NTC * n // sets) for r in range(sets)]
            if kind == "split":
                return [(sems[f"stored{b}"], 32 * n) for b in range(2)]
            return [(sems["stored"], 16 * NTC * n * (1 if kind == "gate" else 2))]

        def each_pair(eng, body):
            for g, (kind, n, _) in enumerate(segments):
                end = g == len(segments) - 1

                def one(li, g=g, n=n, end=end):
                    follows = not (end and isinstance(li, int) and li == n - 1)
                    if g and isinstance(li, int) and li == 0 and eng is not nc.sync:
                        for sem, value in stores_of(g - 1):
                            eng.wait_ge(sem, value)
                    body(g, li, li + starts[g], follows)
                repeat(eng, n, one, last_apart=end)

        two_pi = 2 * np.pi
        c1 = 6.28125
        c2 = float(np.floor((two_pi - c1) * 2 ** 20) / 2 ** 20)
        c3 = float(two_pi - c1 - c2)
        magic = 1.5 * 2 ** 23

        @block.sync
        def _(sp):
            for b in range(2):
                sp.dma_start(w_raw[b], w[b][0]).then_inc(w_in[b], 16)
            if prep:
                for n, src in enumerate(prep["sources"]):
                    sp.dma_start(fold[n][:], src).then_inc(fold_in, 16)
                if prep["kind"] != "divide":
                    sp.dma_start(gain[:], prep["gain"]).then_inc(gain_in, 16)
                    if bias is not None:
                        sp.dma_start(bias[:], prep["bias"]).then_inc(gain_in, 16)
            if "rope" in kinds:
                sp.dma_start(freq[:], rope[1]).then_inc(freq_in, 16)
            if v and not shared:
                sp.dma_start(wv_raw[:], v_src).then_inc(v_in, 16)
            if key_rope:
                sp.dma_start(kra[:], key_rope[0][0:half]).then_inc(kr_in, 16)
                sp.dma_start(krb[:], key_rope[0][half:ROPE]).then_inc(kr_in, 16)

            def store_factors():
                sp.wait_ge(fold_done, 1)
                for n, (dst, src) in enumerate(zip(prep["folded"], prep["order"])):
                    sp.dma_start(dst, work[src][:]).then_inc(fold_stored, 16)
                sp.wait_ge(fold_stored, 16 * len(prep["folded"]))

            def factors(n, x, t, k, width):
                if x != 0:
                    return
                if own[n] == 0:
                    store_factors()
                if prep["kind"] == "divide":
                    rows_ = prep["rows"].rearrange("(k e o) t -> e o k t", e=2, o=1)
                    for e in range(2):
                        sp.dma_start(factor[n % nx][e * HEAD_DIM:(e + 1) * HEAD_DIM, 0:width, :],
                                     bcast(rows_[e, 0, k:k + width, t * TC:(t + 1) * TC], HEAD_DIM)
                                     ).then_inc(factor_in[n % nx], 16)
                elif k == 0:
                    if t >= 2:
                        sp.wait_ge(x_scaled, own[need[0][t - 2]])
                    for q in range(n_fac):
                        sp.dma_start(chunk_fac[t % 2][q][:], bcast(prep["rows"][q, t * TC:(t + 1) * TC], P)
                                     ).then_inc(factor_in[t % 2], 16)

            def load_pieces(n):
                x, t, k, width = pieces[n]
                if n >= nx:
                    sp.wait_ge(x_lo, n - nx + 1)
                src = xs[x][0].rearrange("(k p) t -> p k t", p=P)
                sp.dma_start(x_raw[n % nx][:, 0:width, :],
                             src[:, k:k + width, t * TC:(t + 1) * TC]).then_inc(x_in[n % nx], 16)

            for n in range(len(pieces)):
                load_pieces(n)
                if prep:
                    factors(n, *pieces[n])
            if "rope" in kinds:
                for t in range(NTC):
                    if t:
                        sp.wait_ge(tab_steps, TAB_STEPS * t)
                    else:
                        sp.wait_ge(x_lo, len(pieces))
                    sp.dma_start(x_raw[0][:, 0, :].bitcast(I32), rope[0][t * TC:(t + 1) * TC].partition_broadcast(P)
                                 ).then_inc(pos_in, 16)

            def body(g, li, i, follows):
                kind, _, arg = segments[g]
                sems = seg_sems[g]
                if follows:
                    for b in range(2):
                        sp.wait_ge(w_lo_ok[b], i + 1)
                        sp.dma_start(w_raw[b], w[b][i + 1]).then_inc(w_in[b], 16)
                for b in range(2):
                    for t in range(NTC):
                        n = li * 8 + b * 4 + t
                        m = li * 4 + t
                        tok = slice(t * TC, (t + 1) * TC)
                        if kind == "resid":
                            wait(sp, sems["ready"], n)
                            sp.dma_start(old[:], arg["old"].rearrange("(r p) t -> r p t", p=P)[i * 2 + b, :, tok]
                                         ).then_inc(sems["old"], 16)
                        if kind in ("raw", "silu", "resid"):
                            sp.wait_ge(sems["ready"], n + 1)
                            sp.dma_start(arg["dst"].rearrange("(r p) t -> r p t", p=P)[li * 2 + b, :, tok],
                                         out_f[:]).then_inc(sems["stored"], 16)
                        elif kind == "gate" and b == 1:
                            sp.wait_ge(sems["ready"], m + 1)
                            sp.dma_start(arg["dst"].rearrange("(r p) t -> r p t", p=P)[li, :, tok],
                                         out_f[:]).then_inc(sems["stored"], 16)
                        elif kind == "split" and t == NTC - 1:
                            sp.wait_ge(sems["ready"], n + 1)
                            for q, tile in ((0, out_h[b]), (1, out_l[b])):
                                sp.dma_start(arg["dst"][q][li * 2 + b], tile[:].bitcast(F32)
                                             ).then_inc(sems[f"stored{b}"], 16)
                        elif kind == "rope" and b == 1:
                            sp.wait_ge(sems["ready"], m + 1)
                            for h in range(2):
                                for q in range(2):
                                    sp.dma_start(arg["dst"][q][h, li, :, tok],
                                                 rope_out[t % sets][2 * h + q][:].bitcast(F32)
                                                 ).then_inc(sems[f"stored{t % sets}"], 16)
            each_pair(sp, body)
            if v and shared:
                for b in range(2):
                    sp.wait_ge(w_lo_ok[b], pairs)
                sp.dma_start(wv_raw[:], v_src).then_inc(v_in, 16)
            if v:
                for n in range(v_group - 1, len(v_items), v_group):
                    h, blk = v_items[n]
                    b = (n // v_group) % 2
                    sp.wait_ge(v_ready, n + 1)
                    sp.dma_start(v_dst[h * v_heads:(h + 1) * v_heads, :, blk - v_group + 1:blk + 1].rearrange(
                        "h p g d -> p h (g d)"), v_out[b][:].bitcast(F32).rearrange("p h g two d -> p h (g two d)")
                        ).then_inc(v_stored[b], 16)
            if key_rope:
                sp.wait_ge(kr_steps, 10)
                for n in range(2):
                    for q in range(2):
                        sp.dma_start(key_rope[1][q][n * half:(n + 1) * half], kr_out[n][q][:].bitcast(F32)
                                     ).then_inc(kr_stored, 16)
                sp.wait_ge(kr_stored, 64)
            if stats:
                for n, (r, t) in enumerate(row_items):
                    sp.wait_ge(row_out, n + 1)
                    sp.dma_start(stats["dst"][r:r + 1, t * TC:(t + 1) * TC], sum_row[:]).then_inc(row_stored, 16)
                sp.wait_ge(row_stored, 16 * len(row_items))
            for g in range(len(segments)):
                for sem, value in stores_of(g):
                    sp.wait_ge(sem, value)
            if v:
                for b in range(2):
                    sp.wait_ge(v_stored[b], 16 * (len(v_items) // v_group // 2))

        @block.scalar
        def _(act):
            def split_w(b, i):
                act.wait_ge(w_in[b], (i + 1) * 16)
                wait(act, product, i * 8 - 4 + b * 4)
                act.copy(w_hi[b], w_raw[b]).then_inc(w_hi_ok[b], 1)

            if prep and prep["kind"] != "divide":
                act.wait_ge(fold_root, 1)
                act.activation(work[1][:], work[1][:], ACT.Sqrt).then_inc(fold_steps, 1)
                act.wait_ge(gain_in, 16 if bias is None else 32)
            for n, (x, t, k, width) in enumerate(pieces):
                slot = x if len(xs) == 2 else 0
                if prep and x == 0:
                    act.wait_ge(x_scaled, own[n] + 1)
                    if prep["kind"] != "divide":
                        for j in range(width):
                            op = act.activation(x_raw[n % nx][:, j, :], x_raw[n % nx][:, j, :], ACT.Identity,
                                                bias=0.0 if bias is None else bias[:, k + j:k + j + 1],
                                                scale=gain[:, k + j:k + j + 1])
                        op.then_inc(x_affine, 1)
                        act.wait_ge(x_affine, own[n] + 1)
                else:
                    act.wait_ge(x_in[n % nx], 16 * (n // nx + 1))
                act.copy(hi[slot][:, k:k + width, t * TC:(t + 1) * TC],
                         x_raw[n % nx][:, 0:width, :]).then_inc(x_hi, 1)
                if n == 1:
                    split_w(0, 0)
                    split_w(1, 0)

            def split_v():
                act.wait_ge(v_in, 16)
                if shared:
                    act.wait_ge(product, 8 * pairs)
                act.copy(wv_hi[:], wv_raw[:]).then_inc(v_w_hi, 1)

            if v and not shared:
                split_v()
            if "rope" in kinds:
                for t in range(NTC):
                    tok = slice(t * TC, (t + 1) * TC)
                    act.wait_ge(tab_args, t + 1)
                    act.activation(sin[:, tok], td[:], ACT.Sin)
                    act.activation(cos[:, tok], ta[:], ACT.Sin).then_inc(tab_done, 1)

            def body(g, li, i, follows):
                kind, _, arg = segments[g]
                sems = seg_sems[g]
                for b in range(2):
                    for t in range(NTC):
                        n = li * 8 + b * 4 + t
                        m = li * 4 + t
                        if kind in ("raw", "silu", "split") or (kind == "gate" and b == 0):
                            act.wait_ge(product, i * 8 + b * 4 + t + 1)
                        if kind == "raw":
                            wait(act, sems["stored"], n * 16)
                            if stats and g in stats["rows"]:
                                wait(act, added, n)
                            act.copy(out_f[:], banks[b][t][:]).then_inc(sems["ready"], 1)
                            act.wait_ge(sems["ready"], n + 1)
                            act.sem_inc(bank_free[b], 1)
                            if stats and g in stats["rows"]:
                                act.activation(square[:], out_f[:], ACT.Square).then_inc(squared, 1)
                        elif kind == "resid":
                            act.wait_ge(sems["ready"], n + 1)
                            wait(act, added, n * 2)
                            act.activation(square[:], out_f[:], ACT.Square).then_inc(squared, 1)
                        elif kind == "silu":
                            wait(act, sems["ready"], n)
                            act.activation(sig[:, 0, :], banks[b][t][:], ACT.Sigmoid).then_inc(sems["sig"], 1)
                        elif kind == "split":
                            if t == 0:
                                wait(act, sems[f"stored{b}"], li * 32)
                            act.copy(out_h[b][:, t * TC:(t + 1) * TC], banks[b][t][:]).then_inc(sems["hi"], 1)
                        elif kind == "gate" and b == 0:
                            wait(act, sems["prod"], 0 if isinstance(li, int) and li == 0 else m - 3)
                            act.activation(sig[:, t, :], banks[0][t][:], ACT.Sigmoid).then_inc(sems["sig"], 1)
                        elif kind == "rope" and b == 1:
                            wait(act, sems[f"stored{t % sets}"], (li * (NTC // sets) + t // sets) * 64)
                            act.wait_ge(sems["sum_a"], m + 1)
                            act.copy(rope_out[t % sets][0][:], ta[:]).then_inc(sems["hi_a"], 1)
                            act.wait_ge(sems["sum_b"], m + 1)
                            act.copy(rope_out[t % sets][2][:], tc_[:]).then_inc(sems["hi_b"], 1)
                    if follows:
                        split_w(b, i + 1)
            each_pair(act, body)
            if v and shared:
                split_v()
            if v:
                for n, (h, blk) in enumerate(v_items):
                    act.wait_ge(v_prod, n + 1)
                    grp = n // v_group
                    if n % v_group == 0 and grp >= 2:
                        act.wait_ge(v_stored[grp % 2], 16 * (grp // 2))
                    act.copy(v_out[grp % 2][:, :, n % v_group, 0, :],
                             banks[(n // 4) % 2][n % 4][:, 0:v_n].rearrange("p (h d) -> p h d", d=HEAD_DIM)
                             ).then_inc(v_hi, 1)
            if stats:
                for n in range(len(row_items)):
                    act.wait_ge(row_sum, n + 1)
                    if n:
                        act.wait_ge(row_stored, 16 * n)
                    act.copy(sum_row[:], banks[0][n % 4][0:1, :]).then_inc(row_out, 1)

        @block.vector
        def _(dve):
            vec = nc.vector

            def split_w(b, i):
                dve.wait_ge(w_hi_ok[b], i + 1)
                vec.tensor_tensor(w_lo[b], w_raw[b], w_hi[b].bitcast(F32),
                                  ALU.subtract).then_inc(w_lo_ok[b], 1)

            def fold_factors():
                count = 0

                def step(op):
                    nonlocal count
                    op.then_inc(fold_steps, 1)
                    count += 1
                    dve.wait_ge(fold_steps, count)

                dve.wait_ge(fold_in, 16 * n_src)
                if prep["kind"] == "divide":
                    if n_src == 2:
                        step(vec.tensor_tensor(fold[0][:], fold[0][:], fold[1][:], ALU.add))
                    vec.reciprocal(work[0][:], fold[0][:]).then_inc(fold_done, 1)
                    return
                width = kcs[0] * P
                if prep["kind"] == "layer":
                    step(vec.tensor_scalar(work[0][:], fold[0][:], 1.0 / width, None, ALU.mult))
                    step(vec.tensor_tensor(work[2][:], work[0][:], work[0][:], ALU.mult))
                    step(vec.scalar_tensor_tensor(work[1][:], fold[1][:], 1.0 / width, work[2][:],
                                                  ALU.mult, ALU.subtract))
                    step(vec.tensor_scalar(work[1][:], work[1][:], 0.0, None, ALU.max))
                else:
                    step(vec.tensor_scalar(work[1][:], fold[0][:], 1.0 / width, None, ALU.mult))
                vec.tensor_scalar(work[1][:], work[1][:], prep["eps"], None, ALU.add).then_inc(fold_root, 1)
                count += 1
                dve.wait_ge(fold_steps, count)
                vec.reciprocal(work[2][:], work[1][:]).then_inc(fold_done, 1)

            if prep:
                fold_factors()
            for n, (x, t, k, width) in enumerate(pieces):
                slot = x if len(xs) == 2 else 0
                raw = x_raw[n % nx][:, 0:width, :]
                if prep and x == 0 and prep["kind"] != "divide":
                    if prep["kind"] == "layer":
                        dve.wait_ge(x_centred, own[n] + 1)
                    else:
                        dve.wait_ge(x_in[n % nx], 16 * (n // nx + 1))
                        dve.wait_ge(factor_in[t % 2], 16 * n_fac * (t // 2 + 1))
                    fac = chunk_fac[t % 2][n_fac - 1]
                    vec.tensor_tensor(raw, raw, fac[:].rearrange("p (o t) -> p o t", o=1).broadcast_to(
                        [P, width, TC]), ALU.mult).then_inc(x_scaled, 1)
                dve.wait_ge(x_hi, n + 1)
                at = (slice(None), slice(k, k + width), slice(t * TC, (t + 1) * TC))
                vec.tensor_tensor(lo[slot][at], raw, hi[slot][at].bitcast(F32), ALU.subtract).then_inc(x_lo, 1)
                if n == 1:
                    split_w(0, 0)
                    split_w(1, 0)

            def split_v():
                dve.wait_ge(v_w_hi, 1)
                vec.tensor_tensor(wv_lo[:], wv_raw[:], wv_hi[:].bitcast(F32),
                                  ALU.subtract).then_inc(v_w_lo, 1)

            if v and not shared:
                split_v()
            if "rope" in kinds:
                pos, ang = x_raw[1][:, 0, :], x_raw[1][:, 1, :]
                count = 0

                def step(op):
                    nonlocal count
                    op.then_inc(tab_steps, 1)
                    count += 1
                    dve.wait_ge(tab_steps, count)

                dve.wait_ge(freq_in, 16)
                dve.wait_ge(x_lo, len(pieces))
                for t in range(NTC):
                    dve.wait_ge(pos_in, 16 * (t + 1))
                    step(vec.tensor_copy(pos, x_raw[0][:, 0, :].bitcast(I32)))
                    step(vec.tensor_scalar(ang, pos, freq[:], None, ALU.mult))
                    step(vec.tensor_scalar(tb[:], ang, float(1 / two_pi), None, ALU.mult))
                    step(vec.tensor_scalar(tb[:], tb[:], magic, None, ALU.add))
                    step(vec.tensor_scalar(tb[:], tb[:], magic, None, ALU.subtract))
                    step(vec.scalar_tensor_tensor(tc_[:], tb[:], -c1, ang, ALU.mult, ALU.add))
                    step(vec.scalar_tensor_tensor(tc_[:], tb[:], -c2, tc_[:], ALU.mult, ALU.add))
                    step(vec.scalar_tensor_tensor(tc_[:], tb[:], -c3, tc_[:], ALU.mult, ALU.add))
                    if t:
                        dve.wait_ge(tab_done, t)
                    step(vec.tensor_scalar(td[:], tc_[:], 3.1415925, -3.1415925, ALU.min, ALU.max))
                    step(vec.scalar_tensor_tensor(tb[:], td[:], -1.0, td[:], ALU.mult, ALU.max))
                    assert count == TAB_STEPS * (t + 1)
                    vec.tensor_scalar(ta[:], tb[:], -1.0, float(np.pi / 2), ALU.mult, ALU.add).then_inc(tab_args, 1)
                dve.wait_ge(tab_done, NTC)

            def body(g, li, i, follows):
                kind, _, arg = segments[g]
                sems = seg_sems[g]
                for b in range(2):
                    for t in range(NTC):
                        n = li * 8 + b * 4 + t
                        m = li * 4 + t
                        tok = slice(t * TC, (t + 1) * TC)
                        if kind == "silu":
                            dve.wait_ge(sems["sig"], n + 1)
                            wait(dve, sems["stored"], n * 16)
                            vec.tensor_tensor(out_f[:], banks[b][t][:], sig[:, 0, :], ALU.mult
                                              ).then_inc(sems["ready"], 1)
                            dve.wait_ge(sems["ready"], n + 1)
                            dve.sem_inc(bank_free[b], 1)
                        elif kind == "split":
                            dve.wait_ge(sems["hi"], n + 1)
                            vec.tensor_tensor(out_l[b][:, tok], banks[b][t][:], out_h[b][:, tok].bitcast(F32),
                                              ALU.subtract).then_inc(sems["ready"], 1)
                            dve.wait_ge(sems["ready"], n + 1)
                            dve.sem_inc(bank_free[b], 1)
                        elif kind == "resid":
                            dve.wait_ge(product, i * 8 + b * 4 + t + 1)
                            dve.wait_ge(sems["old"], (n + 1) * 16)
                            wait(dve, sems["stored"], n * 16)
                            wait(dve, added, n * 2)
                            vec.scalar_tensor_tensor(out_f[:], old[:], float(ALPHA), banks[b][t][:],
                                                     ALU.mult, ALU.add).then_inc(sems["ready"], 1)
                            dve.wait_ge(sems["ready"], n + 1)
                            dve.sem_inc(bank_free[b], 1)
                        elif kind == "gate" and b == 1:
                            dve.wait_ge(sems["sig"], m + 1)
                            dve.wait_ge(product, i * 8 + 4 + t + 1)
                            wait(dve, sems["part"], m)
                            vec.tensor_tensor(prod[:], banks[1][t][:], sig[:, t, :], ALU.mult
                                              ).then_inc(sems["prod"], 1)
                            dve.wait_ge(sems["prod"], m + 1)
                            dve.sem_inc(bank_free[0], 1)
                            dve.sem_inc(bank_free[1], 1)
                            wait(dve, sems["ready"], m)
                            vec.tensor_tensor(part[:], prod[:], tile_of(lo[0], i, tok), ALU.add
                                              ).then_inc(sems["part"], 1)
                        elif kind == "rope" and b == 1:
                            st = sems["steps"]
                            dve.wait_ge(product, i * 8 + 4 + t + 1)
                            wait(dve, sems["ready"], m)
                            a, c = banks[0][t], banks[1][t]
                            vec.tensor_tensor(ta[:], a[:], cos[:, tok], ALU.mult).then_inc(st, 1)
                            vec.tensor_tensor(tb[:], c[:], sin[:, tok], ALU.mult).then_inc(st, 1)
                            vec.tensor_tensor(tc_[:], c[:], cos[:, tok], ALU.mult).then_inc(st, 1)
                            vec.tensor_tensor(td[:], a[:], sin[:, tok], ALU.mult).then_inc(st, 1)
                            dve.wait_ge(st, m * 4 + 4)
                            dve.sem_inc(bank_free[0], 1)
                            dve.sem_inc(bank_free[1], 1)
                            out = rope_out[t % sets]
                            dve.wait_ge(sems["hi_a"], m + 1)
                            vec.tensor_tensor(out[1][:], ta[:], out[0][:].bitcast(F32), ALU.subtract)
                            dve.wait_ge(sems["hi_b"], m + 1)
                            vec.tensor_tensor(out[3][:], tc_[:], out[2][:].bitcast(F32),
                                              ALU.subtract).then_inc(sems["ready"], 1)
                    if follows:
                        split_w(b, i + 1)
            each_pair(dve, body)
            if v and shared:
                split_v()
            if v:
                for n, (h, blk) in enumerate(v_items):
                    dve.wait_ge(v_hi, n + 1)
                    out = v_out[(n // v_group) % 2]
                    vec.tensor_tensor(out[:, :, n % v_group, 1, :],
                                      banks[(n // 4) % 2][n % 4][:, 0:v_n].rearrange(
                                          "p (h d) -> p h d", d=HEAD_DIM),
                                      out[:, :, n % v_group, 0, :].bitcast(F32), ALU.subtract).then_inc(v_ready, 1)

        @block.tensor
        def _(pe):
            def body(i):
                first = isinstance(i, int) and i == 0
                for b in range(2):
                    pe.wait_ge(w_lo_ok[b], i + 1)
                    for t in range(NTC):
                        if first and (b == 0 or len(xs) == 2):
                            pe.wait_ge(x_lo, need[b][t])
                        wait(pe, bank_free[b], 0 if first else i * 4 + (t - 3))
                        tok = slice(t * TC, (t + 1) * TC)
                        for k in range(kcs[b]):
                            at = slice(k * P, (k + 1) * P)
                            nc.tensor.matmul(banks[b][t][:], w_hi[b][:, at], hi[b][:, k, tok],
                                             start=(k == 0), stop=False)
                            nc.tensor.matmul(banks[b][t][:], w_hi[b][:, at], lo[b][:, k, tok],
                                             start=False, stop=False)
                            last = nc.tensor.matmul(banks[b][t][:], w_lo[b][:, at], hi[b][:, k, tok],
                                                    start=False, stop=(k == kcs[b] - 1))
                        last.then_inc(product, 1)
            repeat(pe, pairs, body)
            if v:
                pe.wait_ge(v_w_lo, 1)
                for n, (h, blk) in enumerate(v_items):
                    if n < 8:
                        pe.wait_ge(bank_free[n // 4], 4 * (pairs - 1) + n % 4 + 1)
                    else:
                        pe.wait_ge(v_ready, n - 7)
                    out = banks[(n // 4) % 2][n % 4][:, 0:v_n]
                    tok = slice(blk * P, (blk + 1) * P)
                    for k in range(kc_v):
                        at = slice(k * v_cols + h * v_n, k * v_cols + (h + 1) * v_n)
                        nc.tensor.matmul(out, hi[0][:, k, tok], wv_hi[:, at], start=(k == 0), stop=False)
                        nc.tensor.matmul(out, hi[0][:, k, tok], wv_lo[:, at], start=False, stop=False)
                        last = nc.tensor.matmul(out, lo[0][:, k, tok], wv_hi[:, at],
                                                start=False, stop=(k == kc_v - 1))
                    last.then_inc(v_prod, 1)
            if stats:
                pe.wait_ge(bank_free[0], 4 * pairs)
                pe.wait_ge(added, stats["adds"])
                for n, (r, t) in enumerate(row_items):
                    if n >= 4:
                        pe.wait_ge(row_out, n - 3)
                    nc.tensor.matmul(banks[0][n % 4][0:1, :], consts["ones"][:, 0:1],
                                     sums[r][:, t * TC:(t + 1) * TC], start=True, stop=True).then_inc(row_sum, 1)

        @block.gpsimd
        def _(pool):
            if constants:
                fill_constants(pool, consts, filled)
            if stats:
                for tile in sums:
                    op = pool.memset(tile[:], 0.0)
                op.then_inc(sums_zero, 1)
                pool.wait_ge(sums_zero, 1)
            if prep and prep["kind"] in ("divide", "layer"):
                for n, (x, t, k, width) in enumerate(pieces):
                    if x != 0:
                        continue
                    raw = x_raw[n % nx][:, 0:width, :]
                    pool.wait_ge(x_in[n % nx], 16 * (n // nx + 1))
                    if prep["kind"] == "divide":
                        pool.wait_ge(factor_in[n % nx], 32 * (n // nx + 1))
                        pool.tensor_tensor(raw, raw, factor[n % nx][:, 0:width, :], ALU.mult).then_inc(x_scaled, 1)
                    else:
                        pool.wait_ge(factor_in[t % 2], 16 * n_fac * (t // 2 + 1))
                        pool.tensor_tensor(raw, raw, chunk_fac[t % 2][0][:].rearrange(
                            "p (o t) -> p o t", o=1).broadcast_to([P, width, TC]), ALU.subtract
                            ).then_inc(x_centred, 1)
            if key_rope:
                count = 0

                def step(op):
                    nonlocal count
                    op.then_inc(kr_steps, 1)
                    count += 1
                    pool.wait_ge(kr_steps, count)

                pool.wait_ge(kr_in, 32)
                pool.wait_ge(tab_done, NTC)
                for n, (x, y, op) in enumerate(((kra, krb, ALU.subtract), (krb, kra, ALU.add))):
                    step(pool.tensor_tensor(kr1[:], x[:], cos[0:half, :], ALU.mult))
                    step(pool.tensor_tensor(kr2[:], y[:], sin[0:half, :], ALU.mult))
                    step(pool.tensor_tensor(kr1[:], kr1[:], kr2[:], op))
                    step(pool.tensor_scalar(kr_out[n][0][:], kr1[:], 1.0, None, ALU.mult))
                    step(pool.tensor_tensor(kr_out[n][1][:], kr1[:], kr_out[n][0][:].bitcast(F32), ALU.subtract))

            def body(g, li, i, follows):
                kind, _, arg = segments[g]
                sems = seg_sems[g]
                for b in range(2):
                    for t in range(NTC):
                        n = li * 8 + b * 4 + t
                        m = li * 4 + t
                        tok = slice(t * TC, (t + 1) * TC)
                        if kind == "resid":
                            (row_s, _), (row_q, _) = stats["rows"][g]
                            wait(pool, added, n * 2)
                            pool.wait_ge(sems["ready"], n + 1)
                            pool.tensor_tensor(sums[row_s][:, tok], sums[row_s][:, tok], out_f[:], ALU.add
                                               ).then_inc(added, 1)
                            pool.wait_ge(squared, n + 1)
                            pool.tensor_tensor(sums[row_q][:, tok], sums[row_q][:, tok], square[:], ALU.add
                                               ).then_inc(added, 1)
                        elif kind == "raw":
                            row = stats["rows"][g][li * 2 + b][0]
                            pool.wait_ge(squared, n + 1)
                            if row is None:
                                pool.sem_inc(added, 1)
                            else:
                                pool.tensor_tensor(sums[row][:, tok], sums[row][:, tok], square[:], ALU.add
                                                   ).then_inc(added, 1)
                                pool.wait_ge(added, n + 1)
                        elif kind == "gate" and b == 1:
                            pool.wait_ge(sems["part"], m + 1)
                            wait(pool, sems["stored"], m * 16)
                            pool.tensor_tensor(out_f[:], part[:], tile_of(hi[0], i, tok), ALU.add
                                               ).then_inc(sems["ready"], 1)
                        elif kind == "rope" and b == 1:
                            pool.wait_ge(sems["steps"], m * 4 + 2)
                            pool.tensor_tensor(ta[:], ta[:], tb[:], ALU.subtract).then_inc(sems["sum_a"], 1)
                            pool.wait_ge(sems["steps"], m * 4 + 4)
                            pool.tensor_tensor(tc_[:], tc_[:], td[:], ALU.add).then_inc(sems["sum_b"], 1)
            if stats and "raw" in kinds:
                for li in range(segments[0][1]):
                    body(0, li, li, True)
            elif kinds & {"resid", "gate", "rope"}:
                for g, (kind, n, _) in enumerate(segments):
                    if kind in ("resid", "gate", "rope"):
                        repeat(pool, n, lambda li, g=g: body(g, li, li + starts[g], True))


def attention_phase(nc, consts, name, cfg):
    from contextlib import ExitStack
    with ExitStack() as ctx:
        s = Scope(nc, ctx, name)
        rows, qw, kw, vb = cfg["rows"], cfg["q_cols"], cfg["k_cols"], cfg["v_blocks"]
        scale, its, chunks = cfg["scale"], cfg["iterations"], cfg["chunks"]
        steps, items, sinks = cfg["steps"], cfg["items"], cfg["sinks"]
        blocks = qw // P
        pad = cfg["pad"]
        lag = 2
        kr = rows + 1
        q_hi = [s.sb(f"qh{b}", [kr, qw], F32R) for b in range(2)]
        q_lo = [s.sb(f"ql{b}", [kr, qw], F32R) for b in range(2)]
        k_hi = [s.sb(f"kh{b}", [kr, kw], F32R) for b in range(2)]
        k_lo = [s.sb(f"kl{b}", [kr, kw], F32R) for b in range(2)]
        vals = [s.sb(f"v{b}", [P, vb, P], F32R) for b in range(2)]
        prob = [s.sb(f"p{b}", [P, TC]) for b in range(3)]
        p_hi = [s.sb(f"ph{b}", [P, TC], F32R) for b in range(3)]
        p_lo = [s.sb(f"pl{b}", [P, TC], F32R) for b in range(3)]
        acc = [s.sb(f"acc{b}", [P, TC]) for b in range(2)]
        n_mx = cfg["max_cols"]
        zeros = s.sb("zeros", [P, TC if any(st["first"] and st["last"] for st in steps[0]) else P])
        mx, m_all = s.sb("mx", [P, n_mx]), s.sb("m_all", [P, blocks])
        m_t = s.sb("m_t", [blocks, P], F32R)
        o_low = s.sb("o_low", [HEAD_DIM, TC])
        o_sum = [s.sb(f"o_sum{b}", [HEAD_DIM, TC]) for b in range(2)]
        den_row = [s.sb(f"den_row{b}", [1, TC]) for b in range(2)]
        gate = [s.sb(f"gate{b}", [HEAD_DIM, TC]) for b in range(2)]
        o_out = [s.sb(f"o_out{b}", [HEAD_DIM, TC]) for b in range(2)]
        if sinks is not None:
            sink_q, sink_t = s.sb("sink_q", [P, GROUP]), s.sb("sink_t", [blocks, 1])
            sink_e = s.sb("sink_e", [blocks, P])
            sink_in, sink_e_ok, sink_e_stored = s.sem("sink_in"), s.sem("sink_e_ok"), s.sem("sink_e_stored")
        score = [s.ps(f"score{b}", [P, TC]) for b in range(3)]
        mx_w = cfg["max_width"]
        mx_ps = [s.ps(f"mx{b}", [P, mx_w]) for b in range(2 * TC // mx_w)]
        o_ps = [s.ps(f"o{b}", [P, TC]) for b in range(2)]
        den_ps = s.ps("den", [P, TC])
        ld_a, ld_b, mrow = ([s.sem(f"{n}{b}") for b in range(2)] for n in ("load_a", "load_b", "max_row"))
        gate_in, stored, den_stored = ([s.sem(f"{n}{b}") for b in range(2)]
                                       for n in ("gate_in", "stored", "den_stored"))
        (const_ok, scores, probs, p_hi_ok, p_lo_ok, summed, weighed, mx_prod, mx_done, m_done, m_turned,
         m_t_ok, low_ok, sum_ok, den_ok, row_ok, gated) = (s.sem(n) for n in (
             "const_ok", "scores", "probs", "p_hi_ok", "p_lo_ok", "summed", "weighed", "mx_prod", "mx_done",
             "m_done", "m_turned", "m_t_ok", "low_ok", "sum_ok", "den_ok", "row_ok", "gated"))
        block = ctx.enter_context(nc.Block())

        ns = [len(x) for x in steps]
        ni = [len(x) for x in items]
        def step0(it, b):
            return it * sum(ns) + (ns[0] if b else 0)

        def chunk0(it, b):
            return it * 2 * chunks + b * chunks

        def item0(it, b):
            return it * sum(ni) + (ni[0] if b else 0)

        def unit(it, b):
            return it * 2 + b

        def alone(st):
            return st["first"] and st["last"]

        def operations(st):
            return (0 if st["first"] and not alone(st) else 1) + (1 if st["second"] and st["off"] else 0)

        for unit_steps in steps:
            for k, st in enumerate(unit_steps):
                st["second"] = k > 0 and unit_steps[k - 1]["first"] and not st["first"]
        upto = [[sum(operations(st) for st in unit_steps[:k]) for k in range(len(unit_steps) + 1)]
                for unit_steps in steps]

        def sums(it, b, k):
            return it * (upto[0][-1] + upto[1][-1]) + (upto[0][-1] if b else 0) + upto[b][k + 1]

        def sums_using(it, b, k):
            return sums(it, b, k + 1 if steps[b][k]["first"] and not alone(steps[b][k]) else k)

        last_step = [[max(k for k, st in enumerate(steps[b]) if st["chunk"] == c) for c in range(chunks)]
                     for b in range(2)]
        first_at, last_at = cfg["items_from"], cfg["items_to"]

        def after(b, k):
            n, span = ni[1 - b], last_at[b] - first_at[b] + 1
            if not first_at[b] <= k <= last_at[b]:
                return []
            j = k - first_at[b]
            return list(range(j * n // span, (j + 1) * n // span))

        def next_of(it, b):
            return (it, 1) if b == 0 else (it + 1, 0)

        def is_first(it, b):
            return isinstance(it, int) and it == 0 and b == 0

        @block.sync
        def _(sp):
            def load(it, b):
                u = unit(it, b)
                if not (isinstance(it, int) and it == 0):
                    sp.wait_ge(weighed, step0(it, b) - (ns[1 - b]))
                for dst, src in cfg["load_a"](it, b, q_hi[b], k_hi[b]):
                    sp.dma_start(dst.bitcast(F32), src).then_inc(ld_a[b], 16)
                if sinks is not None:
                    if not is_first(it, b):
                        sp.wait_ge(sink_e_ok, u)
                    sp.dma_start(sink_q[:], sinks[it * GROUP:(it + 1) * GROUP].partition_broadcast(P)
                                 if isinstance(it, int) else
                                 sinks[bass.ds(it * GROUP, GROUP)].partition_broadcast(P)).then_inc(sink_in, 16)
                    own = sinks[bass.ds(it * GROUP, GROUP)].rearrange("(j x) -> j x", x=1)
                    for n in range(blocks // GROUP):
                        sp.dma_start(sink_t[n * GROUP:(n + 1) * GROUP, :], own).then_inc(sink_in, 16)
                for dst, src in cfg["load_b"](it, b, q_lo[b], k_lo[b], vals[b]):
                    sp.dma_start(dst.bitcast(F32), src).then_inc(ld_b[b], 16)

            def load_max(it, b):
                u = unit(it, b)
                sp.wait_ge(m_t_ok, u + 1)
                sp.dma_start(q_hi[b][rows:rows + 1, :].bitcast(F32).rearrange("o (n q) -> o n q", q=P),
                             m_t[:].bitcast(F32)
                             ).then_inc(mrow[b], 16)
                if sinks is not None:
                    sp.wait_ge(sink_e_ok, u + 1)
                    sp.dma_start(cfg["sink_dst"](it, b), sink_e[:]).then_inc(sink_e_stored, 16)

            def load_gate(it, b, c):
                n = chunk0(it, b) + c
                if not (is_first(it, b) and c < 2):
                    sp.wait_ge(gated, n - 1)
                sp.dma_start(cfg["gate"](it, b, c, gate[c % 2]), cfg["gate_src"](it, b, c)
                             ).then_inc(gate_in[c % 2], 16)

            def store(it, b, c):
                sp.wait_ge(gated, chunk0(it, b) + c + 1)
                sp.dma_start(cfg["dst"](it, b, c), cfg["gate"](it, b, c, o_out[c % 2])
                             ).then_inc(stored[c % 2], 16)
                sp.wait_ge(row_ok, chunk0(it, b) + c + 1)
                sp.dma_start(cfg["den_dst"](it, b, c), cfg["row"](den_row[c % 2])
                             ).then_inc(den_stored[c % 2], 16)

            load(0, 0)
            load_max(0, 0)

            def body(it):
                for b in range(2):
                    follows = b == 0 or not (isinstance(it, int) and it == its - 1)
                    nxt = next_of(it, b)
                    if follows:
                        load(*nxt)
                    if b == 1:
                        store(it, 0, chunks - 1)
                    elif not is_first(it, b):
                        store(it - 1, 1, chunks - 1)
                    load_gate(it, b, 0)
                    for c in range(1, chunks):
                        load_gate(it, b, c)
                        store(it, b, c - 1)
                        if follows and c == cfg["max_after_chunk"]:
                            load_max(*nxt)
            repeat(sp, its, body, last_apart=True)
            store(its - 1, 1, chunks - 1)
            for b in range(2):
                sp.wait_ge(stored[b], 16 * its * chunks)
                sp.wait_ge(den_stored[b], 16 * its * chunks)
            if sinks is not None:
                sp.wait_ge(sink_e_stored, 16 * its * 2)

        @block.tensor
        def _(pe):
            def mm(out, lhs, rhs, start, stop):
                return nc.tensor.matmul(out, lhs, rhs, start=start, stop=stop)

            def item(it, b, n):
                x = items[b][n]
                buf = mx_ps[n % len(mx_ps)]
                if n == 0:
                    pe.wait_ge(ld_a[b], 16 * cfg["n_load_a"] * (it + 1))
                prev = item0(it, b) + n - len(mx_ps) + 1
                if n < len(mx_ps):
                    if not is_first(it, b):
                        pe.wait_ge(m_t_ok, unit(it, b))
                else:
                    pe.wait_ge(mx_done, prev)
                for q, k, width, mask, col in x["products"]:
                    lastm = mm(buf[:, col:col + width], q_hi[b][0:rows, q:q + P], k_hi[b][0:rows, k:k + width],
                               True, mask is None)
                    if mask is not None:
                        mt, m0, mw = mask
                        lastm = mm(buf[:, col + m0:col + m0 + mw], consts["ident_b"][:],
                                   consts[mt][:, 2 * P - mw:2 * P] if mt == "window_q" else consts[mt][:],
                                   False, True)
                lastm.then_inc(mx_prod, 1)

            def turn(it, b):
                pe.wait_ge(m_done, unit(it, b) + 1)
                nc.tensor.transpose(mx_ps[0][0:blocks, 0:P], m_all[:], consts["ident"][:]).then_inc(m_turned, 1)

            def weigh(it, b, k):
                st = steps[b][k]
                c, off = st["chunk"], st["off"]
                n = step0(it, b) + k
                pe.wait_ge(p_lo_ok, n + 1)
                if st["first"] and not (is_first(it, b) and c < 2):
                    pe.wait_ge(sum_ok, chunk0(it, b) + c - 1)
                if k == 0:
                    pe.wait_ge(ld_b[b], 16 * cfg["n_load_b"] * (it + 1))
                v = vals[b][:, st["v"], :]
                out = o_ps[c % 2][:, off:TC]
                mm(out, v, p_hi[k % 3][:, off:TC], st["first"], False)
                mm(out, v, p_lo[k % 3][:, off:TC], False, st["last"]).then_inc(weighed, 1)

            def denominator(it, b, c):
                n = chunk0(it, b) + c
                pe.wait_ge(summed, sums(it, b, last_step[b][c]))
                if not (is_first(it, b) and c == 0):
                    pe.wait_ge(row_ok, n)
                mm(den_ps[0:1, :], consts["ones"][:, 0:1], acc[c % 2][:], True, True
                   ).then_inc(den_ok, 1)

            pe.wait_ge(const_ok, 1)
            for n in range(ni[0]):
                item(0, 0, n)
            turn(0, 0)

            def body(it):
                for b in range(2):
                    follows = b == 0 or not (isinstance(it, int) and it == its - 1)
                    nxt = next_of(it, b)
                    pe.wait_ge(ld_b[b], 16 * cfg["n_load_b"] * (it + 1))
                    pe.wait_ge(mrow[b], 16 * (it + 1))
                    for k, st in enumerate(steps[b]):
                        n = step0(it, b) + k
                        if k >= 3:
                            pe.wait_ge(p_hi_ok, n - 2)
                        elif not is_first(it, b):
                            pe.wait_ge(p_hi_ok, step0(it, b))
                        off, kb, q0 = st["off"], st["k"] * P, st["chunk"] * TC
                        out = score[k % 3][:, off:TC]
                        q = slice(q0 + off, q0 + TC)
                        ks = slice(kb, kb + P)
                        low = kr if pad else rows
                        mm(out, k_hi[b][0:kr, ks], q_hi[b][0:kr, q], True, False)
                        mm(out, k_hi[b][0:low, ks], q_lo[b][0:low, q], False, False)
                        if st["mask"]:
                            w = cfg["mask_width"]
                            mm(score[k % 3][:, off:off + w], consts["ident_b"][:], consts[st["mask"]][:].rearrange(
                                "p j q -> p (j q)")[:, 0:w], False, False)
                        mm(out, k_lo[b][0:low, ks], q_hi[b][0:low, q], False, True).then_inc(scores, 1)
                        if follows:
                            for x in after(b, k):
                                item(*nxt, x)
                            if k == last_at[b] + 2:
                                turn(*nxt)
                        if k >= lag:
                            weigh(it, b, k - lag)
                        for c in range(chunks - 1):
                            if k == last_step[b][c] + lag + 1:
                                denominator(it, b, c)
                    for k in range(ns[b] - lag, ns[b]):
                        weigh(it, b, k)
                    for c in range(chunks):
                        if c == chunks - 1 or last_step[b][c] + lag + 1 >= ns[b]:
                            denominator(it, b, c)
            repeat(pe, its, body, last_apart=True)

        @block.scalar
        def _(act):
            def sink_exp(it, b):
                if sinks is None:
                    return
                u = unit(it, b)
                act.wait_ge(m_t_ok, u + 1)
                act.wait_ge(sink_in, 16 * (1 + blocks // GROUP) * (u + 1))
                if not is_first(it, b):
                    act.wait_ge(sink_e_stored, 16 * u)
                act.activation(sink_e[:], m_t[:].bitcast(F32), ACT.Exp, bias=sink_t[:], scale=scale
                               ).then_inc(sink_e_ok, 1)

            def low_half(it, b, c):
                n = chunk0(it, b) + c
                act.wait_ge(weighed, step0(it, b) + last_step[b][c] + 1)
                if not (is_first(it, b) and c == 0):
                    act.wait_ge(sum_ok, n)
                act.copy(o_low[:], o_ps[c % 2][HEAD_DIM:P, :]).then_inc(low_ok, 1)

            def denominators(it, b, c):
                act.wait_ge(den_ok, chunk0(it, b) + c + 1)
                if not (is_first(it, b) and c < 2):
                    act.wait_ge(den_stored[c % 2], 16 * (it * chunks + (chunks // 2 if b else 0) + c // 2))
                act.copy(den_row[c % 2][:], den_ps[0:1, :]).then_inc(row_ok, 1)

            sink_exp(0, 0)

            def body(it):
                for b in range(2):
                    follows = b == 0 or not (isinstance(it, int) and it == its - 1)
                    for k, st in enumerate(steps[b]):
                        n = step0(it, b) + k
                        off = st["off"]
                        act.wait_ge(scores, n + 1)
                        if k >= 3:
                            act.wait_ge(p_lo_ok, n - 2)
                            act.wait_ge(summed, sums_using(it, b, k - 3))
                        elif not is_first(it, b):
                            act.wait_ge(p_lo_ok, step0(it, b))
                            act.wait_ge(summed, sums(it, b, -1))
                        act.activation(prob[k % 3][:, off:TC], score[k % 3][:, off:TC], ACT.Exp, scale=scale
                                       ).then_inc(probs, 1)
                        if k >= 3:
                            act.wait_ge(weighed, n - 2)
                        elif not is_first(it, b):
                            act.wait_ge(weighed, step0(it, b))
                        act.activation(p_hi[k % 3][:, off:TC], score[k % 3][:, off:TC], ACT.Exp, scale=scale
                                       ).then_inc(p_hi_ok, 1)
                        if follows and k == last_at[b] + 3:
                            sink_exp(*next_of(it, b))
                        for c in range(chunks):
                            if k == last_step[b][c] + lag + 1:
                                low_half(it, b, c)
                            if k == last_step[b][c] + lag + 2:
                                denominators(it, b, c)
                    for c in range(chunks):
                        if last_step[b][c] + lag + 1 >= ns[b]:
                            low_half(it, b, c)
                        if last_step[b][c] + lag + 2 >= ns[b]:
                            denominators(it, b, c)
            repeat(act, its, body, last_apart=True)

        @block.vector
        def _(dve):
            vec = nc.vector
            for b in range(2):
                vec.memset(k_hi[b][rows:kr, :].bitcast(F32), 1.0)
                if pad:
                    vec.memset(k_lo[b][rows:kr, :].bitcast(F32), 0.0)
                    vec.memset(q_lo[b][rows:kr, :].bitcast(F32), 0.0)
            vec.memset(zeros[:], 0.0)
            vec.memset(mx[:], -3e38).then_inc(const_ok, 1)

            def item(it, b, n):
                x = items[b][n]
                dve.wait_ge(mx_prod, item0(it, b) + n + 1)
                if n == 0 and not is_first(it, b):
                    dve.wait_ge(m_done, unit(it, b))
                buf = mx_ps[n % len(mx_ps)]
                src = buf[:].rearrange("p (j k) -> p j k", k=x["stride"])[:, 0:x["groups"], 0:x["width"]]
                vec.tensor_reduce(mx[:, x["col"]:x["col"] + x["groups"]], src, AX.X, ALU.max
                                  ).then_inc(mx_done, 1)

            def gather(it, b):
                u = unit(it, b)
                dve.wait_ge(mx_done, item0(it, b) + ni[b])
                if not is_first(it, b):
                    dve.wait_ge(m_turned, u)
                if sinks is None:
                    for n, (col, per, out) in enumerate(cfg["gather"]):
                        op = vec.tensor_reduce(m_all[:, out:out + 4],
                                               mx[:, col:col + 4 * per].rearrange("p (i k) -> p i k", k=per),
                                               AX.X, ALU.max)
                else:
                    dve.wait_ge(sink_in, 16 * (1 + blocks // GROUP) * (u + 1))
                    op = vec.scalar_tensor_tensor(
                        m_all[:].rearrange("p (n j) -> p n j", j=GROUP),
                        sink_q[:].rearrange("p (x j) -> p x j", x=1).broadcast_to([P, blocks // GROUP, GROUP]),
                        1.0 / scale, mx[:].rearrange("p (n j) -> p n j", j=GROUP), ALU.mult, ALU.max)
                op.then_inc(m_done, 1)

            def negate(it, b):
                u = unit(it, b)
                dve.wait_ge(m_turned, u + 1)
                if not is_first(it, b):
                    dve.wait_ge(mrow[1 - b], 16 * (it + 1 if b else it))
                    if sinks is not None:
                        dve.wait_ge(sink_e_ok, u)
                vec.tensor_scalar(m_t[:], mx_ps[0][0:blocks, 0:P], -1.0, None, ALU.mult).then_inc(m_t_ok, 1)

            def finish(it, b, c):
                n = chunk0(it, b) + c
                dve.wait_ge(low_ok, n + 1)
                if not (is_first(it, b) and c < 2):
                    dve.wait_ge(gated, n - 1)
                vec.tensor_tensor(o_sum[c % 2][:], o_ps[c % 2][0:HEAD_DIM, :], o_low[:], ALU.add
                                  ).then_inc(sum_ok, 1)

            for n in range(ni[0]):
                item(0, 0, n)
            gather(0, 0)
            negate(0, 0)

            def body(it):
                for b in range(2):
                    follows = b == 0 or not (isinstance(it, int) and it == its - 1)
                    nxt = next_of(it, b)
                    for k, st in enumerate(steps[b]):
                        n = step0(it, b) + k
                        off = st["off"]
                        if follows:
                            for x in after(b, k):
                                item(*nxt, x)
                        dve.wait_ge(p_hi_ok, n + 1)
                        vec.tensor_tensor(p_lo[k % 3][:, off:TC], prob[k % 3][:, off:TC],
                                          p_hi[k % 3][:, off:TC].bitcast(F32), ALU.subtract
                                          ).then_inc(p_lo_ok, 1)
                        if follows:
                            if k == last_at[b]:
                                gather(*nxt)
                            if k == last_at[b] + 2:
                                negate(*nxt)
                        for c in range(chunks):
                            if k == last_step[b][c] + lag + 2:
                                finish(it, b, c)
                    for c in range(chunks):
                        if last_step[b][c] + lag + 2 >= ns[b]:
                            finish(it, b, c)
            repeat(dve, its, body, last_apart=True)

        @block.gpsimd
        def _(pool):
            pool.wait_ge(const_ok, 1)

            def out_gate(it, b, c):
                n = chunk0(it, b) + c
                pool.wait_ge(sum_ok, n + 1)
                pool.wait_ge(gate_in[c % 2], 16 * (it * chunks + (chunks // 2 if b else 0) + c // 2 + 1))
                if not (is_first(it, b) and c < 2):
                    pool.wait_ge(stored[c % 2], 16 * (it * chunks + (chunks // 2 if b else 0) + c // 2))
                pool.tensor_tensor(o_out[c % 2][:], o_sum[c % 2][:], gate[c % 2][:], ALU.mult).then_inc(gated, 1)

            def body(it):
                for b in range(2):
                    for k, st in enumerate(steps[b]):
                        n = step0(it, b) + k
                        c, off = st["chunk"], st["off"]
                        pool.wait_ge(probs, n + 1)
                        mine, both = acc[c % 2], slice(off, TC)
                        if (alone(st) or st["second"]) and not (is_first(it, b) and c < 2):
                            pool.wait_ge(den_ok, chunk0(it, b) + c - 1)
                        if alone(st):
                            pool.tensor_tensor(mine[:], prob[k % 3][:], zeros[:], ALU.add).then_inc(summed, 1)
                        elif st["second"]:
                            if off:
                                pool.tensor_tensor(mine[:, 0:off], prob[(k - 1) % 3][:, 0:off], zeros[:, 0:off],
                                                   ALU.add).then_inc(summed, 1)
                            pool.tensor_tensor(mine[:, both], prob[(k - 1) % 3][:, both], prob[k % 3][:, both],
                                               ALU.add).then_inc(summed, 1)
                        elif not st["first"]:
                            pool.wait_ge(summed, sums(it, b, k - 1))
                            pool.tensor_tensor(mine[:, both], mine[:, both], prob[k % 3][:, both], ALU.add
                                               ).then_inc(summed, 1)
                        for cc in range(chunks):
                            if k == last_step[b][cc] + lag + 3:
                                out_gate(it, b, cc)
                    for cc in range(chunks):
                        if last_step[b][cc] + lag + 3 >= ns[b]:
                            out_gate(it, b, cc)
            repeat(pool, its, body, last_apart=True)


def swa_config(q, k, v, gates, out, dens, sinks, sink_exps):
    half_b = NB // 2
    steps, items = [], []
    for b in range(2):
        st, it = [], []
        for c in range(half_b):
            own = c + b
            blks = ([(own - 1, "prev_t")] if own > 0 else []) + [(own, "causal_t")]
            for n, (kb, mask) in enumerate(blks):
                st.append(dict(chunk=c, k=kb, v=kb, off=0, mask=mask, first=n == 0, last=n == len(blks) - 1))
            width = P * len(blks)
            it.append(dict(products=[(c * TC + j * P, blks[0][0] * P, width, ("window_q", 0, width), j * 2 * P)
                                     for j in range(GROUP)],
                           stride=2 * P, groups=GROUP, width=width, col=c * GROUP))
        steps.append(st)
        items.append(it)

    def tok(b):
        return (half_b * b - b) * P, (half_b + b) * P

    def queries(it, b, tile, part):
        src = q[part].rearrange("s g (j r) (n t) -> s g r n j t", j=GROUP, t=P)
        for s in range(2):
            for j in range(GROUP):
                yield (tile[s * 32:(s + 1) * 32, :].rearrange("r (n j t) -> r n j t", j=GROUP, t=P)[:, :, j, :],
                       src[s, it, :, b * half_b:(b + 1) * half_b, j, :])

    def keys(it, b, tile, part):
        t0, n = tok(b)
        src = k[part].rearrange("s o (g r) t -> s (o g) r t", g=KV_HEADS)
        for s in range(2):
            yield tile[s * 32:(s + 1) * 32, 0:n], src[s, it, :, t0:t0 + n]

    def load_a(it, b, q_hi, k_hi):
        yield from queries(it, b, q_hi, 0)
        yield from keys(it, b, k_hi, 0)

    def load_b(it, b, q_lo, k_lo, vals):
        yield from queries(it, b, q_lo, 1)
        yield from keys(it, b, k_lo, 1)
        t0, n = tok(b)
        yield vals[:, 0:n // P, :], v[it, :, t0 // P:(t0 + n) // P]

    def heads(x, it, b, c):
        t0 = (b * half_b + c) * P
        return x.rearrange("(g j d) t -> g d j t", j=GROUP, d=HEAD_DIM)[it, :, :, t0:t0 + P]

    return dict(rows=HEAD_DIM, q_cols=SEQ * GROUP // 2, k_cols=(half_b + 1) * P, v_blocks=half_b + 1,
                scale=SWA_SCALE, iterations=KV_HEADS, chunks=half_b, steps=steps, items=items, sinks=sinks,
                max_cols=half_b * GROUP, max_width=2 * TC, items_from=(3, 3), items_to=(10, 10), pad=True,
                mask_width=TC, load_a=load_a, load_b=load_b, n_load_a=10, n_load_b=11,
                gate=lambda it, b, c, tile: tile[:].rearrange("d (j t) -> d j t", j=GROUP),
                gate_src=lambda it, b, c: heads(gates, it, b, c), dst=lambda it, b, c: heads(out, it, b, c),
                row=lambda tile: tile[:].rearrange("o (j t) -> o j t", j=GROUP),
                den_dst=lambda it, b, c: dens.rearrange("(g o j) t -> g o j t", o=1, j=GROUP)[
                    it, :, :, (b * half_b + c) * P:(b * half_b + c + 1) * P],
                sink_dst=lambda it, b: sink_exps.rearrange("(g j) (n t) -> g n j t", j=GROUP, t=P)[
                    it, b * half_b:(b + 1) * half_b],
                max_after_chunk=half_b - 1)


def mla_config(q_nope, q_rope, k_nope, k_rope, v, gates, out, dens):
    steps, items, gather = [], [], []
    for c in range(NTC):
        for kb in range(4 * c + 4):
            off = max(0, kb - 4 * c) * P
            steps.append(dict(chunk=c, k=kb, v=kb, off=off, mask="causal_t" if kb >= 4 * c else None,
                              first=kb == 0, last=kb == 4 * c + 3))
        gather.append((len(items), c + 1, 4 * c))
        for i in range(4 * c, 4 * c + 4):
            for kc in range(c + 1):
                width = TC if kc < c else (i % 4 + 1) * P
                mask = ("causal_q", width - P, P) if kc == c else None
                items.append(dict(products=[(i * P, kc * TC, width, mask, 0)], stride=TC, groups=1,
                                  width=width, col=len(items)))

    def load(it, b, q_tile, k_tile, part):
        u = it * 2 + b
        half = ROPE // 2
        qr = q_rope[part].rearrange("s l (h r) t -> s (l h) r t", r=half)
        yield q_tile[0:NOPE, :], q_nope[part].rearrange("l (h d) t -> (l h) d t", d=NOPE)[u]
        for s in range(2):
            yield q_tile[NOPE + s * half:NOPE + (s + 1) * half, :], qr[s, u]
        yield k_tile[0:NOPE, :], k_nope[part].rearrange("l (h d) t -> (l h) d t", d=NOPE)[u]
        yield k_tile[NOPE:NOPE + ROPE, :], k_rope[part]

    def load_a(it, b, q_hi, k_hi):
        yield from load(it, b, q_hi, k_hi, 0)

    def load_b(it, b, q_lo, k_lo, vals):
        yield from load(it, b, q_lo, k_lo, 1)
        yield vals[:], v[it * 2 + b]

    def rows_of(x, it, b, c):
        return x.rearrange("(h d) t -> h d t", d=HEAD_DIM)[it * 2 + b, :, c * TC:(c + 1) * TC]

    return dict(rows=NOPE + ROPE, q_cols=SEQ, k_cols=SEQ, v_blocks=NB, scale=MLA_SCALE, iterations=HEADS // 2,
                chunks=NTC, steps=[steps, steps], items=[items, items], sinks=None, max_cols=len(items),
                max_width=TC, items_from=(8, 8), items_to=(34, 34), pad=False, mask_width=P,
                load_a=load_a, load_b=load_b, n_load_a=5, n_load_b=6, gather=gather,
                gate=lambda it, b, c, tile: tile[:],
                gate_src=lambda it, b, c: rows_of(gates, it, b, c), dst=lambda it, b, c: rows_of(out, it, b, c),
                row=lambda tile: tile[:],
                den_dst=lambda it, b, c: dens.rearrange("(h o) t -> h o t", o=1)[
                    it * 2 + b, :, c * TC:(c + 1) * TC],
                max_after_chunk=NTC - 1)


def build(nc, a, out):
    from contextlib import ExitStack
    ctx = ExitStack()
    with ctx:
        def dram(name, shape, dt=F32):
            return nc.dram_tensor(f"scratch_{name}", shape, dt, kind="Internal").ap()

        def parts(name, shape):
            return [dram(f"{name}_hi", shape), dram(f"{name}_lo", shape)]

        consts = {}
        for n, shape, dt in (("ident", [P, P], F32), ("ident_b", [P, P], BF16), ("ones", [P, P], F32),
                             ("causal_t", [P, GROUP, P], BF16), ("prev_t", [P, GROUP, P], BF16),
                             ("causal_q", [P, P], BF16), ("window_q", [P, 2 * P], BF16)):
            consts[n] = ctx.enter_context(nc.sbuf_tensor(f"const_{n}", shape, dt))

        def spread(rows):
            n, t = rows.shape
            cols = n * t // P
            return rows.rearrange("n (q c) -> (n q) c", c=cols)

        def close_layer(layer, x, attn, sources, dst):
            summed, sums = dram(f"sum{layer}", [D_MODEL, SEQ]), dram(f"sums{layer}", [2, SEQ])
            inv = dram(f"inv{layer}", [HEADS, SEQ])
            gemm_phase(nc, consts, f"wo{layer}", [(attn, KD)], [a[f"w_out{layer}_{b}"] for b in range(2)],
                       [("resid", KD // 2, dict(old=x, dst=summed))],
                       prep=dict(kind="divide", cols=HEADS * SEQ // P, sources=[spread(d) for d in sources],
                                 folded=[spread(inv)], order=[0], rows=inv),
                       stats=dict(rows={0: [(0, False), (1, True)]}, adds=2 * KD * NTC, dst=sums))
            factors = dram(f"factors{layer}", [2, SEQ])
            gemm_phase(nc, consts, f"pe{layer}", [(summed, KD), (a[f"p{layer}"], PLE // P)],
                       [a[f"pe_gate{layer}"], a[f"pe_proj{layer}"]], [("gate", KD, dict(dst=dst))],
                       prep=dict(kind="layer", cols=SEQ // P, sources=[spread(sums[n:n + 1]) for n in range(2)],
                                 folded=[spread(factors[n:n + 1]) for n in range(2)], order=[0, 2], rows=factors,
                                 gain=a[f"ln_g{layer}"], bias=a[f"ln_b{layer}"], eps=LN_EPS))

        def rms(name, sums, gain):
            factors = dram(name, [1, SEQ])
            return dict(kind="rms", cols=SEQ // P, sources=[spread(sums)], folded=[spread(factors)], order=[2],
                        rows=factors, gain=gain, eps=RMS_EPS)

        q0, k0 = parts("q0", [2, KV_HEADS, P, SEQ]), parts("k0", [2, 1, P, SEQ])
        v0 = dram("v0", [KV_HEADS, P, NB, P])
        z0, o0, x1 = (dram(n, [D_MODEL, SEQ]) for n in ("z0", "o0", "x1"))
        den0, sink_exps = dram("den0", [HEADS, SEQ]), dram("sink_exps", [HEADS, SEQ])
        gemm_phase(nc, consts, "in0", [(a["x"], KD)], [a["w_in0_0"], a["w_in0_1"]],
                   [("silu", 4, dict(dst=z0)), ("rope", 4, dict(dst=q0)), ("rope", 1, dict(dst=k0))],
                   rope=(a["positions"], a["freq0"]), v=(a["w_v0"], KV_HEADS * HEAD_DIM, v0), constants=True)
        attention_phase(nc, consts, "swa", swa_config(q0, k0, v0, z0, o0, den0, a["sinks"], sink_exps))
        close_layer(0, a["x"], o0, [den0, sink_exps], x1)

        c1, sums1 = dram("c1", [Q_LORA + P + KV_LORA, SEQ]), dram("sums_c1", [2, SEQ])
        z1, o1, den1 = dram("z1", [D_MODEL, SEQ]), dram("o1", [D_MODEL, SEQ]), dram("den1", [HEADS, SEQ])
        nq, nkv = Q_LORA // P, KV_LORA // P
        latent = [(0, True)] * nq + [(None, True)] + [(1, True)] * nkv
        gemm_phase(nc, consts, "in1", [(x1, KD)], [a["w_in1_0"], a["w_in1_1"]],
                   [("raw", len(latent) // 2, dict(dst=c1)), ("silu", 4, dict(dst=z1))],
                   stats=dict(rows={0: latent}, adds=len(latent) * NTC, dst=sums1))
        qn, qr = parts("qn", [HEADS // 2, P, SEQ]), parts("qr", [2, 2, P, SEQ])
        kr = parts("kr", [ROPE, SEQ])
        gemm_phase(nc, consts, "uq", [(c1[0:Q_LORA], nq)], [a["w_uq_0"], a["w_uq_1"]],
                   [("split", 4, dict(dst=qn)), ("rope", 2, dict(dst=qr))], rope=(a["positions"], a["freq1"]),
                   prep=rms("rms_q", sums1[0:1], a["q_norm"]), key_rope=(c1[Q_LORA:Q_LORA + ROPE], kr))
        kn, v1 = parts("kn", [HEADS // 2, P, SEQ]), dram("v1", [HEADS, P, NB, P])
        gemm_phase(nc, consts, "ukv", [(c1[Q_LORA + P:], nkv)], [a["w_uk_0"], a["w_uk_1"]],
                   [("split", 4, dict(dst=kn))], v=(a["w_uv"], HEADS * HEAD_DIM, v1),
                   prep=rms("rms_kv", sums1[1:2], a["kv_norm"]))
        attention_phase(nc, consts, "mla", mla_config(qn, qr, kn, kr, v1, z1, o1, den1))
        close_layer(1, x1, o1, [den1], out)


def column_tiles(w, order=None):
    w = w if order is None else w[:, order]
    k, n = w.shape
    return np.ascontiguousarray(w.reshape(k // P, P, n // P, P).transpose(2, 1, 0, 3)).reshape(n // P, P, k)


def lay_out(x, p, positions, w_out, ln_g, ln_b, pe_gate, pe_proj, l0_w_in, l0_sinks, l1_w_in, l1_q_norm,
            l1_kv_norm, l1_w_uq, l1_w_ukv):
    a = {"x": np.ascontiguousarray(x[0].T), "positions": positions[0], "sinks": l0_sinks}
    exps = [np.arange(h, dtype=np.float32) / np.float32(h) for h in (HEAD_DIM // 2, ROPE // 2)]
    for n, e in enumerate(exps):
        a[f"freq{n}"] = np.tile(np.power(np.float32(THETA), -e), P // len(e)).astype(np.float32)[:, None]

    def slots(name, tiles):
        a[f"{name}_0"], a[f"{name}_1"] = np.ascontiguousarray(tiles[0::2]), np.ascontiguousarray(tiles[1::2])

    def by_tile(g):
        return np.ascontiguousarray(g.reshape(-1, P).T)

    for layer in range(DEPTH):
        slots(f"w_out{layer}", column_tiles(w_out[layer]))
        a[f"ln_g{layer}"], a[f"ln_b{layer}"] = by_tile(ln_g[layer]), by_tile(ln_b[layer])
        a[f"pe_gate{layer}"] = column_tiles(pe_gate[layer])
        a[f"pe_proj{layer}"] = column_tiles(pe_proj[layer])
        a[f"p{layer}"] = np.ascontiguousarray(p[layer, 0].T)

    def rotary(first, heads, dim, stride=None):
        stride, half = stride or dim, dim // 2
        per = P // half
        return np.concatenate([first + (g + np.arange(per))[:, None] * stride + s * half + np.arange(half)
                               for g in range(0, heads, per) for s in range(2)]).ravel()

    kv = KV_HEADS * HEAD_DIM
    q_end, k_end, v_end = D_MODEL, D_MODEL + kv, D_MODEL + 2 * kv
    slots("w_in0", column_tiles(l0_w_in, np.concatenate([
        np.arange(v_end, l0_w_in.shape[1]), rotary(0, HEADS, HEAD_DIM), rotary(q_end, KV_HEADS, HEAD_DIM)])))

    def token_weights(w):
        k, n = w.shape
        return np.ascontiguousarray(w.reshape(k // P, P, n).transpose(1, 0, 2)).reshape(P, -1)

    a["w_v0"] = token_weights(l0_w_in[:, k_end:v_end])
    pad = np.zeros((D_MODEL, P - ROPE), l1_w_in.dtype)
    c = [Q_LORA, Q_LORA + KV_LORA, Q_LORA + KV_LORA + ROPE]
    slots("w_in1", column_tiles(np.concatenate(
        [l1_w_in[:, :c[0]], l1_w_in[:, c[1]:c[2]], pad, l1_w_in[:, c[0]:c[1]], l1_w_in[:, c[2]:]], 1)))
    a["q_norm"], a["kv_norm"] = by_tile(l1_q_norm), by_tile(l1_kv_norm)
    heads = np.arange(HEADS)[:, None]
    slots("w_uq", column_tiles(l1_w_uq, np.concatenate([
        (heads * (NOPE + ROPE) + np.arange(NOPE)).ravel(), rotary(NOPE, HEADS, ROPE, NOPE + ROPE)])))
    slots("w_uk", column_tiles(l1_w_ukv, (heads * 2 * NOPE + np.arange(NOPE)).ravel()))
    a["w_uv"] = token_weights(l1_w_ukv[:, (heads * 2 * NOPE + NOPE + np.arange(NOPE)).ravel()])
    return a


def kernel(x, p, positions, w_out, ln_g, ln_b, pe_gate, pe_proj, l0_w_in, l0_sinks, l1_w_in, l1_q_norm,
           l1_kv_norm, l1_w_uq, l1_w_ukv, **unused):
    import concourse.bacc as bacc
    from concourse.bass_utils import run_bass_kernel_spmd

    arrays = {f"in_{n}": np.ascontiguousarray(v) for n, v in lay_out(
        *(np.asarray(v) for v in (x, p, positions, w_out, ln_g, ln_b, pe_gate, pe_proj, l0_w_in, l0_sinks,
                                  l1_w_in, l1_q_norm, l1_kv_norm, l1_w_uq, l1_w_ukv))).items()}
    nc = bacc.Bacc("TRN2", target_bir_lowering=False, num_devices=1)
    ins = {n[3:]: nc.dram_tensor(n, v.shape, mybir.dt.from_np(v.dtype), kind="ExternalInput").ap()
           for n, v in arrays.items()}
    out = nc.dram_tensor("out_t", (D_MODEL, SEQ), F32, kind="ExternalOutput").ap()
    build(nc, ins, out)
    r = run_bass_kernel_spmd(nc, [arrays], core_ids=[0])
    return np.ascontiguousarray(r.results[0]["out_t"].T)[None]
```

```python
import numpy as np

import concourse.bass as bass
from concourse import mybir
from concourse.alu_op_type import AluOpType as ALU

ACT = mybir.ActivationFunctionType
AX = mybir.AxisListType
F32 = mybir.dt.float32
F32R = mybir.dt.float32r
BF16 = mybir.dt.bfloat16
I32 = mybir.dt.int32

P = 128
D_MODEL = 1024
SEQ = 2048
DEPTH = 2
HEADS = 16
HEAD_DIM = 64
KV_HEADS = 4
GROUP = HEADS // KV_HEADS
Q_LORA = 384
KV_LORA = 256
ROPE = 32
NOPE = 64
PLE = 256
ALPHA = (2 * DEPTH) ** 0.25
LN_EPS = 1e-5
RMS_EPS = 1e-6
THETA = 10000.0
TC = 512
NTC = SEQ // TC
NB = SEQ // P
KD = D_MODEL // P
BIG = -1e30
TAB_STEPS = 10
SWA_SCALE = HEAD_DIM ** -0.5
MLA_SCALE = (NOPE + ROPE) ** -0.5


def wait(eng, sem, value):
    if isinstance(value, int) and value <= 0:
        return
    eng.wait_ge(sem, value)


def repeat(eng, count, body, last_apart=False):
    body(0)
    end = count - 1 if last_apart and count > 1 else count
    if end == 2:
        body(1)
    elif end > 2:
        with eng.Fori(1, end) as i:
            body(i)
    if end < count:
        body(end)


def bcast(row, n):
    return row.partition_broadcast(n)


def tile_of(parts, i, tok):
    return (parts[:, i, tok] if isinstance(i, int) else parts[:, bass.ds(i, 1), tok].rearrange(
        "p o t -> p (o t)")).bitcast(F32)


class Scope:

    def __init__(self, nc, ctx, name):
        self.nc, self.ctx, self.name, self.sems = nc, ctx, name, []
        ctx.callback(self.close)

    def close(self):
        for sem in self.sems:
            self.nc.gpsimd.sem_clear(sem)
            self.nc.release_semaphore(sem)

    def sb(self, name, shape, dt=F32):
        return self.ctx.enter_context(self.nc.sbuf_tensor(f"{self.name}_{name}", shape, dt))

    def ps(self, name, shape, dt=F32):
        return self.ctx.enter_context(self.nc.psum_tensor(f"{self.name}_{name}", shape, dt))

    def sem(self, name):
        sem = self.nc.alloc_semaphore(f"{self.name}_{name}")
        if not name.split("_")[-1].startswith("stored"):
            self.sems.append(sem)
        return sem


def fill_constants(pool, consts, filled):
    n = 0
    for name, value in (("ident", 0.0), ("ident_b", 0.0), ("ones", 1.0), ("causal_t", 0.0), ("prev_t", 0.0),
                        ("causal_q", 0.0), ("window_q", 0.0)):
        pool.memset(consts[name][:], value).then_inc(filled, 1)
        n += 1
    pool.wait_ge(filled, n)

    def select(tile, op, fill, step, pattern):
        pool.affine_select(out=tile, in_=tile, compare_op=op, fill=fill, base=0, pattern=pattern,
                           channel_multiplier=step)

    for name in ("ident", "ident_b"):
        select(consts[name][:], ALU.not_equal, 1.0, 1, [[-1, P]])
    select(consts["causal_t"][:], ALU.is_ge, BIG, -1, [[0, GROUP], [1, P]])
    select(consts["prev_t"][:], ALU.is_gt, BIG, 1, [[0, GROUP], [-1, P]])
    select(consts["causal_q"][:], ALU.is_ge, BIG, 1, [[-1, P]])
    select(consts["window_q"][:, 0:P], ALU.is_gt, BIG, -1, [[1, P]])
    select(consts["window_q"][:, P:2 * P], ALU.is_ge, BIG, 1, [[-1, P]])


def gemm_phase(nc, consts, name, xs, w, segments, tables=None, v=None, prep=None, stats=None, key_rope=None,
               constants=False):
    from contextlib import ExitStack
    with ExitStack() as ctx:
        s = Scope(nc, ctx, name)
        pairs = sum(n for _, n, _ in segments)
        kinds = {kind for kind, _, _ in segments}
        kcs = [xs[0][1], xs[-1][1]]
        small = kcs[0] < KD
        hi, lo, pieces = [], [], []
        for x, (src, kc, _) in enumerate(xs):
            hi.append(s.sb(f"xh{x}", [P, kc, SEQ], F32R))
            lo.append(s.sb(f"xl{x}", [P, kc, SEQ], F32R))
            width = 2 if kc % 2 == 0 else 1
            pieces += [(x, t, k, width) for t in range(NTC) for k in range(0, kc, width)]
        pieces.sort(key=lambda p: (p[1], -p[0], p[2]))
        need = [[max(n for n, p in enumerate(pieces) if p[1] == t and p[0] == x) + 1 for t in range(NTC)]
                for x in range(len(xs))]
        need = [need[0], need[-1]]
        hi, lo = [hi[0], hi[-1]], [lo[0], lo[-1]]

        def at_piece(tiles, piece):
            x, t, k, width = piece
            return tiles[-x][:, k:k + width, t * TC:(t + 1) * TC]

        def ready_at(slot, t, k):
            return next(n for n, (x, tp, kp, width) in enumerate(pieces)
                        if x == (slot if len(xs) == 2 else 0) and tp == t and kp <= k < kp + width) + 1
        nx = 6
        outer = [n for n, piece in enumerate(pieces) if xs[piece[0]][2]]
        inner = [n for n, piece in enumerate(pieces) if prep and piece[0] == 0]
        rings = [(members, [s.sb(f"ring{r}{b}", [P, 2, TC]) for b in range(size)])
                 for r, (members, size) in enumerate(((outer, 1 if prep else 2), (inner, 2 if small else 3)))
                 if members]

        def ready_of(n):
            x, t, k, width = pieces[n]
            for members, tiles in rings:
                if n in members:
                    return tiles[members.index(n) % len(tiles)][:, 0:width, :]
            return lo[-x][:, k:k + width, t * TC:(t + 1) * TC].bitcast(F32)

        def raw_of(n):
            x, t, k, width = pieces[n]
            return ready_of(n) if xs[x][2] else lo[-x][:, k:k + width, t * TC:(t + 1) * TC].bitcast(F32)

        def ring_free(eng, n):
            for members, tiles in rings:
                if n in members and members.index(n) >= len(tiles):
                    eng.wait_ge(x_lo, members[members.index(n) - len(tiles)] + 1)

        both = sum(kcs) * P
        w_raw_t, w_hi_t, w_lo_t = s.sb("wraw", [P, both]), s.sb("whi", [P, both], F32R), s.sb("wlo", [P, both], F32R)
        at_slot = [slice(0, kcs[0] * P), slice(kcs[0] * P, both)]
        w_raw, w_hi, w_lo = ([t[:, at_slot[b]] for b in range(2)] for t in (w_raw_t, w_hi_t, w_lo_t))
        banks = [[s.ps(f"bank{b}{t}", [P, TC]) for t in range(NTC)] for b in range(2)]
        x_in = [s.sem(f"x_in{b}") for b in range(nx)]
        x_hi, x_lo = s.sem("x_hi"), s.sem("x_lo")
        w_in = [s.sem(f"w_in{b}") for b in range(2)]
        w_hi_ok = [s.sem(f"w_hi_ok{b}") for b in range(2)]
        w_lo_ok = [s.sem(f"w_lo_ok{b}") for b in range(2)]
        product = s.sem("product")
        bank_free = [s.sem(f"bank_free{b}") for b in range(2)]
        sets = 2 if small else 1
        making = tables is not None and "positions" in tables
        if tables:
            cos, sin = s.sb("cos", [P, SEQ]), s.sb("sin", [P, SEQ])
            temps = [[s.sb(f"t{n}{r}", [P, TC]) for n in "abcd"] for r in range(sets if "rope" in kinds else 1)]
            ta, tb, tc_, td = temps[0]
            tab_in = s.sem("tab_in")
        if making:
            freq = s.sb("freq", [P, 1])
            pos_in, freq_in, tab_steps, tab_args, tab_done, tab_stored = (
                s.sem(n) for n in ("pos_in", "freq_in", "tab_steps", "tab_args", "tab_done", "tab_stored"))
        if "rope" in kinds:
            rope_out = [[s.sb(f"rope{r}{n}", [P, TC], F32R) for n in range(4)] for r in range(sets)]
        if kinds & {"raw", "silu", "resid", "gate"}:
            out_f = [s.sb(f"out_f{b}", [P, TC]) for b in range(2)]
        if kinds & {"silu", "gate"}:
            sig = s.sb("sig", [P, NTC, TC] if "gate" in kinds else [P, 1, TC])
        if making:
            pos, ang, pos_raw = out_f[0][:], sig[:, 0, :], out_f[1][:].bitcast(I32)
        if "resid" in kinds:
            old = [s.sb(f"old{b}", [P, TC]) for b in range(2)]
        if "gate" in kinds:
            prod, part = rings[0][1][0][:, 0, :], rings[0][1][0][:, 1, :]
        if "split" in kinds:
            out_h = [s.sb(f"out_h{b}", [P, SEQ], F32R) for b in range(2)]
            out_l = [s.sb(f"out_l{b}", [P, SEQ], F32R) for b in range(2)]
        if stats:
            square = s.sb("square", [P, TC])
            n_rows = len({row for g in stats["rows"].values() for row, _ in g if row is not None})
            sums = [s.sb(f"sums{r}", [P, SEQ]) for r in range(n_rows)]
            squared, added, sums_zero, row_sum, row_out, row_stored = (
                s.sem(n) for n in ("squared", "added", "sums_zero", "row_sum", "row_out", "row_stored"))
            row_items = [(r, t) for t in range(NTC) for r in range(n_rows)]
        if prep:
            cols = prep["cols"]
            n_src = len(prep["sources"])
            fold = [s.sb(f"fold{n}", [P, cols]) for n in range(n_src)]
            work = [s.sb(f"work{n}", [P, cols]) for n in range(1 if prep["kind"] == "divide" else 3)]
            fold_in, fold_steps, fold_root, fold_done, fold_stored = (
                s.sem(n) for n in ("fold_in", "fold_steps", "fold_root", "fold_done", "fold_stored"))
            if prep["kind"] == "divide":
                nf = 2
                factor = [s.sb(f"factor{b}", [P, 2, TC]) for b in range(nf)]
                factor_in = [s.sem(f"factor_in{b}") for b in range(nf)]
            else:
                n_fac = 2 if prep["kind"] == "layer" else 1
                chunk_fac = [[sig[:, 2 * b + n, :] for n in range(n_fac)] for b in range(2)] if "gate" in kinds else [
                    [s.sb(f"fac{b}{n}", [P, TC]) for n in range(n_fac)] for b in range(2)]
                factor_in = [s.sem(f"factor_in{b}") for b in range(2)]
                gain = s.sb("gain", [P, kcs[0]])
                bias = s.sb("bias", [P, kcs[0]]) if prep["kind"] == "layer" else None
                gain_in, x_centred = s.sem("gain_in"), s.sem("x_centred")
            x_scaled = s.sem("x_scaled")
            own = [sum(1 for q in pieces[:n] if q[0] == 0) for n in range(len(pieces) + 1)]
        seg_sems = [{n: s.sem(f"seg{g}_{n}") for n in {
            "rope": ("steps", "sum_a", "sum_b", "hi_a", "hi_b", "ready") + ("stored0", "stored1")[:sets],
            "raw": ("ready", "stored0", "stored1"), "silu": ("sig", "ready", "stored0", "stored1"),
            "split": ("hi", "ready", "stored0", "stored1"), "resid": ("old0", "old1", "ready", "stored0", "stored1"),
            "gate": ("sig", "prod", "part", "ready", "stored0", "stored1")}[kind]}
            for g, (kind, _, _) in enumerate(segments)]
        if v:
            v_src, v_cols, v_dst = v
            kc_v = kcs[0]
            v_parts = -(-v_cols // TC)
            v_n = v_cols // v_parts
            v_heads = v_n // HEAD_DIM
            shared = kc_v * v_cols == both
            wv_raw, wv_hi, wv_lo = (w_raw_t, w_hi_t, w_lo_t) if shared else (
                s.sb("wvraw", [P, kc_v * v_cols]), s.sb("wvhi", [P, kc_v * v_cols], F32R),
                s.sb("wvlo", [P, kc_v * v_cols], F32R))
            def v_half(tile, b):
                return tile[:, b * both // 2:(b + 1) * both // 2]

            v_group = 4 if small else 1
            v_out = [s.sb(f"vout{b}", [P, v_heads, v_group, 2, HEAD_DIM], F32R) for b in range(2)]
            v_in, v_w_hi, v_w_lo, v_prod, v_hi, v_ready = (
                s.sem(n) for n in ("v_in", "v_w_hi", "v_w_lo", "v_prod", "v_hi", "v_ready"))
            v_stored = [s.sem(f"v_stored{b}") for b in range(2)]
            v_items = [(h, b) for h in range(v_parts) for b in range(NB)]
        if key_rope:
            half, kr_cols = ROPE // 2, ROPE // 2 * SEQ // P

            def kr_spread(rows):
                return rows.rearrange("r (q c) -> (r q) c", c=kr_cols)

            kra, krb, kr1, kr2, kr_cos, kr_sin = (s.sb(f"kr{n}", [P, kr_cols]) for n in (
                "a", "b", "1", "2", "cos", "sin"))
            kr_out = [[s.sb(f"kr_out{n}{q}", [P, kr_cols], F32R) for q in range(2)] for n in range(2)]
            kr_in, kr_steps, kr_stored = (s.sem(n) for n in ("kr_in", "kr_steps", "kr_stored"))
        if constants:
            filled = s.sem("filled")
        block = ctx.enter_context(nc.Block())
        starts = [sum(n for _, n, _ in segments[:g]) for g in range(len(segments))]

        def stores_of(g):
            kind, n, _ = segments[g]
            sems = seg_sems[g]
            if kind == "rope":
                return [(sems[f"stored{r}"], 64 * NTC * n // sets) for r in range(sets)]
            if kind == "split":
                return [(sems[f"stored{b}"], 64 * n) for b in range(2)]
            return [(sems[f"stored{b}"], 16 * NTC // 2 * n * (1 if kind == "gate" else 2)) for b in range(2)]

        tables_at = tables["at"] if making else next(
            (g for g, (kind, _, _) in enumerate(segments) if kind == "rope"), None)

        def staging(g):
            return segments[g][0] if segments[g][0] in ("rope", "split") else "whole"

        def each_pair(eng, body, first_tables):
            for g, (kind, n, _) in enumerate(segments):
                end = g == len(segments) - 1

                def one(li, g=g, n=n, end=end):
                    follows = not (end and isinstance(li, int) and li == n - 1)
                    if isinstance(li, int) and li == 0 and eng is not nc.sync:
                        before = [h for h in range(g) if staging(h) == staging(g) or (making and g == tables_at)]
                        for sem, value in stores_of(before[-1]) if before else ():
                            eng.wait_ge(sem, value)
                    if g == tables_at and isinstance(li, int) and li == 0:
                        first_tables()
                    body(g, li, li + starts[g], follows)
                repeat(eng, n, one, last_apart=end)

        def product_of(i, b, t):
            return 2 * t + b if isinstance(i, int) and i == 0 else i * 8 + b * 4 + t

        two_pi = 2 * np.pi
        c1 = 6.28125
        c2 = float(np.floor((two_pi - c1) * 2 ** 20) / 2 ** 20)
        c3 = float(two_pi - c1 - c2)
        magic = 1.5 * 2 ** 23

        @block.sync
        def _(sp):
            def load_first(b):
                sp.dma_start(w_raw[b], w[b][0]).then_inc(w_in[b], 16)

            if prep:
                for n, src in enumerate(prep["sources"]):
                    sp.dma_start(fold[n][:], src).then_inc(fold_in, 16)
                if prep["kind"] != "divide":
                    sp.dma_start(gain[:], prep["gain"]).then_inc(gain_in, 16)
                    if bias is not None:
                        sp.dma_start(bias[:], prep["bias"]).then_inc(gain_in, 16)
            load_first(0)
            if prep:
                load_first(1)
            if making:
                sp.dma_start(freq[:], tables["freq"]).then_inc(freq_in, 16)
            if v and not shared:
                sp.dma_start(wv_raw[:], v_src).then_inc(v_in, 16)
            if key_rope:
                for tile, rows_ in ((kra, key_rope[0][0:half]), (krb, key_rope[0][half:ROPE]),
                                    (kr_cos, tables["src"][0][0:half]), (kr_sin, tables["src"][1][0:half])):
                    sp.dma_start(tile[:], kr_spread(rows_)).then_inc(kr_in, 16)

            def store_factors():
                sp.wait_ge(fold_done, 1)
                for n, (dst, src) in enumerate(zip(prep["folded"], prep["order"])):
                    sp.dma_start(dst, work[src][:]).then_inc(fold_stored, 16)
                sp.wait_ge(fold_stored, 16 * len(prep["folded"]))

            def factors(n, x, t, k, width):
                if x != 0:
                    return
                if own[n] == 0:
                    store_factors()
                if prep["kind"] == "divide":
                    rows_ = prep["rows"].rearrange("(k e o) t -> e o k t", e=2, o=1)
                    if own[n] >= nf:
                        sp.wait_ge(x_scaled, own[n] - nf + 1)
                    for e in range(2):
                        sp.dma_start(factor[own[n] % nf][e * HEAD_DIM:(e + 1) * HEAD_DIM, 0:width, :],
                                     bcast(rows_[e, 0, k:k + width, t * TC:(t + 1) * TC], HEAD_DIM)
                                     ).then_inc(factor_in[own[n] % nf], 16)
                elif k == 0:
                    if t >= 2:
                        sp.wait_ge(x_scaled, own[need[0][t - 2]])
                    for q in range(n_fac):
                        sp.dma_start(chunk_fac[t % 2][q][:], bcast(prep["rows"][q, t * TC:(t + 1) * TC], P)
                                     ).then_inc(factor_in[t % 2], 16)

            def load_pieces(n):
                x, t, k, width = pieces[n]
                if n >= nx:
                    sp.wait_ge(x_in[n % nx], 16 * (n // nx))
                src = xs[x][0].rearrange("(k p) t -> p k t", p=P)
                if xs[x][2]:
                    ring_free(sp, n)
                sp.dma_start(raw_of(n),
                             src[:, k:k + width, t * TC:(t + 1) * TC]).then_inc(x_in[n % nx], 16)

            for n in range(len(pieces)):
                load_pieces(n)
                if prep:
                    factors(n, *pieces[n])
                elif n == 0:
                    load_first(1)
            if tables and not making:
                for tile, src in ((cos, tables["src"][0]), (sin, tables["src"][1])):
                    sp.dma_start(tile[:], src).then_inc(tab_in, 16)

            def table_traffic():
                if not making:
                    return
                for sem, value in stores_of(tables_at - 1):
                    sp.wait_ge(sem, value)
                if stats:
                    sp.wait_ge(squared, 2 * NTC * segments[0][1])
                for t in range(NTC):
                    if t:
                        sp.wait_ge(tab_steps, TAB_STEPS * (t - 1) + 1)
                    sp.dma_start(pos_raw, bcast(tables["positions"][t * TC:(t + 1) * TC], P)
                                 ).then_inc(pos_in, 16)
                if "dst" in tables:
                    sp.wait_ge(tab_done, NTC)
                    for tile, dst in ((cos, tables["dst"][0]), (sin, tables["dst"][1])):
                        sp.dma_start(dst, tile[:]).then_inc(tab_stored, 16)

            def load_old(g, i, place):
                sems, t = seg_sems[g], place % NTC
                pair, b = place // 8, place // NTC % 2
                src = segments[g][2]["old"][pair * 2 * P:].rearrange("(i b p) t -> i b p t", b=2, p=P)
                wait(sp, sems["ready"], i * 8 + place - 1)
                sp.dma_start(old[t % 2][:], src[i, b, :, t * TC:(t + 1) * TC]).then_inc(sems[f"old{t % 2}"], 16)

            def body(g, li, i, follows):
                kind, _, arg = segments[g]
                sems = seg_sems[g]
                if kind == "resid" and isinstance(li, int) and li == 0:
                    load_old(g, 0, 0)
                if follows:
                    for b in range(2):
                        sp.wait_ge(w_lo_ok[b], i + 1)
                        sp.dma_start(w_raw[b], w[b][i + 1]).then_inc(w_in[b], 16)
                elif v and shared:
                    for b in range(2):
                        sp.wait_ge(w_lo_ok[b], pairs)
                        sp.dma_start(v_half(wv_raw, b), v_src[:, b * both // 2:(b + 1) * both // 2]
                                     ).then_inc(v_in, 16)
                for b in range(2):
                    for t in range(NTC):
                        n = li * 8 + b * 4 + t
                        m = li * 4 + t
                        tok = slice(t * TC, (t + 1) * TC)
                        if kind == "resid" and (follows or b * 4 + t < 7):
                            load_old(g, i, b * 4 + t + 1)
                        if kind in ("raw", "silu", "resid"):
                            sp.wait_ge(sems["ready"], n + 1)
                            sp.dma_start(arg["dst"].rearrange("(r p) t -> r p t", p=P)[li * 2 + b, :, tok],
                                         out_f[t % 2][:]).then_inc(sems[f"stored{t % 2}"], 16)
                        elif kind == "gate" and b == 1:
                            sp.wait_ge(sems["ready"], m + 1)
                            sp.dma_start(arg["dst"].rearrange("(r p) t -> r p t", p=P)[li, :, tok],
                                         out_f[t % 2][:]).then_inc(sems[f"stored{t % 2}"], 16)
                        elif kind == "split" and t % 2:
                            sp.wait_ge(sems["ready"], n + 1)
                            two = slice((t - 1) * TC, (t + 1) * TC)
                            for q, tile in ((0, out_h[b]), (1, out_l[b])):
                                sp.dma_start(arg["dst"][q][li * 2 + b, :, two], tile[:, two].bitcast(F32)
                                             ).then_inc(sems[f"stored{b}"], 16)
                        elif kind == "rope" and b == 1:
                            sp.wait_ge(sems["ready"], m + 1)
                            for h in range(2):
                                for q in range(2):
                                    sp.dma_start(arg["dst"][q][h, li, :, tok],
                                                 rope_out[t % sets][2 * h + q][:].bitcast(F32)
                                                 ).then_inc(sems[f"stored{t % sets}"], 16)
            each_pair(sp, body, table_traffic)
            if v:
                for n in range(v_group - 1, len(v_items), v_group):
                    h, blk = v_items[n]
                    b = (n // v_group) % 2
                    sp.wait_ge(v_ready, n + 1)
                    sp.dma_start(v_dst[h * v_heads:(h + 1) * v_heads, :, blk - v_group + 1:blk + 1].rearrange(
                        "h p g d -> p h (g d)"), v_out[b][:].bitcast(F32).rearrange("p h g two d -> p h (g two d)")
                        ).then_inc(v_stored[b], 16)
            if key_rope:
                sp.wait_ge(kr_steps, 10)
                for n in range(2):
                    for q in range(2):
                        sp.dma_start(kr_spread(key_rope[1][q][n * half:(n + 1) * half]),
                                     kr_out[n][q][:].bitcast(F32)).then_inc(kr_stored, 16)
                sp.wait_ge(kr_stored, 64)
            if making and "dst" in tables:
                sp.wait_ge(tab_stored, 32)
            if stats:
                sp.wait_ge(row_out, len(row_items))
                for r in range(n_rows):
                    sp.dma_start(stats["dst"][r:r + 1, :], sums[r][0:1, :]).then_inc(row_stored, 16)
                sp.wait_ge(row_stored, 16 * n_rows)
            for g in range(len(segments)):
                for sem, value in stores_of(g):
                    sp.wait_ge(sem, value)
            if v:
                for b in range(2):
                    sp.wait_ge(v_stored[b], 16 * (len(v_items) // v_group // 2))

        @block.scalar
        def _(act):
            def split_w(b, i):
                act.wait_ge(w_in[b], (i + 1) * 16)
                wait(act, product, product_of(0, b, NTC - 1) + 1 if isinstance(i, int) and i == 1
                     else i * 8 - 4 + b * 4)
                act.copy(w_hi[b], w_raw[b]).then_inc(w_hi_ok[b], 1)

            if prep and prep["kind"] != "divide":
                act.wait_ge(fold_root, 1)
                act.activation(work[1][:], work[1][:], ACT.Sqrt).then_inc(fold_steps, 1)
                act.wait_ge(gain_in, 16 if bias is None else 32)
            split_w(0, 0)
            if prep:
                split_w(1, 0)
            for n, (x, t, k, width) in enumerate(pieces):
                raw, high = ready_of(n), at_piece(hi, pieces[n])
                if prep and x == 0:
                    act.wait_ge(x_scaled, own[n] + 1)
                else:
                    act.wait_ge(x_in[n % nx], 16 * (n // nx + 1))
                if prep and x == 0 and prep["kind"] == "layer":
                    for j in range(width):
                        op = act.activation(high[:, j, :], raw[:, j, :], ACT.Identity, bias=bias[:, k + j:k + j + 1])
                else:
                    op = act.copy(high, raw)
                op.then_inc(x_hi, 1)
                if not prep and n == 0:
                    split_w(1, 0)

            def split_v(b):
                if shared:
                    act.wait_ge(v_in, 32)
                    act.wait_ge(product, 8 * pairs - 4 + 4 * b)
                    act.copy(v_half(wv_hi, b), v_half(wv_raw, b)).then_inc(v_w_hi, 1)
                else:
                    act.wait_ge(v_in, 16)
                    act.copy(wv_hi[:], wv_raw[:]).then_inc(v_w_hi, 1)

            if v and not shared:
                split_v(0)
            def table_sines():
                for t in range(NTC if making else 0):
                    tok = slice(t * TC, (t + 1) * TC)
                    act.wait_ge(tab_args, t + 1)
                    act.activation(sin[:, tok], td[:], ACT.Sin)
                    act.activation(cos[:, tok], ta[:], ACT.Sin).then_inc(tab_done, 1)

            def body(g, li, i, follows):
                kind, _, arg = segments[g]
                sems = seg_sems[g]
                first = isinstance(i, int) and i == 0
                for b in range(2):
                    if first and follows:
                        split_w(b, 1)
                    for t in range(NTC):
                        n = li * 8 + b * 4 + t
                        m = li * 4 + t
                        if kind in ("raw", "silu", "split") or (kind == "gate" and b == 0):
                            act.wait_ge(product, product_of(i, b, t) + 1)
                        if kind == "raw":
                            wait(act, sems[f"stored{t % 2}"], (li * 4 + b * 2 + t // 2) * 16)
                            if stats and g in stats["rows"]:
                                wait(act, added, n)
                            act.copy(out_f[t % 2][:], banks[b][t][:]).then_inc(sems["ready"], 1)
                            act.wait_ge(sems["ready"], n + 1)
                            act.sem_inc(bank_free[b], 1)
                            if stats and g in stats["rows"]:
                                act.activation(square[:], out_f[t % 2][:], ACT.Square).then_inc(squared, 1)
                        elif kind == "resid":
                            act.wait_ge(sems["ready"], n + 1)
                            wait(act, added, n * 2)
                            act.activation(square[:], out_f[t % 2][:], ACT.Square).then_inc(squared, 1)
                        elif kind == "silu":
                            wait(act, sems["ready"], n)
                            act.activation(sig[:, 0, :], banks[b][t][:], ACT.Sigmoid).then_inc(sems["sig"], 1)
                        elif kind == "split":
                            if t == 0:
                                wait(act, sems[f"stored{b}"], li * 64)
                            act.copy(out_h[b][:, t * TC:(t + 1) * TC], banks[b][t][:]).then_inc(sems["hi"], 1)
                        elif kind == "gate" and b == 0:
                            wait(act, sems["prod"], 0 if isinstance(li, int) and li == 0 else m - 3)
                            act.activation(sig[:, t, :], banks[0][t][:], ACT.Sigmoid).then_inc(sems["sig"], 1)
                        elif kind == "rope" and b == 1:
                            wait(act, sems[f"stored{t % sets}"], (li * (NTC // sets) + t // sets) * 64)
                            act.wait_ge(sems["sum_a"], m + 1)
                            act.copy(rope_out[t % sets][0][:], temps[t % sets][0][:]).then_inc(sems["hi_a"], 1)
                            act.wait_ge(sems["sum_b"], m + 1)
                            act.copy(rope_out[t % sets][2][:], temps[t % sets][2][:]).then_inc(sems["hi_b"], 1)
                    if follows:
                        if not first:
                            split_w(b, i + 1)
                    elif v and shared:
                        split_v(b)
            each_pair(act, body, table_sines)
            if v:
                for n, (h, blk) in enumerate(v_items):
                    act.wait_ge(v_prod, n + 1)
                    grp = n // v_group
                    if n % v_group == 0 and grp >= 2:
                        act.wait_ge(v_stored[grp % 2], 16 * (grp // 2))
                    act.copy(v_out[grp % 2][:, :, n % v_group, 0, :],
                             banks[(n // 4) % 2][n % 4][:, 0:v_n].rearrange("p (h d) -> p h d", d=HEAD_DIM)
                             ).then_inc(v_hi, 1)
            if stats:
                for n, (r, t) in enumerate(row_items):
                    act.wait_ge(row_sum, n + 1)
                    act.copy(sums[r][0:1, t * TC:(t + 1) * TC], banks[0][n % 4][0:1, :]).then_inc(row_out, 1)

        @block.vector
        def _(dve):
            vec = nc.vector

            def split_w(b, i):
                dve.wait_ge(w_hi_ok[b], i + 1)
                vec.tensor_tensor(w_lo[b], w_raw[b], w_hi[b].bitcast(F32),
                                  ALU.subtract).then_inc(w_lo_ok[b], 1)

            def fold_factors():
                count = 0

                def step(op):
                    nonlocal count
                    op.then_inc(fold_steps, 1)
                    count += 1
                    dve.wait_ge(fold_steps, count)

                dve.wait_ge(fold_in, 16 * n_src)
                if prep["kind"] == "divide":
                    if n_src == 2:
                        step(vec.tensor_tensor(fold[0][:], fold[0][:], fold[1][:], ALU.add))
                    vec.reciprocal(work[0][:], fold[0][:]).then_inc(fold_done, 1)
                    return
                width = kcs[0] * P
                if prep["kind"] == "layer":
                    step(vec.tensor_scalar(work[0][:], fold[0][:], 1.0 / width, None, ALU.mult))
                    step(vec.tensor_tensor(work[2][:], work[0][:], work[0][:], ALU.mult))
                    step(vec.scalar_tensor_tensor(work[1][:], fold[1][:], 1.0 / width, work[2][:],
                                                  ALU.mult, ALU.subtract))
                    step(vec.tensor_scalar(work[1][:], work[1][:], 0.0, None, ALU.max))
                else:
                    step(vec.tensor_scalar(work[1][:], fold[0][:], 1.0 / width, None, ALU.mult))
                vec.tensor_scalar(work[1][:], work[1][:], prep["eps"], None, ALU.add).then_inc(fold_root, 1)
                count += 1
                dve.wait_ge(fold_steps, count)
                vec.reciprocal(work[2][:], work[1][:]).then_inc(fold_done, 1)

            if prep:
                fold_factors()

            def scale(n, x, t, k, width):
                if not prep or x != 0 or prep["kind"] == "divide":
                    return
                if prep["kind"] == "layer":
                    dve.wait_ge(x_centred, own[n] + 1)
                    raw = ready_of(n)
                else:
                    dve.wait_ge(x_in[n % nx], 16 * (n // nx + 1))
                    dve.wait_ge(factor_in[t % 2], 16 * n_fac * (t // 2 + 1))
                    ring_free(dve, n)
                    raw = raw_of(n)
                for j in range(width):
                    op = vec.scalar_tensor_tensor(ready_of(n)[:, j, :], raw[:, j, :], gain[:, k + j:k + j + 1],
                                                  chunk_fac[t % 2][n_fac - 1][:], ALU.mult, ALU.mult)
                op.then_inc(x_scaled, 1)

            def lower(n, x, t, k, width):
                dve.wait_ge(x_hi, n + 1)
                low, high = at_piece(lo, pieces[n]), at_piece(hi, pieces[n]).bitcast(F32)
                raw = ready_of(n)
                if prep and x == 0 and prep["kind"] == "layer":
                    for j in range(width):
                        op = vec.scalar_tensor_tensor(low[:, j, :], raw[:, j, :], bias[:, k + j:k + j + 1],
                                                      high[:, j, :], ALU.add, ALU.subtract)
                else:
                    op = vec.tensor_tensor(low, raw, high, ALU.subtract)
                op.then_inc(x_lo, 1)

            if prep and prep["kind"] != "divide":
                dve.wait_ge(gain_in, 16 if bias is None else 32)
            split_w(0, 0)
            if prep:
                split_w(1, 0)
            for n in range(len(pieces)):
                scale(n, *pieces[n])
                if n:
                    lower(n - 1, *pieces[n - 1])
                if not prep and n == 1:
                    split_w(1, 0)
            lower(len(pieces) - 1, *pieces[-1])

            def split_v(b):
                dve.wait_ge(v_w_hi, b + 1)
                if shared:
                    vec.tensor_tensor(v_half(wv_lo, b), v_half(wv_raw, b), v_half(wv_hi, b).bitcast(F32),
                                      ALU.subtract).then_inc(v_w_lo, 1)
                else:
                    vec.tensor_tensor(wv_lo[:], wv_raw[:], wv_hi[:].bitcast(F32),
                                      ALU.subtract).then_inc(v_w_lo, 1)

            if v and not shared:
                split_v(0)
            def table_angles():
                if not making:
                    if tables:
                        dve.wait_ge(tab_in, 32)
                    return
                count = 0

                def step(op):
                    nonlocal count
                    op.then_inc(tab_steps, 1)
                    count += 1
                    dve.wait_ge(tab_steps, count)

                dve.wait_ge(freq_in, 16)
                for t in range(NTC):
                    dve.wait_ge(pos_in, 16 * (t + 1))
                    step(vec.tensor_copy(pos, pos_raw))
                    step(vec.tensor_scalar(ang, pos, freq[:], None, ALU.mult))
                    step(vec.tensor_scalar(tb[:], ang, float(1 / two_pi), None, ALU.mult))
                    step(vec.tensor_scalar(tb[:], tb[:], magic, None, ALU.add))
                    step(vec.tensor_scalar(tb[:], tb[:], magic, None, ALU.subtract))
                    step(vec.scalar_tensor_tensor(tc_[:], tb[:], -c1, ang, ALU.mult, ALU.add))
                    step(vec.scalar_tensor_tensor(tc_[:], tb[:], -c2, tc_[:], ALU.mult, ALU.add))
                    step(vec.scalar_tensor_tensor(tc_[:], tb[:], -c3, tc_[:], ALU.mult, ALU.add))
                    if t:
                        dve.wait_ge(tab_done, t)
                    step(vec.tensor_scalar(td[:], tc_[:], 3.1415925, -3.1415925, ALU.min, ALU.max))
                    step(vec.scalar_tensor_tensor(tb[:], td[:], -1.0, td[:], ALU.mult, ALU.max))
                    assert count == TAB_STEPS * (t + 1)
                    vec.tensor_scalar(ta[:], tb[:], -1.0, float(np.pi / 2), ALU.mult, ALU.add).then_inc(tab_args, 1)
                dve.wait_ge(tab_done, NTC)

            def rotate(sems, i, m, t):
                a, c = banks[0][t], banks[1][t]
                tok = slice(t * TC, (t + 1) * TC)
                dve.wait_ge(product, product_of(i, 1, t) + 1)
                wait(dve, sems["ready"], m - (sets - 1))
                for out, x, table in zip(temps[t % sets], (a, c, c, a), (cos, sin, cos, sin)):
                    vec.tensor_tensor(out[:], x[:], table[:, tok], ALU.mult).then_inc(sems["steps"], 1)
                dve.wait_ge(sems["steps"], m * 4 + 4)
                dve.sem_inc(bank_free[0], 1)
                dve.sem_inc(bank_free[1], 1)

            def lower_parts(sems, m, t):
                out, (first, _, second, _) = rope_out[t % sets], temps[t % sets]
                dve.wait_ge(sems["hi_a"], m + 1)
                vec.tensor_tensor(out[1][:], first[:], out[0][:].bitcast(F32), ALU.subtract)
                dve.wait_ge(sems["hi_b"], m + 1)
                vec.tensor_tensor(out[3][:], second[:], out[2][:].bitcast(F32), ALU.subtract
                                  ).then_inc(sems["ready"], 1)

            def body(g, li, i, follows):
                kind, _, arg = segments[g]
                sems = seg_sems[g]
                first = isinstance(i, int) and i == 0
                for b in range(2):
                    if first and follows:
                        split_w(b, 1)
                    for t in range(NTC):
                        n = li * 8 + b * 4 + t
                        m = li * 4 + t
                        tok = slice(t * TC, (t + 1) * TC)
                        if kind == "silu":
                            dve.wait_ge(sems["sig"], n + 1)
                            wait(dve, sems[f"stored{t % 2}"], (li * 4 + b * 2 + t // 2) * 16)
                            vec.tensor_tensor(out_f[t % 2][:], banks[b][t][:], sig[:, 0, :], ALU.mult
                                              ).then_inc(sems["ready"], 1)
                            dve.wait_ge(sems["ready"], n + 1)
                            dve.sem_inc(bank_free[b], 1)
                        elif kind == "split":
                            dve.wait_ge(sems["hi"], n + 1)
                            vec.tensor_tensor(out_l[b][:, tok], banks[b][t][:], out_h[b][:, tok].bitcast(F32),
                                              ALU.subtract).then_inc(sems["ready"], 1)
                            dve.wait_ge(sems["ready"], n + 1)
                            dve.sem_inc(bank_free[b], 1)
                        elif kind == "resid":
                            dve.wait_ge(product, product_of(i, b, t) + 1)
                            dve.wait_ge(sems[f"old{t % 2}"], (li * 4 + b * 2 + t // 2 + 1) * 16)
                            wait(dve, sems[f"stored{t % 2}"], (li * 4 + b * 2 + t // 2) * 16)
                            wait(dve, added, n * 2)
                            vec.scalar_tensor_tensor(out_f[t % 2][:], old[t % 2][:], float(ALPHA), banks[b][t][:],
                                                     ALU.mult, ALU.add).then_inc(sems["ready"], 1)
                            dve.wait_ge(sems["ready"], n + 1)
                            dve.sem_inc(bank_free[b], 1)
                        elif kind == "gate" and b == 1:
                            dve.wait_ge(sems["sig"], m + 1)
                            dve.wait_ge(product, product_of(i, 1, t) + 1)
                            wait(dve, sems["part"], m)
                            vec.tensor_tensor(prod[:], banks[1][t][:], sig[:, t, :], ALU.mult
                                              ).then_inc(sems["prod"], 1)
                            dve.wait_ge(sems["prod"], m + 1)
                            dve.sem_inc(bank_free[0], 1)
                            dve.sem_inc(bank_free[1], 1)
                            wait(dve, sems["ready"], m)
                            vec.tensor_tensor(part[:], prod[:], tile_of(lo[0], i, tok), ALU.add
                                              ).then_inc(sems["part"], 1)
                        elif kind == "rope" and b == 1:
                            rotate(sems, i, m, t)
                            if sets == 1:
                                lower_parts(sems, m, t)
                            else:
                                if t:
                                    lower_parts(sems, m - 1, t - 1)
                                if t == NTC - 1:
                                    lower_parts(sems, m, t)
                    if follows:
                        if not first:
                            split_w(b, i + 1)
                    elif v and shared:
                        split_v(b)
            each_pair(dve, body, table_angles)
            if v:
                for n, (h, blk) in enumerate(v_items):
                    dve.wait_ge(v_hi, n + 1)
                    out = v_out[(n // v_group) % 2]
                    vec.tensor_tensor(out[:, :, n % v_group, 1, :],
                                      banks[(n // 4) % 2][n % 4][:, 0:v_n].rearrange(
                                          "p (h d) -> p h d", d=HEAD_DIM),
                                      out[:, :, n % v_group, 0, :].bitcast(F32), ALU.subtract).then_inc(v_ready, 1)

        @block.tensor
        def _(pe):
            def body(i):
                first = isinstance(i, int) and i == 0
                order = [(b, t) for t in range(NTC) for b in range(2)] if first else [
                    (b, t) for b in range(2) for t in range(NTC)]
                for b, t in order:
                    if t == 0:
                        pe.wait_ge(w_lo_ok[b], i + 1)
                    wait(pe, bank_free[b], 0 if first else i * 4 + (t - 3))
                    tok = slice(t * TC, (t + 1) * TC)
                    for k in range(kcs[b]):
                        if first and (k == 0 or ready_at(b, t, k) != ready_at(b, t, k - 1)):
                            pe.wait_ge(x_lo, ready_at(b, t, k))
                        at = slice(k * P, (k + 1) * P)
                        nc.tensor.matmul(banks[b][t][:], w_hi[b][:, at], hi[b][:, k, tok],
                                         start=(k == 0), stop=False)
                        nc.tensor.matmul(banks[b][t][:], w_hi[b][:, at], lo[b][:, k, tok],
                                         start=False, stop=False)
                        last = nc.tensor.matmul(banks[b][t][:], w_lo[b][:, at], hi[b][:, k, tok],
                                                start=False, stop=(k == kcs[b] - 1))
                    last.then_inc(product, 1)
            repeat(pe, pairs, body)
            if v:
                pe.wait_ge(v_w_lo, 2 if shared else 1)
                for n, (h, blk) in enumerate(v_items):
                    if n < 8:
                        pe.wait_ge(bank_free[n // 4], 4 * (pairs - 1) + n % 4 + 1)
                    else:
                        pe.wait_ge(v_ready, n - 7)
                    out = banks[(n // 4) % 2][n % 4][:, 0:v_n]
                    tok = slice(blk * P, (blk + 1) * P)
                    for k in range(kc_v):
                        at = slice(k * v_cols + h * v_n, k * v_cols + (h + 1) * v_n)
                        nc.tensor.matmul(out, hi[0][:, k, tok], wv_hi[:, at], start=(k == 0), stop=False)
                        nc.tensor.matmul(out, hi[0][:, k, tok], wv_lo[:, at], start=False, stop=False)
                        last = nc.tensor.matmul(out, lo[0][:, k, tok], wv_hi[:, at],
                                                start=False, stop=(k == kc_v - 1))
                    last.then_inc(v_prod, 1)
            if stats:
                pe.wait_ge(bank_free[0], 4 * pairs)
                for n, (r, t) in enumerate(row_items):
                    if stats["last_adds"]:
                        pe.wait_ge(added, stats["adds"] - 2 * (NTC - 1 - t))
                    elif n == 0:
                        pe.wait_ge(added, stats["adds"])
                    if n >= 4:
                        pe.wait_ge(row_out, n - 3)
                    nc.tensor.matmul(banks[0][n % 4][0:1, :], consts["ones"][:, 0:1],
                                     sums[r][:, t * TC:(t + 1) * TC], start=True, stop=True).then_inc(row_sum, 1)

        @block.gpsimd
        def _(pool):
            if constants:
                fill_constants(pool, consts, filled)
            if stats:
                for tile in sums:
                    op = pool.memset(tile[:], 0.0)
                op.then_inc(sums_zero, 1)
                pool.wait_ge(sums_zero, 1)
            if prep and prep["kind"] in ("divide", "layer"):
                for n, (x, t, k, width) in enumerate(pieces):
                    if x != 0:
                        continue
                    raw, scaled = raw_of(n), ready_of(n)
                    pool.wait_ge(x_in[n % nx], 16 * (n // nx + 1))
                    ring_free(pool, n)
                    if prep["kind"] == "divide":
                        m = own[n]
                        pool.wait_ge(factor_in[m % nf], 32 * (m // nf + 1))
                        pool.tensor_tensor(scaled, raw, factor[m % nf][:, 0:width, :], ALU.mult).then_inc(x_scaled, 1)
                    else:
                        pool.wait_ge(factor_in[t % 2], 16 * n_fac * (t // 2 + 1))
                        pool.tensor_tensor(scaled, raw, chunk_fac[t % 2][0][:].rearrange(
                            "p (o t) -> p o t", o=1).broadcast_to([P, width, TC]), ALU.subtract
                            ).then_inc(x_centred, 1)
            if key_rope:
                count = 0

                def step(op):
                    nonlocal count
                    op.then_inc(kr_steps, 1)
                    count += 1
                    pool.wait_ge(kr_steps, count)

                pool.wait_ge(kr_in, 64)
                for n, (x, y, op) in enumerate(((kra, krb, ALU.subtract), (krb, kra, ALU.add))):
                    step(pool.tensor_tensor(kr1[:], x[:], kr_cos[:], ALU.mult))
                    step(pool.tensor_tensor(kr2[:], y[:], kr_sin[:], ALU.mult))
                    step(pool.tensor_tensor(kr1[:], kr1[:], kr2[:], op))
                    step(pool.tensor_scalar(kr_out[n][0][:], kr1[:], 1.0, None, ALU.mult))
                    step(pool.tensor_tensor(kr_out[n][1][:], kr1[:], kr_out[n][0][:].bitcast(F32), ALU.subtract))

            def body(g, li, i, follows):
                kind, _, arg = segments[g]
                sems = seg_sems[g]
                for b in range(2):
                    for t in range(NTC):
                        n = li * 8 + b * 4 + t
                        m = li * 4 + t
                        tok = slice(t * TC, (t + 1) * TC)
                        if kind == "resid":
                            (row_s, _), (row_q, _) = stats["rows"][g]
                            wait(pool, added, n * 2)
                            pool.wait_ge(sems["ready"], n + 1)
                            pool.tensor_tensor(sums[row_s][:, tok], sums[row_s][:, tok], out_f[t % 2][:], ALU.add
                                               ).then_inc(added, 1)
                            pool.wait_ge(squared, n + 1)
                            pool.tensor_tensor(sums[row_q][:, tok], sums[row_q][:, tok], square[:], ALU.add
                                               ).then_inc(added, 1)
                        elif kind == "raw":
                            row = stats["rows"][g][li * 2 + b][0]
                            pool.wait_ge(squared, n + 1)
                            if row is None:
                                pool.sem_inc(added, 1)
                            else:
                                pool.tensor_tensor(sums[row][:, tok], sums[row][:, tok], square[:], ALU.add
                                                   ).then_inc(added, 1)
                                pool.wait_ge(added, n + 1)
                        elif kind == "gate" and b == 1:
                            pool.wait_ge(sems["part"], m + 1)
                            wait(pool, sems[f"stored{t % 2}"], (li * 2 + t // 2) * 16)
                            pool.tensor_tensor(out_f[t % 2][:], part[:], tile_of(hi[0], i, tok), ALU.add
                                               ).then_inc(sems["ready"], 1)
                        elif kind == "rope" and b == 1:
                            x1_cos, x2_sin, x2_cos, x1_sin = temps[t % sets]
                            pool.wait_ge(sems["steps"], m * 4 + 2)
                            pool.tensor_tensor(x1_cos[:], x1_cos[:], x2_sin[:], ALU.subtract
                                               ).then_inc(sems["sum_a"], 1)
                            pool.wait_ge(sems["steps"], m * 4 + 4)
                            pool.tensor_tensor(x2_cos[:], x2_cos[:], x1_sin[:], ALU.add).then_inc(sems["sum_b"], 1)
            if stats and "raw" in kinds:
                for li in range(segments[0][1]):
                    body(0, li, li, True)
            elif kinds & {"resid", "gate", "rope"}:
                for g, (kind, n, _) in enumerate(segments):
                    if kind in ("resid", "gate", "rope"):
                        repeat(pool, n, lambda li, g=g: body(g, li, li + starts[g], True))


def attention_phase(nc, consts, name, cfg):
    from contextlib import ExitStack
    with ExitStack() as ctx:
        s = Scope(nc, ctx, name)
        rows, qw, kw, vb = cfg["rows"], cfg["q_cols"], cfg["k_cols"], cfg["v_blocks"]
        scale, its, chunks = cfg["scale"], cfg["iterations"], cfg["chunks"]
        steps, items, sinks = cfg["steps"], cfg["items"], cfg["sinks"]
        blocks = qw // P
        pad = cfg["pad"]
        lag = 2
        kr = rows + 1
        q_hi = [s.sb(f"qh{b}", [kr, qw], F32R) for b in range(2)]
        q_lo = [s.sb(f"ql{b}", [kr, qw], F32R) for b in range(2)]
        k_hi = [s.sb(f"kh{b}", [kr, kw], F32R) for b in range(2)]
        k_lo = [s.sb(f"kl{b}", [kr, kw], F32R) for b in range(2)]
        vals = [s.sb(f"v{b}", [P, vb, P], F32R) for b in range(2)]
        prob = [s.sb(f"p{b}", [P, TC]) for b in range(4)]
        p_hi = [s.sb(f"ph{b}", [P, TC], F32R) for b in range(4)]
        p_lo = [s.sb(f"pl{b}", [P, TC], F32R) for b in range(4)]
        acc = [s.sb(f"acc{b}", [P, TC]) for b in range(2)]
        n_mx = cfg["max_cols"]
        zeros = s.sb("zeros", [P, TC if any(st["first"] and st["last"] for st in steps[0]) else P])
        mx, m_all = s.sb("mx", [P, n_mx]), s.sb("m_all", [P, blocks])
        m_t = s.sb("m_t", [blocks, P], F32R)
        o_low = s.sb("o_low", [HEAD_DIM, TC])
        o_sum = [s.sb(f"o_sum{b}", [HEAD_DIM, TC]) for b in range(2)]
        den_row = [s.sb(f"den_row{b}", [1, TC]) for b in range(2)]
        gate = [s.sb(f"gate{b}", [HEAD_DIM, TC]) for b in range(2)]
        o_out = [s.sb(f"o_out{b}", [HEAD_DIM, TC]) for b in range(2)]
        if sinks is not None:
            sink_q, sink_t = s.sb("sink_q", [P, GROUP]), s.sb("sink_t", [blocks, 1])
            sink_e = s.sb("sink_e", [blocks, P])
            sink_in, sink_e_ok, sink_e_stored = s.sem("sink_in"), s.sem("sink_e_ok"), s.sem("sink_e_stored")
        score = [s.ps(f"score{b}", [P, TC]) for b in range(3)]
        mx_w = cfg["max_width"]
        mx_ps = [s.ps(f"mx{b}", [P, mx_w]) for b in range(2 * TC // mx_w)]
        o_ps = [s.ps(f"o{b}", [P, TC]) for b in range(2)]
        den_ps = s.ps("den", [P, TC])
        ld_a, ld_b, mrow = ([s.sem(f"{n}{b}") for b in range(2)] for n in ("load_a", "load_b", "max_row"))
        gate_in, stored, den_stored = ([s.sem(f"{n}{b}") for b in range(2)]
                                       for n in ("gate_in", "stored", "den_stored"))
        (const_ok, scores, probs, p_hi_ok, p_lo_ok, summed, weighed, mx_prod, mx_done, m_done, m_turned,
         m_t_ok, low_ok, sum_ok, den_ok, row_ok, gated) = (s.sem(n) for n in (
             "const_ok", "scores", "probs", "p_hi_ok", "p_lo_ok", "summed", "weighed", "mx_prod", "mx_done",
             "m_done", "m_turned", "m_t_ok", "low_ok", "sum_ok", "den_ok", "row_ok", "gated"))
        if pad:
            pad_ok = s.sem("pad_ok")
        block = ctx.enter_context(nc.Block())

        ns = [len(x) for x in steps]
        ni = [len(x) for x in items]
        def step0(it, b):
            return it * sum(ns) + (ns[0] if b else 0)

        def chunk0(it, b):
            return it * 2 * chunks + b * chunks

        def item0(it, b):
            return it * sum(ni) + (ni[0] if b else 0)

        def unit(it, b):
            return it * 2 + b

        def alone(st):
            return st["first"] and st["last"]

        def operations(st):
            return (0 if st["first"] and not alone(st) else 1) + (1 if st["second"] and st["off"] else 0)

        for unit_steps in steps:
            for k, st in enumerate(unit_steps):
                st["second"] = k > 0 and unit_steps[k - 1]["first"] and not st["first"]
        upto = [[sum(operations(st) for st in unit_steps[:k]) for k in range(len(unit_steps) + 1)]
                for unit_steps in steps]

        def sums(it, b, k):
            return it * (upto[0][-1] + upto[1][-1]) + (upto[0][-1] if b else 0) + upto[b][k + 1]

        def sums_using(it, b, k):
            return sums(it, b, k + 1 if steps[b][k]["first"] and not alone(steps[b][k]) else k)

        last_step = [[max(k for k, st in enumerate(steps[b]) if st["chunk"] == c) for c in range(chunks)]
                     for b in range(2)]
        first_at, last_at = cfg["items_from"], cfg["items_to"]

        def after(b, k):
            n, span = ni[1 - b], last_at[b] - first_at[b] + 1
            if not first_at[b] <= k <= last_at[b]:
                return []
            j = k - first_at[b]
            return list(range(j * n // span, (j + 1) * n // span))

        def next_of(it, b):
            return (it, 1) if b == 0 else (it + 1, 0)

        def is_first(it, b):
            return isinstance(it, int) and it == 0 and b == 0

        def prev_of(it, b):
            return (it, 0) if b == 1 else (it - 1, 1)

        def bank_of(b, k):
            return (k + b) % 3

        def buf(b, k):
            return (k + b * ns[0]) % 4

        def earlier(it, b, k, place):
            same = [j for j in range(k) if place(b, j) == place(b, k)]
            if same:
                return it, b, same[-1]
            if is_first(it, b):
                return None
            pi, pb = prev_of(it, b)
            return pi, pb, max(j for j in range(ns[pb]) if place(pb, j) == place(b, k))

        def count(e):
            return step0(e[0], e[1]) + e[2] + 1

        def late_step(it, b, k, delay):
            if k >= delay:
                return [(it, b, k - delay)] if not is_end(it) else []
            if is_first(it, b):
                return []
            pi, pb = prev_of(it, b)
            return [(pi, pb, ns[pb] + k - delay)]

        def late_chunk(it, b, k, delay):
            return [(ui, ub, c) for ui, ub, j in late_step(it, b, k, delay)
                    for c in range(chunks) if last_step[ub][c] == j]

        def is_end(it):
            return isinstance(it, int) and it == its

        tail = lag + 3

        @block.sync
        def _(sp):
            def load_high(it, b):
                if not (isinstance(it, int) and it == 0):
                    sp.wait_ge(scores, step0(it, b) - ns[1 - b])
                for dst, src in cfg["load_a"](it, b, q_hi[b], k_hi[b]):
                    sp.dma_start(dst.bitcast(F32), src).then_inc(ld_a[b], 16)

            def load_low(it, b):
                u = unit(it, b)
                if sinks is not None and b == 0:
                    if not is_first(it, b):
                        sp.wait_ge(sink_e_ok, u)
                    sp.dma_start(sink_q[:], sinks[it * GROUP:(it + 1) * GROUP].partition_broadcast(P)
                                 if isinstance(it, int) else
                                 sinks[bass.ds(it * GROUP, GROUP)].partition_broadcast(P)).then_inc(sink_in, 16)
                    per = blocks // GROUP
                    for j in range(GROUP):
                        sp.dma_start(sink_t[j * per:(j + 1) * per, :], bcast(sinks[bass.ds(it * GROUP + j, 1)], per)
                                     ).then_inc(sink_in, 16)
                for n, (dst, src) in enumerate(cfg["load_b"](it, b, q_lo[b], k_lo[b], vals[b])):
                    if n == cfg["n_load_b"] - 1 and not (isinstance(it, int) and it == 0):
                        sp.wait_ge(weighed, step0(it, b) - ns[1 - b])
                    sp.dma_start(dst.bitcast(F32), src).then_inc(ld_b[b], 16)

            def load_max(it, b):
                u = unit(it, b)
                sp.wait_ge(m_t_ok, u + 1)
                sp.dma_start(cfg["max_row"](q_hi[b][rows:rows + 1, :]).bitcast(F32), m_t[:].bitcast(F32)
                             ).then_inc(mrow[b], 16)
                if sinks is not None:
                    sp.wait_ge(sink_e_ok, u + 1)
                    sp.dma_start(cfg["sink_dst"](it, b), sink_e[:]).then_inc(sink_e_stored, 16)

            def load_gate(it, b, c):
                n = chunk0(it, b) + c
                if not (is_first(it, b) and c < 2):
                    sp.wait_ge(gated, n - 1)
                sp.dma_start(cfg["gate"](it, b, c, gate[c % 2]), cfg["gate_src"](it, b, c)
                             ).then_inc(gate_in[c % 2], 16)

            def store(it, b, c):
                sp.wait_ge(gated, chunk0(it, b) + c + 1)
                sp.dma_start(cfg["dst"](it, b, c), cfg["gate"](it, b, c, o_out[c % 2])
                             ).then_inc(stored[c % 2], 16)
                sp.wait_ge(row_ok, chunk0(it, b) + c + 1)
                sp.dma_start(cfg["den_dst"](it, b, c), cfg["row"](den_row[c % 2])
                             ).then_inc(den_stored[c % 2], 16)

            load_high(0, 0)
            load_low(0, 0)
            load_max(0, 0)

            def body(it):
                for b in range(2):
                    follows = b == 0 or not (isinstance(it, int) and it == its - 1)
                    nxt, prev = next_of(it, b), prev_of(it, b)
                    if follows:
                        load_high(*nxt)
                    if not is_first(it, b):
                        load_gate(*prev, chunks - 1)
                        store(*prev, chunks - 2)
                    if follows:
                        load_low(*nxt)
                    if not is_first(it, b):
                        store(*prev, chunks - 1)
                    load_gate(it, b, 0)
                    for c in range(1, chunks - 1):
                        load_gate(it, b, c)
                        store(it, b, c - 1)
                        if follows and c == cfg["max_after_chunk"]:
                            load_max(*nxt)
            repeat(sp, its, body, last_apart=True)
            load_gate(its - 1, 1, chunks - 1)
            for c in (chunks - 2, chunks - 1):
                store(its - 1, 1, c)
            for b in range(2):
                sp.wait_ge(stored[b], 16 * its * chunks)
                sp.wait_ge(den_stored[b], 16 * its * chunks)
            if sinks is not None:
                sp.wait_ge(sink_e_stored, 16 * its * 2)

        @block.tensor
        def _(pe):
            def mm(out, lhs, rhs, start, stop):
                return nc.tensor.matmul(out, lhs, rhs, start=start, stop=stop)

            def item(it, b, n):
                x = items[b][n]
                bank = mx_ps[n % len(mx_ps)]
                if n == 0:
                    pe.wait_ge(ld_a[b], 16 * cfg["n_load_a"] * (it + 1))
                prev = item0(it, b) + n - len(mx_ps) + 1
                if n < len(mx_ps):
                    if not is_first(it, b):
                        pe.wait_ge(m_t_ok, unit(it, b))
                else:
                    pe.wait_ge(mx_done, prev)
                for q, k, width, mask, col in x["products"]:
                    lastm = mm(bank[:, col:col + width], q_hi[b][0:rows, q:q + P], k_hi[b][0:rows, k:k + width],
                               True, mask is None)
                    if mask is not None:
                        mt, m0, mw = mask
                        lastm = mm(bank[:, col + m0:col + m0 + mw], consts["ident_b"][:],
                                   consts[mt][:, 2 * P - mw:2 * P] if mt == "window_q" else consts[mt][:],
                                   False, True)
                lastm.then_inc(mx_prod, 1)

            def turn(it, b):
                pe.wait_ge(m_done, unit(it, b) + 1)
                nc.tensor.transpose(mx_ps[0][0:blocks, 0:P], m_all[:], consts["ident"][:]).then_inc(m_turned, 1)

            def weigh(it, b, k):
                st = steps[b][k]
                c, off = st["chunk"], st["off"]
                n = step0(it, b) + k
                pe.wait_ge(p_lo_ok, n + 1)
                if st["first"] and not (is_first(it, b) and c < 2):
                    pe.wait_ge(sum_ok, chunk0(it, b) + c - 1)
                if k == 0:
                    pe.wait_ge(ld_b[b], 16 * cfg["n_load_b"] * (it + 1))
                v = vals[b][:, st["v"], :]
                out = o_ps[c % 2][:, off:TC]
                mm(out, v, p_hi[buf(b, k)][:, off:TC], st["first"], False)
                mm(out, v, p_lo[buf(b, k)][:, off:TC], False, st["last"]).then_inc(weighed, 1)

            def denominator(it, b, c):
                n = chunk0(it, b) + c
                pe.wait_ge(summed, sums(it, b, last_step[b][c]))
                if not (is_first(it, b) and c == 0):
                    pe.wait_ge(row_ok, n)
                mm(den_ps[0:1, :], consts["ones"][:, 0:1], acc[c % 2][:], True, True
                   ).then_inc(den_ok, 1)

            def follow_up(it, b, k):
                for e in late_step(it, b, k, lag):
                    weigh(*e)
                for e in late_chunk(it, b, k, lag + 1):
                    denominator(*e)

            for n in range(ni[0]):
                item(0, 0, n)
            turn(0, 0)
            pe.wait_ge(const_ok, 1)
            if pad:
                pe.wait_ge(pad_ok, 1)

            def body(it):
                for b in range(2):
                    follows = b == 0 or not (isinstance(it, int) and it == its - 1)
                    nxt = next_of(it, b)
                    pe.wait_ge(ld_b[b], 16 * cfg["n_load_b"] * (it + 1))
                    pe.wait_ge(mrow[b], 16 * (it + 1))
                    for k, st in enumerate(steps[b]):
                        e = earlier(it, b, k, bank_of)
                        if e:
                            pe.wait_ge(p_hi_ok, count(e))
                        off, kb = st["off"], st["k"] * P
                        bank = score[bank_of(b, k)]
                        out = cfg["split"](bank[:, off:TC])
                        ks = slice(kb, kb + P)
                        low = kr if pad else rows

                        def q(tile, n_rows):
                            return cfg["q_view"](tile[b][0:n_rows, :], st["chunk"], off)

                        mm(out, k_hi[b][0:kr, ks], q(q_hi, kr), True, False)
                        mm(out, k_hi[b][0:low, ks], q(q_lo, low), False, False)
                        if st["mask"]:
                            w = cfg["mask_width"]
                            mm(bank[:, off:off + w], consts["ident_b"][:], consts[st["mask"]][:].rearrange(
                                "p j q -> p (j q)")[:, 0:w], False, False)
                        mm(out, k_lo[b][0:low, ks], q(q_hi, low), False, True).then_inc(scores, 1)
                        if follows:
                            for x in after(b, k):
                                item(*nxt, x)
                            if k == last_at[b] + 1:
                                turn(*nxt)
                        follow_up(it, b, k)
            repeat(pe, its, body, last_apart=True)
            for k in range(tail):
                follow_up(its, 0, k)

        @block.scalar
        def _(act):
            def sink_exp(it, b):
                if sinks is None:
                    return
                u = unit(it, b)
                act.wait_ge(m_t_ok, u + 1)
                act.wait_ge(sink_in, 16 * (1 + GROUP) * (it + 1))
                if not is_first(it, b):
                    act.wait_ge(sink_e_stored, 16 * u)
                act.activation(sink_e[:], m_t[:].bitcast(F32), ACT.Exp, bias=sink_t[:], scale=scale
                               ).then_inc(sink_e_ok, 1)

            def low_half(it, b, c):
                n = chunk0(it, b) + c
                act.wait_ge(weighed, step0(it, b) + last_step[b][c] + 1)
                if not (is_first(it, b) and c == 0):
                    act.wait_ge(sum_ok, n)
                act.copy(o_low[:], o_ps[c % 2][HEAD_DIM:P, :]).then_inc(low_ok, 1)

            def denominators(it, b, c):
                act.wait_ge(den_ok, chunk0(it, b) + c + 1)
                if not (is_first(it, b) and c < 2):
                    act.wait_ge(den_stored[c % 2], 16 * (it * chunks + (chunks // 2 if b else 0) + c // 2))
                act.copy(den_row[c % 2][:], den_ps[0:1, :]).then_inc(row_ok, 1)

            def follow_up(it, b, k):
                for e in late_chunk(it, b, k, lag):
                    low_half(*e)
                for e in late_chunk(it, b, k, lag + 2):
                    denominators(*e)

            sink_exp(0, 0)

            def body(it):
                for b in range(2):
                    follows = b == 0 or not (isinstance(it, int) and it == its - 1)
                    for k, st in enumerate(steps[b]):
                        n = step0(it, b) + k
                        off = st["off"]
                        act.wait_ge(scores, n + 1)
                        e, i = earlier(it, b, k, buf), buf(b, k)
                        bank = score[bank_of(b, k)]
                        if e:
                            act.wait_ge(p_lo_ok, count(e))
                            act.wait_ge(summed, sums_using(*e))
                        act.activation(prob[i][:, off:TC], bank[:, off:TC], ACT.Exp, scale=scale
                                       ).then_inc(probs, 1)
                        if e:
                            act.wait_ge(weighed, count(e))
                        act.activation(p_hi[i][:, off:TC], bank[:, off:TC], ACT.Exp, scale=scale
                                       ).then_inc(p_hi_ok, 1)
                        if follows and k == last_at[b] + 2:
                            sink_exp(*next_of(it, b))
                        follow_up(it, b, k)
            repeat(act, its, body, last_apart=True)
            for k in range(tail):
                follow_up(its, 0, k)

        @block.vector
        def _(dve):
            vec = nc.vector
            for b in range(2):
                vec.memset(k_hi[b][rows:kr, :].bitcast(F32), 1.0)
                if pad:
                    vec.memset(k_lo[b][rows:kr, :].bitcast(F32), 0.0)
            vec.memset(zeros[:], 0.0).then_inc(const_ok, 1)

            def item(it, b, n):
                x = items[b][n]
                dve.wait_ge(mx_prod, item0(it, b) + n + 1)
                if n == 0 and not is_first(it, b):
                    dve.wait_ge(m_done, unit(it, b))
                src = mx_ps[n % len(mx_ps)][:].rearrange("p (j k) -> p j k", k=x["stride"])[:, 0:x["groups"], 0:x["width"]]
                vec.tensor_reduce(mx[:].rearrange("p (j n) -> p j n", j=x["groups"])[:, :, x["col"]], src,
                                  AX.X, ALU.max).then_inc(mx_done, 1)

            def gather(it, b):
                u = unit(it, b)
                dve.wait_ge(mx_done, item0(it, b) + ni[b])
                if not is_first(it, b):
                    dve.wait_ge(m_turned, u)
                if sinks is None:
                    for n, (col, per, out) in enumerate(cfg["gather"]):
                        op = vec.tensor_reduce(m_all[:, out:out + 4],
                                               mx[:, col:col + 4 * per].rearrange("p (i k) -> p i k", k=per),
                                               AX.X, ALU.max)
                else:
                    dve.wait_ge(sink_in, 16 * (1 + GROUP) * (it + 1))
                    op = vec.scalar_tensor_tensor(
                        m_all[:].rearrange("p (j n) -> p j n", j=GROUP),
                        sink_q[:].rearrange("p (j x) -> p j x", x=1).broadcast_to([P, GROUP, blocks // GROUP]),
                        1.0 / scale, mx[:].rearrange("p (j n) -> p j n", j=GROUP), ALU.mult, ALU.max)
                op.then_inc(m_done, 1)

            def negate(it, b):
                u = unit(it, b)
                dve.wait_ge(m_turned, u + 1)
                if not is_first(it, b):
                    dve.wait_ge(mrow[1 - b], 16 * (it + 1 if b else it))
                    if sinks is not None:
                        dve.wait_ge(sink_e_ok, u)
                vec.tensor_scalar(m_t[:], mx_ps[0][0:blocks, 0:P], -1.0, None, ALU.mult).then_inc(m_t_ok, 1)

            def finish(it, b, c):
                n = chunk0(it, b) + c
                dve.wait_ge(low_ok, n + 1)
                if not (is_first(it, b) and c < 2):
                    dve.wait_ge(gated, n - 1)
                vec.tensor_tensor(o_sum[c % 2][:], o_ps[c % 2][0:HEAD_DIM, :], o_low[:], ALU.add
                                  ).then_inc(sum_ok, 1)

            def follow_up(it, b, k):
                for e in late_chunk(it, b, k, lag):
                    finish(*e)

            for n in range(ni[0]):
                item(0, 0, n)
            gather(0, 0)
            negate(0, 0)

            def body(it):
                for b in range(2):
                    follows = b == 0 or not (isinstance(it, int) and it == its - 1)
                    nxt = next_of(it, b)
                    for k, st in enumerate(steps[b]):
                        n = step0(it, b) + k
                        off = st["off"]
                        if follows:
                            for x in after(b, k):
                                item(*nxt, x)
                        dve.wait_ge(p_hi_ok, n + 1)
                        i = buf(b, k)
                        vec.tensor_tensor(p_lo[i][:, off:TC], prob[i][:, off:TC],
                                          p_hi[i][:, off:TC].bitcast(F32), ALU.subtract
                                          ).then_inc(p_lo_ok, 1)
                        if follows:
                            if k == last_at[b]:
                                gather(*nxt)
                            if k == last_at[b] + 1:
                                negate(*nxt)
                        follow_up(it, b, k)
            repeat(dve, its, body, last_apart=True)
            for k in range(tail):
                follow_up(its, 0, k)

        @block.gpsimd
        def _(pool):
            if pad:
                for b in range(2):
                    op = pool.memset(q_lo[b][rows:kr, :].bitcast(F32), 0.0)
                op.then_inc(pad_ok, 1)
            pool.wait_ge(const_ok, 1)

            def out_gate(it, b, c):
                n = chunk0(it, b) + c
                pool.wait_ge(sum_ok, n + 1)
                pool.wait_ge(gate_in[c % 2], 16 * (it * chunks + (chunks // 2 if b else 0) + c // 2 + 1))
                if not (is_first(it, b) and c < 2):
                    pool.wait_ge(stored[c % 2], 16 * (it * chunks + (chunks // 2 if b else 0) + c // 2))
                pool.tensor_tensor(o_out[c % 2][:], o_sum[c % 2][:], gate[c % 2][:], ALU.mult).then_inc(gated, 1)

            def follow_up(it, b, k):
                for e in late_chunk(it, b, k, lag + 3):
                    out_gate(*e)

            def body(it):
                for b in range(2):
                    for k, st in enumerate(steps[b]):
                        n = step0(it, b) + k
                        c, off = st["chunk"], st["off"]
                        pool.wait_ge(probs, n + 1)
                        mine, both = acc[c % 2], slice(off, TC)
                        if (alone(st) or st["second"]) and not (is_first(it, b) and c < 2):
                            pool.wait_ge(den_ok, chunk0(it, b) + c - 1)
                        if alone(st):
                            pool.tensor_tensor(mine[:], prob[buf(b, k)][:], zeros[:], ALU.add).then_inc(summed, 1)
                        elif st["second"]:
                            if off:
                                pool.tensor_tensor(mine[:, 0:off], prob[buf(b, k - 1)][:, 0:off], zeros[:, 0:off],
                                                   ALU.add).then_inc(summed, 1)
                            pool.tensor_tensor(mine[:, both], prob[buf(b, k - 1)][:, both], prob[buf(b, k)][:, both],
                                               ALU.add).then_inc(summed, 1)
                        elif not st["first"]:
                            pool.wait_ge(summed, sums(it, b, k - 1))
                            pool.tensor_tensor(mine[:, both], mine[:, both], prob[buf(b, k)][:, both], ALU.add
                                               ).then_inc(summed, 1)
                        follow_up(it, b, k)
            repeat(pool, its, body, last_apart=True)
            for k in range(tail + 1):
                follow_up(its, 0, k)


def swa_config(q, k, v, gates, out, dens, sinks, sink_exps):
    half_b = NB // 2
    steps, items = [], []
    for b in range(2):
        st, it = [], []
        for c in range(half_b):
            own = c + b
            blks = ([(own - 1, "prev_t")] if own > 0 else []) + [(own, "causal_t")]
            for n, (kb, mask) in enumerate(blks):
                st.append(dict(chunk=c, k=kb, v=kb, off=0, mask=mask, first=n == 0, last=n == len(blks) - 1))
            width = P * len(blks)
            it.append(dict(products=[(j * half_b * P + c * P, blks[0][0] * P, width, ("window_q", 0, width), j * 2 * P)
                                     for j in range(GROUP)],
                           stride=2 * P, groups=GROUP, width=width, col=c))
        steps.append(st)
        items.append(it)

    def tok(b):
        return (half_b * b - b) * P, (half_b + b) * P

    def queries(it, b, tile, part):
        src = q[part].rearrange("s g (j r) t -> s g r j t", j=GROUP)
        for s in range(2):
            yield (tile[s * 32:(s + 1) * 32, :].rearrange("r (j t) -> r j t", j=GROUP),
                   src[s, it, :, :, b * half_b * P:(b + 1) * half_b * P])

    def keys(it, b, tile, part):
        t0, n = tok(b)
        src = k[part].rearrange("s o (g r) t -> s (o g) r t", g=KV_HEADS)
        for s in range(2):
            yield tile[s * 32:(s + 1) * 32, 0:n], src[s, it, :, t0:t0 + n]

    def load_a(it, b, q_hi, k_hi):
        yield from queries(it, b, q_hi, 0)
        yield from keys(it, b, k_hi, 0)

    def load_b(it, b, q_lo, k_lo, vals):
        yield from queries(it, b, q_lo, 1)
        yield from keys(it, b, k_lo, 1)
        t0, n = tok(b)
        yield vals[:, 0:n // P, :], v[it, :, t0 // P:(t0 + n) // P]

    def heads(x, it, b, c):
        t0 = (b * half_b + c) * P
        return x.rearrange("(g j d) t -> g d j t", j=GROUP, d=HEAD_DIM)[it, :, :, t0:t0 + P]

    return dict(rows=HEAD_DIM, q_cols=SEQ * GROUP // 2, k_cols=(half_b + 1) * P, v_blocks=half_b + 1,
                scale=SWA_SCALE, iterations=KV_HEADS, chunks=half_b, steps=steps, items=items, sinks=sinks,
                max_cols=half_b * GROUP, max_width=2 * TC, items_from=(4, 5), items_to=(11, 12), pad=True,
                mask_width=TC, load_a=load_a, load_b=load_b, n_load_a=4, n_load_b=5,
                gate=lambda it, b, c, tile: tile[:].rearrange("d (j t) -> d j t", j=GROUP),
                gate_src=lambda it, b, c: heads(gates, it, b, c), dst=lambda it, b, c: heads(out, it, b, c),
                q_view=lambda tile, c, off: tile.rearrange("r (j t) -> r j t", j=GROUP)[:, :, c * P:(c + 1) * P],
                split=lambda bank: bank.rearrange("p (j t) -> p j t", j=GROUP),
                max_row=lambda row: row.rearrange("o (n t) -> o n t", t=P),
                row=lambda tile: tile[:].rearrange("o (j t) -> o j t", j=GROUP),
                den_dst=lambda it, b, c: dens.rearrange("(g o j) t -> g o j t", o=1, j=GROUP)[
                    it, :, :, (b * half_b + c) * P:(b * half_b + c + 1) * P],
                sink_dst=lambda it, b: sink_exps.rearrange("(g j) (n t) -> g j n t", j=GROUP, t=P)[
                    it, :, b * half_b:(b + 1) * half_b],
                max_after_chunk=half_b - 4)


def mla_config(q_nope, q_rope, k_nope, k_rope, v, gates, out, dens):
    steps, items, gather = [], [], []
    for c in range(NTC):
        for kb in range(4 * c + 4):
            off = max(0, kb - 4 * c) * P
            steps.append(dict(chunk=c, k=kb, v=kb, off=off, mask="causal_t" if kb >= 4 * c else None,
                              first=kb == 0, last=kb == 4 * c + 3))
        gather.append((len(items), c + 1, 4 * c))
        for i in range(4 * c, 4 * c + 4):
            for kc in range(c + 1):
                width = TC if kc < c else (i % 4 + 1) * P
                mask = ("causal_q", width - P, P) if kc == c else None
                items.append(dict(products=[(i * P, kc * TC, width, mask, 0)], stride=TC, groups=1,
                                  width=width, col=len(items)))

    def load(it, b, q_tile, k_tile, part):
        u = it * 2 + b
        half = ROPE // 2
        qr = q_rope[part].rearrange("s l (h r) t -> s (l h) r t", r=half)
        yield q_tile[0:NOPE, :], q_nope[part].rearrange("l (h d) t -> (l h) d t", d=NOPE)[u]
        for s in range(2):
            yield q_tile[NOPE + s * half:NOPE + (s + 1) * half, :], qr[s, u]
        yield k_tile[0:NOPE, :], k_nope[part].rearrange("l (h d) t -> (l h) d t", d=NOPE)[u]
        yield k_tile[NOPE:NOPE + ROPE, :], k_rope[part]

    def load_a(it, b, q_hi, k_hi):
        yield from load(it, b, q_hi, k_hi, 0)

    def load_b(it, b, q_lo, k_lo, vals):
        yield from load(it, b, q_lo, k_lo, 1)
        yield vals[:], v[it * 2 + b]

    def rows_of(x, it, b, c):
        return x.rearrange("(h d) t -> h d t", d=HEAD_DIM)[it * 2 + b, :, c * TC:(c + 1) * TC]

    return dict(rows=NOPE + ROPE, q_cols=SEQ, k_cols=SEQ, v_blocks=NB, scale=MLA_SCALE, iterations=HEADS // 2,
                chunks=NTC, steps=[steps, steps], items=[items, items], sinks=None, max_cols=len(items),
                max_width=TC, items_from=(6, 6), items_to=(34, 34), pad=False, mask_width=P,
                load_a=load_a, load_b=load_b, n_load_a=5, n_load_b=6, gather=gather,
                gate=lambda it, b, c, tile: tile[:],
                gate_src=lambda it, b, c: rows_of(gates, it, b, c), dst=lambda it, b, c: rows_of(out, it, b, c),
                q_view=lambda tile, c, off: tile[:, c * TC + off:(c + 1) * TC], split=lambda bank: bank,
                max_row=lambda row: row.rearrange("o (n t) -> o n t", t=P), row=lambda tile: tile[:],
                den_dst=lambda it, b, c: dens.rearrange("(h o) t -> h o t", o=1)[
                    it * 2 + b, :, c * TC:(c + 1) * TC],
                max_after_chunk=NTC - 2)


def build(nc, a, out):
    from contextlib import ExitStack
    ctx = ExitStack()
    with ctx:
        def dram(name, shape, dt=F32):
            return nc.dram_tensor(f"scratch_{name}", shape, dt, kind="Internal").ap()

        def parts(name, shape):
            return [dram(f"{name}_hi", shape), dram(f"{name}_lo", shape)]

        consts = {}
        for n, shape, dt in (("ident", [P, P], F32), ("ident_b", [P, P], BF16), ("ones", [P, P], F32),
                             ("causal_t", [P, GROUP, P], BF16), ("prev_t", [P, GROUP, P], BF16),
                             ("causal_q", [P, P], BF16), ("window_q", [P, 2 * P], BF16)):
            consts[n] = ctx.enter_context(nc.sbuf_tensor(f"const_{n}", shape, dt))

        def spread(rows):
            n, t = rows.shape
            cols = n * t // P
            return rows.rearrange("n (q c) -> (n q) c", c=cols)

        def close_layer(layer, x, attn, sources, dst):
            summed, sums = dram(f"sum{layer}", [D_MODEL, SEQ]), dram(f"sums{layer}", [2, SEQ])
            inv = dram(f"inv{layer}", [HEADS, SEQ])
            gemm_phase(nc, consts, f"wo{layer}", [(attn, KD, False)], [a[f"w_out{layer}_{b}"] for b in range(2)],
                       [("resid", KD // 2, dict(old=x, dst=summed))],
                       prep=dict(kind="divide", cols=HEADS * SEQ // P, sources=[spread(d) for d in sources],
                                 folded=[spread(inv)], order=[0], rows=inv),
                       stats=dict(rows={0: [(0, False), (1, True)]}, adds=2 * KD * NTC, last_adds=True, dst=sums))
            factors = dram(f"factors{layer}", [2, SEQ])
            gemm_phase(nc, consts, f"pe{layer}", [(summed, KD, False), (a[f"p{layer}"], PLE // P, True)],
                       [a[f"pe_gate{layer}"], a[f"pe_proj{layer}"]], [("gate", KD, dict(dst=dst))],
                       prep=dict(kind="layer", cols=SEQ // P, sources=[spread(sums[n:n + 1]) for n in range(2)],
                                 folded=[spread(factors[n:n + 1]) for n in range(2)], order=[0, 2], rows=factors,
                                 gain=a[f"ln_g{layer}"], bias=a[f"ln_b{layer}"], eps=LN_EPS))

        def rms(name, sums, gain):
            factors = dram(name, [1, SEQ])
            return dict(kind="rms", cols=SEQ // P, sources=[spread(sums)], folded=[spread(factors)], order=[2],
                        rows=factors, gain=gain, eps=RMS_EPS)

        q0, k0 = parts("q0", [2, KV_HEADS, P, SEQ]), parts("k0", [2, 1, P, SEQ])
        v0 = dram("v0", [KV_HEADS, P, NB, P])
        z0, o0, x1 = (dram(n, [D_MODEL, SEQ]) for n in ("z0", "o0", "x1"))
        den0, sink_exps = dram("den0", [HEADS, SEQ]), dram("sink_exps", [HEADS, SEQ])
        gemm_phase(nc, consts, "in0", [(a["x"], KD, True)], [a["w_in0_0"], a["w_in0_1"]],
                   [("silu", 2, dict(dst=z0[0:4 * P])), ("rope", 4, dict(dst=q0)), ("rope", 1, dict(dst=k0)),
                    ("silu", 2, dict(dst=z0[4 * P:]))],
                   tables=dict(positions=a["positions"], freq=a["freq0"], at=1), v=(a["w_v0"], KV_HEADS * HEAD_DIM, v0), constants=True)
        attention_phase(nc, consts, "swa", swa_config(q0, k0, v0, z0, o0, den0, a["sinks"], sink_exps))
        close_layer(0, a["x"], o0, [den0, sink_exps], x1)

        c1, sums1 = dram("c1", [Q_LORA + P + KV_LORA, SEQ]), dram("sums_c1", [2, SEQ])
        z1, o1, den1 = dram("z1", [D_MODEL, SEQ]), dram("o1", [D_MODEL, SEQ]), dram("den1", [HEADS, SEQ])
        nq, nkv = Q_LORA // P, KV_LORA // P
        mla_tables = [dram(n, [P, SEQ]) for n in ("mla_cos", "mla_sin")]
        latent = [(0, True)] * nq + [(None, True)] + [(1, True)] * nkv
        gemm_phase(nc, consts, "in1", [(x1, KD, False)], [a["w_in1_0"], a["w_in1_1"]],
                   [("raw", len(latent) // 2, dict(dst=c1)), ("silu", 4, dict(dst=z1))],
                   tables=dict(positions=a["positions"], freq=a["freq1"], at=1, dst=mla_tables),
                   stats=dict(rows={0: latent}, adds=len(latent) * NTC, last_adds=False,
                              dst=sums1))
        qn, qr = parts("qn", [HEADS // 2, P, SEQ]), parts("qr", [2, 2, P, SEQ])
        kr = parts("kr", [ROPE, SEQ])
        gemm_phase(nc, consts, "uq", [(c1[0:Q_LORA], nq, False)], [a["w_uq_0"], a["w_uq_1"]],
                   [("split", 1, dict(dst=[d[0:2] for d in qn])), ("rope", 2, dict(dst=qr)),
                    ("split", 3, dict(dst=[d[2:] for d in qn]))], tables=dict(src=mla_tables),
                   prep=rms("rms_q", sums1[0:1], a["q_norm"]), key_rope=(c1[Q_LORA:Q_LORA + ROPE], kr))
        kn, v1 = parts("kn", [HEADS // 2, P, SEQ]), dram("v1", [HEADS, P, NB, P])
        gemm_phase(nc, consts, "ukv", [(c1[Q_LORA + P:], nkv, False)], [a["w_uk_0"], a["w_uk_1"]],
                   [("split", 4, dict(dst=kn))], v=(a["w_uv"], HEADS * HEAD_DIM, v1),
                   prep=rms("rms_kv", sums1[1:2], a["kv_norm"]))
        attention_phase(nc, consts, "mla", mla_config(qn, qr, kn, kr, v1, z1, o1, den1))
        close_layer(1, x1, o1, [den1], out)


def column_tiles(w, order=None):
    w = w if order is None else w[:, order]
    k, n = w.shape
    return np.ascontiguousarray(w.reshape(k // P, P, n // P, P).transpose(2, 1, 0, 3)).reshape(n // P, P, k)


def lay_out(x, p, positions, w_out, ln_g, ln_b, pe_gate, pe_proj, l0_w_in, l0_sinks, l1_w_in, l1_q_norm,
            l1_kv_norm, l1_w_uq, l1_w_ukv):
    a = {"x": np.ascontiguousarray(x[0].T), "positions": positions[0], "sinks": l0_sinks}
    exps = [np.arange(h, dtype=np.float32) / np.float32(h) for h in (HEAD_DIM // 2, ROPE // 2)]
    for n, e in enumerate(exps):
        a[f"freq{n}"] = np.tile(np.power(np.float32(THETA), -e), P // len(e)).astype(np.float32)[:, None]

    def slots(name, tiles):
        a[f"{name}_0"], a[f"{name}_1"] = np.ascontiguousarray(tiles[0::2]), np.ascontiguousarray(tiles[1::2])

    def by_tile(g):
        return np.ascontiguousarray(g.reshape(-1, P).T)

    for layer in range(DEPTH):
        slots(f"w_out{layer}", column_tiles(w_out[layer]))
        a[f"ln_g{layer}"], a[f"ln_b{layer}"] = by_tile(ln_g[layer]), by_tile(ln_b[layer])
        a[f"pe_gate{layer}"] = column_tiles(pe_gate[layer])
        a[f"pe_proj{layer}"] = column_tiles(pe_proj[layer])
        a[f"p{layer}"] = np.ascontiguousarray(p[layer, 0].T)

    def rotary(first, heads, dim, stride=None):
        stride, half = stride or dim, dim // 2
        per = P // half
        return np.concatenate([first + (g + np.arange(per))[:, None] * stride + s * half + np.arange(half)
                               for g in range(0, heads, per) for s in range(2)]).ravel()

    kv = KV_HEADS * HEAD_DIM
    q_end, k_end, v_end = D_MODEL, D_MODEL + kv, D_MODEL + 2 * kv
    slots("w_in0", column_tiles(l0_w_in, np.concatenate([
        np.arange(v_end, v_end + 4 * P), rotary(0, HEADS, HEAD_DIM), rotary(q_end, KV_HEADS, HEAD_DIM),
        np.arange(v_end + 4 * P, l0_w_in.shape[1])])))

    def token_weights(w):
        k, n = w.shape
        return np.ascontiguousarray(w.reshape(k // P, P, n).transpose(1, 0, 2)).reshape(P, -1)

    a["w_v0"] = token_weights(l0_w_in[:, k_end:v_end])
    pad = np.zeros((D_MODEL, P - ROPE), l1_w_in.dtype)
    c = [Q_LORA, Q_LORA + KV_LORA, Q_LORA + KV_LORA + ROPE]
    slots("w_in1", column_tiles(np.concatenate(
        [l1_w_in[:, :c[0]], l1_w_in[:, c[1]:c[2]], pad, l1_w_in[:, c[0]:c[1]], l1_w_in[:, c[2]:]], 1)))
    a["q_norm"], a["kv_norm"] = by_tile(l1_q_norm), by_tile(l1_kv_norm)
    heads = np.arange(HEADS)[:, None]
    nope = (heads * (NOPE + ROPE) + np.arange(NOPE)).ravel()
    slots("w_uq", column_tiles(l1_w_uq, np.concatenate([
        nope[:2 * P], rotary(NOPE, HEADS, ROPE, NOPE + ROPE), nope[2 * P:]])))
    slots("w_uk", column_tiles(l1_w_ukv, (heads * 2 * NOPE + np.arange(NOPE)).ravel()))
    a["w_uv"] = token_weights(l1_w_ukv[:, (heads * 2 * NOPE + NOPE + np.arange(NOPE)).ravel()])
    return a


def kernel(x, p, positions, w_out, ln_g, ln_b, pe_gate, pe_proj, l0_w_in, l0_sinks, l1_w_in, l1_q_norm,
           l1_kv_norm, l1_w_uq, l1_w_ukv, **unused):
    import concourse.bacc as bacc
    from concourse.bass_utils import run_bass_kernel_spmd

    arrays = {f"in_{n}": np.ascontiguousarray(v) for n, v in lay_out(
        *(np.asarray(v) for v in (x, p, positions, w_out, ln_g, ln_b, pe_gate, pe_proj, l0_w_in, l0_sinks,
                                  l1_w_in, l1_q_norm, l1_kv_norm, l1_w_uq, l1_w_ukv))).items()}
    nc = bacc.Bacc("TRN2", target_bir_lowering=False, num_devices=1)
    ins = {n[3:]: nc.dram_tensor(n, v.shape, mybir.dt.from_np(v.dtype), kind="ExternalInput").ap()
           for n, v in arrays.items()}
    out = nc.dram_tensor("out_t", (D_MODEL, SEQ), F32, kind="ExternalOutput").ap()
    build(nc, ins, out)
    r = run_bass_kernel_spmd(nc, [arrays], core_ids=[0])
    return np.ascontiguousarray(r.results[0]["out_t"].T)[None]
```
